# Optimizing a Trainium2 kernel written in Bass

```python
import math
import jax, jax.numpy as jnp
from jax import lax
import numpy as np

D_MODEL = 1024
BATCH = 1
SEQ = 512
DEPTH = 1

PLE_DIM = 256
D_FF = 2816
GM_HEADS = 4
GM_HEAD_DIM = 128
GM_WIDTH = GM_HEADS * GM_HEAD_DIM
GM_CHUNK = 128
DN_HEADS = 4
DN_HEAD_DIM = 128
DN_WIDTH = DN_HEADS * DN_HEAD_DIM
DN_CHUNK = 64
N_DIR = 2
CONV_WIDTH = 5
MIX_WIDTH = GM_WIDTH + DN_WIDTH
EPS = 1e-6
SPLITS = (GM_WIDTH, 2 * GM_WIDTH, 2 * GM_WIDTH + 3 * DN_WIDTH, 2 * GM_WIDTH + 4 * DN_WIDTH,
          2 * GM_WIDTH + 4 * DN_WIDTH + N_DIR * DN_HEADS)
IN_COLS = 2 * GM_WIDTH + 4 * DN_WIDTH + 2 * N_DIR * DN_HEADS

kernel_name = 'hybrid_gmlp_gdn_macaron_encoder'

def rmsnorm(x, g):
    xf = x.astype(jnp.float32)
    y = xf * lax.rsqrt(jnp.mean(xf * xf, axis=-1, keepdims=True) + EPS)
    return (y * g.astype(jnp.float32)).astype(x.dtype)

def layernorm(x, g, b):
    xf = x.astype(jnp.float32)
    mu = jnp.mean(xf, axis=-1, keepdims=True)
    xc = xf - mu
    y = xc * lax.rsqrt(jnp.mean(xc * xc, axis=-1, keepdims=True) + EPS)
    return (y * g.astype(jnp.float32) + b.astype(jnp.float32)).astype(x.dtype)

def l2norm(x):
    return x * lax.rsqrt(jnp.sum(x * x, axis=-1, keepdims=True) + EPS)

def swiglu(x, w_gate, w_up, w_down):
    return (jax.nn.silu(x @ w_gate) * (x @ w_up)) @ w_down

def gmlp_mixer(zu, zv, ln_g, ln_b, ws, bs):
    bsz, s, _ = zu.shape
    u = jax.nn.gelu(zu)
    v = jax.nn.gelu(zv).reshape(bsz, s // GM_CHUNK, GM_CHUNK, GM_HEADS, GM_HEAD_DIM)
    v = layernorm(v, ln_g, ln_b)
    sv = jnp.einsum('hij,bnjhd->bnihd', ws, v) + bs.T[:, :, None]
    return u * sv.reshape(bsz, s, GM_WIDTH)

def chunk_gated_delta(q, k, v, g, beta):
    bsz, nh, s, dk = q.shape
    dv = v.shape[-1]
    nc = s // DN_CHUNK
    q, k, v, g, beta = [t.reshape(bsz, nh, nc, DN_CHUNK, *t.shape[3:]) for t in (q, k, v, g, beta)]
    g = jnp.cumsum(g, axis=-1)
    idx = jnp.arange(DN_CHUNK)
    incl = idx[:, None] >= idx[None, :]
    strict = idx[:, None] > idx[None, :]
    decay = jnp.exp(jnp.where(incl, g[..., :, None] - g[..., None, :], -jnp.inf))
    kk = jnp.einsum('bhncd,bhnmd->bhncm', k, k)
    a_mat = jnp.where(strict, beta[..., None] * kk * decay, 0.0) + jnp.eye(DN_CHUNK, dtype=jnp.float32)
    rhs = jnp.concatenate([v * beta[..., None], k * (beta * jnp.exp(g))[..., None]], axis=-1)
    sol = lax.linalg.triangular_solve(a_mat, rhs, left_side=True, lower=True, unit_diagonal=True)
    u, w = sol[..., :dv], sol[..., dv:]
    qk = jnp.where(incl, jnp.einsum('bhncd,bhnmd->bhncm', q, k) * decay, 0.0)
    q_dec = q * jnp.exp(g)[..., None]
    k_dec = k * jnp.exp(g[..., -1:] - g)[..., None]
    g_last = jnp.exp(g[..., -1])

    def step(state, inp):
        qk_c, qd_c, kd_c, u_c, w_c, gl_c = inp
        v_new = u_c - jnp.einsum('bhcd,bhde->bhce', w_c, state)
        o = jnp.einsum('bhcd,bhde->bhce', qd_c, state) + jnp.einsum('bhcm,bhme->bhce', qk_c, v_new)
        state = state * gl_c[..., None, None] + jnp.einsum('bhcd,bhce->bhde', kd_c, v_new)
        return state, o

    xs = tuple(jnp.moveaxis(t, 2, 0) for t in (qk, q_dec, k_dec, u, w, g_last))
    s0 = jnp.zeros((bsz, nh, dk, dv), jnp.float32)
    _, o = lax.scan(step, s0, xs)
    return jnp.moveaxis(o, 0, 2).reshape(bsz, nh, s, dv)

def deltanet_mixer(zqkv, zg, za, zb, conv_w, a_log, dt_bias, out_norm):
    bsz, s, _ = zqkv.shape
    f32 = jnp.float32
    qkv = lax.conv_general_dilated(zqkv, conv_w[:, None, :].astype(zqkv.dtype), window_strides=(1,),
                                   padding=[(CONV_WIDTH // 2, CONV_WIDTH // 2)],
                                   dimension_numbers=('NWC', 'WIO', 'NWC'),
                                   feature_group_count=3 * DN_WIDTH)
    qkv = jax.nn.silu(qkv).astype(f32).reshape(bsz, s, 3, DN_HEADS, DN_HEAD_DIM)
    q = l2norm(qkv[:, :, 0]) * (DN_HEAD_DIM ** -0.5)
    k = l2norm(qkv[:, :, 1])
    v = qkv[:, :, 2]
    a = za.astype(f32).reshape(bsz, s, N_DIR, DN_HEADS)
    g = -jnp.exp(a_log.astype(f32)) * jax.nn.softplus(a + dt_bias.astype(f32))
    beta = jax.nn.sigmoid(zb.astype(f32).reshape(bsz, s, N_DIR, DN_HEADS))

    def both_dirs(t):
        t2 = jnp.concatenate([t, jnp.flip(t, axis=1)], axis=2)
        return jnp.moveaxis(t2, 1, 2)

    gd = jnp.moveaxis(jnp.concatenate([g[:, :, 0], jnp.flip(g[:, :, 1], axis=1)], axis=2), 1, 2)
    bd = jnp.moveaxis(jnp.concatenate([beta[:, :, 0], jnp.flip(beta[:, :, 1], axis=1)], axis=2), 1, 2)
    o = chunk_gated_delta(both_dirs(q), both_dirs(k), both_dirs(v), gd, bd)
    o = o[:, :DN_HEADS] + jnp.flip(o[:, DN_HEADS:], axis=2)
    o = jnp.moveaxis(o, 1, 2)
    gate = zg.astype(f32).reshape(bsz, s, DN_HEADS, DN_HEAD_DIM)
    y = rmsnorm(o, out_norm) * jax.nn.silu(gate)
    return y.reshape(bsz, s, DN_WIDTH).astype(zqkv.dtype)

def setup_inputs(seed: int = 0) -> dict:
    key = jax.random.key(seed)
    ks = jax.random.split(key, 32)
    f32 = jnp.float32
    L = DEPTH

    def nrm(i, shape, scale):
        return jax.random.normal(ks[i], shape, f32) * scale

    def gain(i, shape):
        return 1.0 + nrm(i, shape, 0.05)

    x = nrm(0, (BATCH, SEQ, D_MODEL), 1.0)
    p = nrm(1, (DEPTH, BATCH, SEQ, PLE_DIM), 1.0)
    a_log = jnp.log(jax.random.uniform(ks[13], (L, N_DIR, DN_HEADS), f32, 1.0, 16.0))
    dt = jnp.exp(jax.random.uniform(ks[14], (L, N_DIR, DN_HEADS), f32, math.log(1e-3), math.log(1e-1)))
    dt_bias = dt + jnp.log(-jnp.expm1(-dt))
    return {
        'x': x,
        'p': p,
        'ffn1_norm': gain(2, (L, D_MODEL)),
        'ffn1_w_gate': nrm(3, (L, D_MODEL, D_FF), D_MODEL ** -0.5),
        'ffn1_w_up': nrm(4, (L, D_MODEL, D_FF), D_MODEL ** -0.5),
        'ffn1_w_down': nrm(5, (L, D_FF, D_MODEL), D_FF ** -0.5),
        'mix_norm': gain(6, (L, D_MODEL)),
        'w_in': nrm(7, (L, D_MODEL, IN_COLS), D_MODEL ** -0.5),
        'gm_ln_g': gain(8, (L, GM_HEADS, GM_HEAD_DIM)),
        'gm_ln_b': nrm(9, (L, GM_HEADS, GM_HEAD_DIM), 0.02),
        'gm_ws': nrm(10, (L, GM_HEADS, GM_CHUNK, GM_CHUNK), GM_CHUNK ** -0.5),
        'gm_bs': 1.0 + nrm(11, (L, GM_HEADS, GM_CHUNK), 0.1),
        'dn_conv_w': nrm(12, (L, CONV_WIDTH, 3 * DN_WIDTH), CONV_WIDTH ** -0.5),
        'dn_a_log': a_log,
        'dn_dt_bias': dt_bias,
        'dn_out_norm': gain(15, (L, DN_HEAD_DIM)),
        'w_out': nrm(16, (L, MIX_WIDTH, D_MODEL), MIX_WIDTH ** -0.5),
        'ffn2_norm': gain(17, (L, D_MODEL)),
        'ffn2_w_gate': nrm(18, (L, D_MODEL, D_FF), D_MODEL ** -0.5),
        'ffn2_w_up': nrm(19, (L, D_MODEL, D_FF), D_MODEL ** -0.5),
        'ffn2_w_down': nrm(20, (L, D_FF, D_MODEL), D_FF ** -0.5),
        'ple_proj': nrm(21, (L, PLE_DIM, D_MODEL), PLE_DIM ** -0.5),
        'ple_norm': gain(22, (L, D_MODEL)),
        'ple_gate_norm': gain(23, (L, D_MODEL)),
        'ple_gate_w': nrm(24, (L, D_MODEL, D_MODEL), D_MODEL ** -0.5),
        'ple_gate_b': nrm(25, (L, D_MODEL), 0.02),
        'final_norm': gain(26, (D_MODEL,)),
    }

def reference(x, p, ffn1_norm, ffn1_w_gate, ffn1_w_up, ffn1_w_down, mix_norm, w_in,
              gm_ln_g, gm_ln_b, gm_ws, gm_bs, dn_conv_w, dn_a_log, dn_dt_bias, dn_out_norm,
              w_out, ffn2_norm, ffn2_w_gate, ffn2_w_up, ffn2_w_down, ple_proj, ple_norm,
              ple_gate_norm, ple_gate_w, ple_gate_b, final_norm):
    h = x
    for i in range(DEPTH):
        h = h + 0.5 * swiglu(rmsnorm(h, ffn1_norm[i]), ffn1_w_gate[i], ffn1_w_up[i], ffn1_w_down[i])
        n = rmsnorm(h, mix_norm[i])
        z = n @ w_in[i]
        zu, zv, zqkv, zg, za, zb = jnp.split(z, SPLITS, axis=-1)
        y_gm = gmlp_mixer(zu, zv, gm_ln_g[i], gm_ln_b[i], gm_ws[i], gm_bs[i])
        y_dn = deltanet_mixer(zqkv, zg, za, zb, dn_conv_w[i], dn_a_log[i], dn_dt_bias[i], dn_out_norm[i])
        h = h + jnp.concatenate([y_gm, y_dn], axis=-1) @ w_out[i]
        h = h + 0.5 * swiglu(rmsnorm(h, ffn2_norm[i]), ffn2_w_gate[i], ffn2_w_up[i], ffn2_w_down[i])
        e = rmsnorm(p[i] @ ple_proj[i], ple_norm[i])
        gate = jax.nn.sigmoid(rmsnorm(h, ple_gate_norm[i]) @ ple_gate_w[i] + ple_gate_b[i])
        h = h + gate * e
    return rmsnorm(h, final_norm)


_drawn_inputs = setup_inputs


def setup_inputs(seed=0):
    import zlib

    import numpy as np

    out = dict(_drawn_inputs(seed))
    spreads = {}
    factors = {'gm_ln_g': 3.47,
     'gm_ln_b': 8.0,
     'dn_out_norm': 3.674,
     'ffn2_norm': 3.811,
     'ple_norm': 10.168,
     'ple_gate_norm': 25.493,
     'ple_gate_b': 60.864}
    for name, (base, spread) in spreads.items():
        noise = np.random.default_rng([zlib.crc32(name.encode()), seed]).standard_normal(out[name].shape)
        drawn = base * np.exp(spread * noise) if base else spread * noise
        out[name] = __import__('jax').numpy.asarray(drawn.astype(out[name].dtype))
    for name, factor in factors.items():
        out[name] = (out[name] * factor).astype(out[name].dtype)
    return out
```

```python
import concourse.bass as bass
from concourse import mybir
from contextlib import ExitStack

P = 128
D = 1024
KT = D // P
T = 512
TT = T // P
FF = 2816
FP = FF // (2 * P)
HD = 4
NJ = 16
PLE = 256
EPS = 1e-6
CONV = 5
NEG = -1e30

F1 = 0
WIN = F1 + 3 * FP
WOUT = WIN + 12
F2 = WOUT + 4
PROJ = F2 + 3 * FP
GATE = PROJ + 1
NSLOT = GATE + 4
LEVELS = [2, 4, 8, 16, 32, 64]


def build(nc, io):
    f32, f32r, i8 = mybir.dt.float32, mybir.dt.float32r, mybir.dt.int8
    ALU, ACT = mybir.AluOpType, mybir.ActivationFunctionType
    ctx = ExitStack()
    with ctx:
        cursor = [(nc.sbuf_base + 63) // 64 * 64]

        def sb(name, shape, dt=f32, offset=None):
            n = 1 if dt == i8 else 4
            for s in shape[1:]:
                n *= s
            if offset is None:
                offset = cursor[0]
                cursor[0] += (n + 63) // 64 * 64
            return nc.alloc_sbuf_tensor_at(name, shape, dt, offset=offset)

        def sem(name):
            return ctx.enter_context(nc.semaphore(name))

        hT = sb("hT", [P, KT, T])
        x_at = cursor[0]
        xhi = sb("xhi", [P, KT, T], f32r)
        xlo = sb("xlo", [P, KT, T], f32r)
        raw = [sb(f"raw{i}", [P, 2048]) for i in range(2)]
        whi = [sb(f"whi{i}", [P, 2048], f32r) for i in range(2)]
        wlo = [sb(f"wlo{i}", [P, 2048], f32r) for i in range(2)]
        ident = sb("ident", [P, P])
        ones = sb("ones", [P, P])
        eps = sb("eps", [P, 1])
        cols = sb("cols", [P, 109])
        tri = sb("tri", [P, 2, P])
        negm = sb("negm", [P, 2, P])
        lev = sb("lev", [P, 7, 2, P], i8)
        ss = sb("ss", [P, 8])
        std = sb("std", [P, 8])
        rstd = sb("rstd", [P, 8])
        ptok = sb("ptok", [P, TT, PLE])
        sqsum = sb("sqsum", [P, T])
        tmp_at = cursor[0]
        tmp = sb("tmp", [P, 4, T])
        arena = cursor[0]
        G_FFN1, G_MIX, G_FFN2, G_GATE, G_PLE, B_GATE, G_CONV, G_OUT = 0, 8, 16, 24, 32, 40, 48, 108

        guhi = sb("guhi", [P, 2 * FP, T], f32r)
        gulo = sb("gulo", [P, 2 * FP, T], f32r)
        end = cursor[0]
        assert end <= nc.sbuf_usable_end, (end, nc.sbuf_usable_end)
        cursor[0] = arena
        xtok = sb("xtok", [P, TT, D])
        vrows = sb("vrows", [109, P])
        sqjunk = sb("sqjunk", [P, D])
        cursor[0] = arena
        qT = sb("qT", [P, HD, T])
        kT = sb("kT", [P, HD, T])
        ktok = sb("ktok", [P, TT, HD, P])
        nkv = sb("nkv", [P, TT, HD, P])
        zg = sb("zg", [P, HD, T])
        uT = sb("uT", [P, HD, T])
        oT = sb("oT", [P, HD, T])
        St = sb("St", [P, 2, HD, P])
        nx_at = cursor[0]
        NTm = sb("NTm", [P, 2, HD, P])
        Xm = sb("Xm", [P, 2, HD, P])
        vg = sb("vg", [P, TT, T], offset=nx_at)
        d_at = cursor[0]
        Dm = sb("Dm", [P, 2, HD, P])
        Em = sb("Em", [P, 2, HD, P])
        wab = sb("wab", [P, 240], offset=d_at)
        wabhi = sb("wabhi", [P, 240], f32r, offset=d_at + 960)
        wablo = sb("wablo", [P, 240], f32r, offset=d_at + 1920)
        abT = sb("abT", [16, T], offset=d_at + 2880)
        bns = sb("bns", [P, 16, 6], offset=d_at + 4928)
        mv = sb("mv", [P, 16, 2], offset=d_at + 5312)
        lsd = sb("lsd", [P, 16], offset=d_at + 5440)
        lrs = sb("lrs", [P, 16], offset=d_at + 5504)
        t_at = cursor[0]
        Tm = sb("Tm", [P, 2, HD, P])
        wsraw = sb("wsraw", [P, HD, P], offset=t_at)
        wsT = sb("wsT", [P, HD, P])
        lng = sb("lng", [P, T])
        lnb = sb("lnb", [P, T])
        bsb = sb("bsb", [P, T])
        assert cursor[0] <= end
        Pm = sb("Pm", [P, 2, HD, P], offset=x_at + 8192)
        qd = sb("qd", [P, 2, HD, P], offset=x_at + 12288)
        Ym = sb("Ym", [P, 2, HD, P], offset=x_at + 24576)
        acc = sb("acc", [P, 2, T], offset=tmp_at)
        mb = sb("mb", [P, 2, T], offset=tmp_at + 4096)
        c_at = cursor[0] - 0
        small = sb("small", [P, 15, 32], offset=tmp_at - 2048)
        (aa, ea, gg, be, Gc, eG, neG, egl, egd, sk, nsk, s2, misc, bc8, misc2) = [small[:, i, :] for i in range(15)]
        nk = misc2[:, 0:16]
        rk2 = misc2[:, 16:32]
        cursor[0] = arena
        eT = sb("eT", [P, KT, T])
        pThi = sb("pThi", [P, 2, T], f32r)
        pTlo = sb("pTlo", [P, 2, T], f32r)
        fbc = sb("fbc", [P, D])
        otile = sb("otile", [P, 2, D])
        fjunk = sb("fjunk", [P, D])
        sgm = sb("sgm", [P, 2, T])
        pTf = sb("pTf", [P, 2, T])
        assert cursor[0] <= end

        ps = ctx.enter_context(nc.psum_tensor("ps", [P, 8, T], f32))

        raw_in = [sem("raw_in0"), sem("raw_in1")]
        hi_done, lo_done, w_done = sem("hi_done"), sem("lo_done"), sem("w_done")
        x_in = [sem(f"x_in{t}") for t in range(TT)]
        vec_in, bc_in, ab_in, ws_in, p_in, f_in = [sem(s) for s in ("vec_in", "bc_in", "ab_in", "ws_in", "p_in", "f_in")]
        const_step, const_done = sem("const_step"), sem("const_done")
        xtr_done, vtr_done, hx_act, hx_dve, cols_done, ss0_done = [
            sem(s) for s in ("xtr_done", "vtr_done", "hx_act", "hx_dve", "cols_done", "ss0_done")]
        silu_done, gu_done, guhi_done, gulo_done = [sem(s) for s in ("silu_done", "gu_done", "guhi_done", "gulo_done")]
        out_done, h_done, sq_done, acc_done = [sem(s) for s in ("out_done", "h_done", "sq_done", "acc_done")]
        stats_done, std_done, rstd_done, rb_done = [sem(s) for s in ("stats_done", "std_done", "rstd_done", "rb_done")]
        xf_done, xhi_done, x_ready = sem("xf_done"), sem("xhi_done"), sem("x_ready")
        conv_tap, conv_done, zact_done, zsq_done, qk_stat, tok_tr, ktok_done, nkv_done = [
            sem(s) for s in ("conv_tap", "conv_done", "zact_done", "zsq_done", "qk_stat", "tok_tr", "ktok_done", "nkv_done")]
        nk_done, rk_step = sem("nk_done"), sem("rk_step")
        ab_pad = sem("ab_pad")
        wab_hi, wab_lo, ab_mm, ab_copy, ab_tr = [sem(s) for s in ("wab_hi", "wab_lo", "ab_mm", "ab_copy", "ab_tr")]
        gate_act, gate_dve, cum_done, col_act, col_dve = [sem(s) for s in ("gate_act", "gate_dve", "cum_done", "col_act", "col_dve")]
        vgelu, ln_step, ln_sd, ln_done, ws_tr, ws_done, ugelu, sv_done, gm_step, gm_done = [
            sem(s) for s in ("vgelu", "ln_step", "ln_sd", "ln_done", "ws_tr", "ws_done", "ugelu", "sv_done", "gm_step", "gm_done")]
        zg_done = sem("zg_done")
        grow_done, kk_done, kq_done, dpre_done, dm_done, em_done, pm_done, nt_done, y_init, y1_done = [
            sem(s) for s in ("grow_done", "kk_done", "kq_done", "dpre_done", "dm_done", "em_done", "pm_done", "nt_done", "y_init", "y1_done")]
        qd_done, xtr2, x1_done = sem("qd_done"), sem("x_transposed"), sem("x1_done")
        t_mm, t_copy, w_mm, wt_mm, xy_done = [sem(s) for s in ("t_mm", "t_copy", "w_mm", "wt_mm", "xy_done")]
        s_zero, ks_mm, r_done, v_mm, vn_done, vs_done, o_mm, s_mm, s_upd, o_acc = [
            sem(s) for s in ("s_zero", "ks_mm", "r_done", "v_mm", "vn_done", "vs_done", "o_mm", "s_mm", "s_upd", "o_acc")]
        osq, ost, osd, oscale, orow, y_step, yhi_done, y_ready = [
            sem(s) for s in ("osq", "ost", "osd", "oscale", "orow", "y_step", "yhi_done", "y_ready")]
        p_tr, p_copy, pt_hi, pt_lo, e_mm, e_copy, e_sq, e_acc = [
            sem(s) for s in ("p_tr", "p_copy", "pt_hi", "pt_lo", "e_mm", "e_copy", "e_sq", "e_acc")]
        e_stats, e_std, e_rstd, e_rb, en_done = [sem(s) for s in ("e_stats", "e_std", "e_rstd", "e_rb", "en_done")]
        g_mm, sg_done, ge_done, hf_done, f_tr, f_ss, f_std, f_rstd, f_out, *stored = [
            sem(s) for s in ("g_mm", "sg_done", "ge_done", "hf_done", "f_tr", "f_ss", "f_std", "f_rstd", "f_out", "stored0")] + [sem("stored1")]

        block = ctx.enter_context(nc.Block())
        BANK = [(o + 4) % 8 for o in range(KT)]

        def wcol(w, n):
            return w[n % 2][:].rearrange("p (k n) -> p k n", n=256)

        def wrow(w, n, c):
            return w[n % 2][:].rearrange("p (k n) -> p k n", n=c)

        @block.sync
        def _(sp):
            def load(n, p, src, dst=None):
                if not isinstance(n, int) or n >= 2:
                    sp.wait_ge(lo_done, n - 1)
                sp.dma_start(raw[p][:].rearrange("p (k n) -> p k n", n=dst or 256), src).then_inc(raw_in[p], 16)

            def col_pair(w, i):
                return w[:, bass.ds(i * 256, 256)].rearrange("(k p) n -> p k n", p=P)

            def row_pair(w, j):
                return w[bass.ds(j * 256, 256), :].rearrange("(f p) n -> p f n", p=P)

            def ffn(n0, wg, wu, wd):
                load(n0, n0 % 2, col_pair(wg, 0))
                load(n0 + 1, (n0 + 1) % 2, col_pair(wu, 0))
                with sp.Fori(1, FP) as i:
                    load(i * 2 + n0, n0 % 2, col_pair(wg, i))
                    load(i * 2 + (n0 + 1), (n0 + 1) % 2, col_pair(wu, i))
                n1 = n0 + 2 * FP
                with sp.Fori(0, FP - 1, 2) as j:
                    load(j + n1, n1 % 2, row_pair(wd, j), D)
                    load(j + (n1 + 1), (n1 + 1) % 2, row_pair(wd, j + 1), D)
                load(n1 + FP - 1, (n1 + FP - 1) % 2, row_pair(wd, FP - 1), D)

            xv = io["x"][0].rearrange("(t p) n -> p t n", p=P)
            for t in range(TT):
                sp.dma_start(xtok[:, t, :], xv[:, t, :]).then_inc(x_in[t], 16)
            ffn(F1, io["ffn1_w_gate"][0], io["ffn1_w_up"][0], io["ffn1_w_down"][0])
            wi = io["w_in"][0]
            q0 = 2 * 512
            for s in range(6):
                load(WIN + s, (WIN + s) % 2, wi[:, q0 + 256 * s:q0 + 256 * (s + 1)].rearrange("(k p) n -> p k n", p=P))
            for s in range(2):
                load(WIN + 6 + s, (WIN + 6 + s) % 2, wi[512 * s:512 * (s + 1), 512:1024].rearrange("(k p) n -> p k n", p=P), 512)
            for s, c0 in enumerate((0, 256, 2560, 2816)):
                load(WIN + 8 + s, (WIN + 8 + s) % 2, wi[:, c0:c0 + 256].rearrange("(k p) n -> p k n", p=P))
            for s in range(4):
                load(WOUT + s, (WOUT + s) % 2, col_pair(io["w_out"][0], s))
            ffn(F2, io["ffn2_w_gate"][0], io["ffn2_w_up"][0], io["ffn2_w_down"][0])
            load(PROJ, PROJ % 2, row_pair(io["ple_proj"][0], 0), D)
            for s in range(4):
                load(GATE + s, (GATE + s) % 2, col_pair(io["ple_gate_w"][0], s))
            ov = io["out"][0].rearrange("(t p) n -> p t n", p=P)
            for t in range(TT):
                sp.wait_ge(f_out, t + 1)
                sp.dma_start(ov[:, t, :], otile[:, t % 2, :]).then_inc(stored[t % 2], 16)
            for half in stored:
                sp.wait_ge(half, 16 * (TT // 2))

        @block.gpsimd
        def _(pool):
            rows = [("ffn1_norm", 0), ("mix_norm", 8), ("ffn2_norm", 16), ("ple_gate_norm", 24), ("ple_norm", 32), ("ple_gate_b", 40)]
            for name, r in rows:
                pool.dma_start(vrows[r:r + 8, :], io[name][0].rearrange("(k p) -> k p", p=P)).then_inc(vec_in, 16)
            pool.dma_start(vrows[48:108, :], io["dn_conv_w"][0].rearrange("j (t p) -> (j t) p", p=P)).then_inc(vec_in, 16)
            pool.dma_start(vrows[108:109, :], io["dn_out_norm"]).then_inc(vec_in, 16)
            pool.dma_start(ptok[:], io["p"][0, 0].rearrange("(t p) n -> p t n", p=P)).then_inc(p_in, 16)
            step = [0]

            def fill(ap, v):
                nc.gpsimd.memset(ap, v).then_inc(const_step, 1)
                step[0] += 1

            def sel(ap, pattern, base, cm, op, fillv):
                pool.wait_ge(const_step, step[0])
                nc.gpsimd.affine_select(out=ap, in_=ap, pattern=pattern, compare_op=op, fill=fillv, base=base,
                                        channel_multiplier=cm).then_inc(const_step, 1)
                step[0] += 1

            fill(ones[:], 1.0)
            fill(eps[:], EPS)
            fill(ident[:], 0.0)
            sel(ident[:], [[-1, P]], 0, 1, ALU.not_equal, 1.0)
            nc.gpsimd.memset(sqjunk[0:1, 0:1], 0.0).then_inc(const_done, 1)
            fill(tri[:], 1.0)
            fill(negm[:], 0.0)
            for d, sg in ((0, 1), (1, -1)):
                sel(tri[:, d, :], [[sg, P]], 0, -sg, ALU.is_ge, 0.0)
                sel(negm[:, d, :], [[sg, P]], 0, -sg, ALU.is_ge, NEG)
            fill(lev[:], 0.0)
            for l in range(7):
                s = 1 << l
                v = lev[:, l, :, :].rearrange("p d (b e r) -> p d b e r", e=2, r=s)
                for d in range(2):
                    part = v[:, d, :, d, :]
                    pool.wait_ge(const_step, step[0])
                    fill(part, 1.0)
                    lo = s if d == 0 else 0
                    sel(part, [[-2 * s, P // (2 * s)], [0, s]], -lo, 1, ALU.is_ge, 0.0)
                    sel(part, [[2 * s, P // (2 * s)], [0, s]], lo + s - 1, -1, ALU.is_ge, 0.0)
            pool.wait_ge(const_step, step[0])
            nc.gpsimd.memset(sqjunk[0:1, 0:1], 0.0).then_inc(const_done, 1)
            pool.wait_ge(w_done, WIN)
            pool.wait_ge(gulo_done, FP + 1)
            pool.dma_start(lng[:], io["gm_ln_g"].rearrange("a h d -> a (h d)").broadcast_to([P, T])).then_inc(bc_in, 16)
            pool.dma_start(lnb[:], io["gm_ln_b"].rearrange("a h d -> a (h d)").broadcast_to([P, T])).then_inc(bc_in, 16)
            pool.dma_start(bsb[:], io["gm_bs"].rearrange("a h d -> a (h d)").broadcast_to([P, T])).then_inc(bc_in, 16)
            pool.dma_start(wab[:, 0:128].rearrange("p (k n) -> p k n", n=16),
                           io["w_in"][0][:, 3072:3088].rearrange("(k p) n -> p k n", p=P)).then_inc(ab_in, 16)
            pool.dma_start(wsraw[:], io["gm_ws"][0].rearrange("h i j -> i h j")).then_inc(ws_in, 16)
            nc.gpsimd.memset(wab[:, 128:240], 0.0).then_inc(ab_pad, 1)
            pool.wait_ge(stats_done, 1)
            pool.dma_start(bc8[:, 0:8], io["dn_dt_bias"].rearrange("a h d -> a (h d)").broadcast_to([P, 8])).then_inc(bc_in, 16)
            pool.dma_start(bc8[:, 8:16], io["dn_a_log"].rearrange("a h d -> a (h d)").broadcast_to([P, 8])).then_inc(bc_in, 16)
            pool.wait_ge(w_done, WOUT)
            pool.wait_ge(zsq_done, 8)
            for pr in range(TT):
                for x in range(2):
                    c = pr if x == 0 else TT - 1 - pr
                    it = 2 * pr + x
                    pool.wait_ge(em_done, it + 1)
                    if pr:
                        pool.wait_ge(o_mm, it - 1)
                    nc.gpsimd.tensor_tensor(out=qd[:, x], in0=qT[:, :, c * P:(c + 1) * P], in1=Em[:, x], op=ALU.mult).then_inc(qd_done, 1)
            pool.wait_ge(w_done, PROJ)
            pool.dma_start(fbc[:], io["final_norm"].rearrange("(a n) -> a n", a=1).broadcast_to([P, D])).then_inc(f_in, 16)

        @block.tensor
        def _(pe):
            mm = nc.tensor.matmul

            def three(out, whi_, wlo_, hi_, lo_, start, stop):
                mm(out, whi_, hi_, start=start, stop=False)
                mm(out, whi_, lo_, start=False, stop=False)
                return mm(out, wlo_, hi_, start=False, stop=stop)

            def col_slot(n, b0, b1, xw=None):
                for k in range(KT):
                    if xw is not None:
                        pe.wait_ge(x_ready, xw + k + 1)
                    for f, b in enumerate((b0, b1)):
                        last = three(ps[:, b, :], wcol(whi, n)[:, k, f * P:(f + 1) * P], wcol(wlo, n)[:, k, f * P:(f + 1) * P],
                                     xhi[:, k, :], xlo[:, k, :], k == 0, k == KT - 1)
                last.then_inc(w_done, 1)

            def row_bcast(bank, src, n, done):
                for t in range(n):
                    last = mm(ps[:, bank, t * P:(t + 1) * P], src[:, t:t + 1].broadcast_to([P, P]), ident[:], start=True, stop=True)
                last.then_inc(done, 1)

            def norm_stats(ni):
                pe.wait_ge(acc_done, 7 * ni)
                for t in range(TT):
                    last = mm(ps[:, BANK[0], t:t + 1], sqsum[:, t * P:(t + 1) * P], ones[:, 0:1], start=True, stop=True)
                last.then_inc(stats_done, 1)

            def norm_bcast(ni):
                pe.wait_ge(rstd_done, ni + 1)
                row_bcast(BANK[1], rstd, TT, rb_done)

            def ffn(u, n0):
                with pe.Fori(0, FP) as i:
                    pe.wait_ge(lo_done, i * 2 + (n0 + 1))
                    pe.wait_ge(silu_done, i + (u * FP + 1))
                    col_slot(n0, 0, 1, xw=(0 if u == 0 else 16))
                    pe.wait_ge(lo_done, i * 2 + (n0 + 2))
                    pe.wait_ge(gu_done, i + (u * FP + 1))
                    col_slot(n0 + 1, 2, 3)
                n1 = n0 + 2 * FP

                def down(n, j, first=False, last_slot=False, jn=0):
                    pe.wait_ge(lo_done, j + (n1 + 1))
                    pe.wait_ge(gulo_done, j + (u * FP + 2))
                    for o in range(KT):
                        if first and o == 4:
                            pe.wait_ge(silu_done, (u + 1) * FP + 1)
                            pe.wait_ge(gu_done, (u + 1) * FP + 1)
                        for fl in range(2):
                            g = bass.ds(j * 2 + fl, 1)
                            last = three(ps[:, BANK[o], :], wrow(whi, n, D)[:, fl, o * P:(o + 1) * P], wrow(wlo, n, D)[:, fl, o * P:(o + 1) * P],
                                         guhi[:, g, :], gulo[:, g, :], first and fl == 0, last_slot and fl == 1)
                        if last_slot and o < KT - 1:
                            last.then_inc(out_done, 1)
                    last.then_inc(w_done, 1)

                down(n1, 0, first=True)
                with pe.Fori(1, FP - 2, 2) as j:
                    down(n1 + 1, j)
                    down(n1 + 2, j + 1)
                down(n1 + FP - 2, FP - 2)
                down(n1 + FP - 1, FP - 1, last_slot=True)

            pe.wait_ge(const_done, 1)
            for t in range(TT):
                pe.wait_ge(x_in[t], 16)
                for k in range(KT):
                    last = nc.tensor.transpose(ps[:, k, t * P:(t + 1) * P], xtok[:, t, k * P:(k + 1) * P], ident[:])
            last.then_inc(xtr_done, 1)
            pe.wait_ge(vec_in, 8 * 16)
            pe.wait_ge(hx_act, 1)
            nc.tensor.transpose(ps[:, 0, 0:109], vrows[:], ident[0:109, 0:109]).then_inc(vtr_done, 1)
            pe.wait_ge(hx_dve, 1)
            pe.wait_ge(hx_act, 4)
            pe.wait_ge(hx_dve, 4)
            norm_bcast(0)
            ffn(0, F1)
            norm_stats(1)
            norm_bcast(1)

            def qkv_post(s):
                for jj in (2 * s, 2 * s + 1):
                    if jj < 8:
                        pe.wait_ge(zsq_done, jj + 1)
                        for c in range(TT):
                            last = mm(ps[:, 4, jj * 4 + c:jj * 4 + c + 1], mb[:, jj % 2, c * P:(c + 1) * P], ones[:, 0:1], start=True, stop=True)
                        last.then_inc(qk_stat, 1)
                    if jj >= 4:
                        src = kT[:, jj - 4] if jj < 8 else mb[:, jj % 2]
                        pe.wait_ge(zact_done, jj + 1)
                        if jj >= 6:
                            if jj - 2 < 8:
                                pe.wait_ge(ktok_done, jj - 5)
                            else:
                                pe.wait_ge(nkv_done, jj - 9)
                        for c in range(TT):
                            last = nc.tensor.transpose(ps[:, 5 + jj % 2, c * P:(c + 1) * P], src[:, c * P:(c + 1) * P], ident[:])
                        last.then_inc(tok_tr, 1)

            for s in range(6):
                n = WIN + s
                pe.wait_ge(lo_done, n + 1)
                if s >= 2:
                    pe.wait_ge(conv_done, 2 * s - 2)
                col_slot(n, (2 * s) % 4, (2 * s) % 4 + 1, xw=8 if s == 0 else None)
                if s == 0:
                    pe.wait_ge(ws_in, 16)
                    for h in range(HD):
                        last = nc.tensor.transpose(ps[:, 7, h * P:(h + 1) * P], wsraw[:, h], ident[:])
                    last.then_inc(ws_tr, 1)
                if s >= 1:
                    qkv_post(s - 1)
            pe.wait_ge(wab_lo, 1)
            pe.wait_ge(ws_done, 1)
            for k in range(KT):
                last = three(ps[:, 7, :], wabhi[:, k * 16:k * 16 + P], wablo[:, k * 16:k * 16 + P], xhi[:, k, :], xlo[:, k, :], k == 0, k == KT - 1)
            last.then_inc(ab_mm, 1)
            for s in range(2):
                n = WIN + 6 + s
                pe.wait_ge(lo_done, n + 1)
                if s == 0:
                    pe.wait_ge(conv_done, 12)
                for t in range(TT):
                    tok = slice(t * P, (t + 1) * P)
                    for kl in range(4):
                        k = 4 * s + kl
                        wh, wl = wrow(whi, n, 512)[:, kl], wrow(wlo, n, 512)[:, kl]
                        mm(ps[:, t, :], xhi[:, k, tok], wh, start=(k == 0), stop=False)
                        mm(ps[:, t, :], xlo[:, k, tok], wh, start=False, stop=False)
                        last = mm(ps[:, t, :], xhi[:, k, tok], wl, start=False, stop=(k == KT - 1))
                last.then_inc(w_done, 1)
                if s == 0:
                    qkv_post(5)
                    pe.wait_ge(ab_copy, 1)
                    for c in range(TT):
                        last = nc.tensor.transpose(ps[:, 7, c * 16:(c + 1) * 16], abT[:, c * P:(c + 1) * P], ident[0:16, 0:16])
                    last.then_inc(ab_tr, 1)
            for s in range(2):
                n = WIN + 8 + s
                pe.wait_ge(lo_done, n + 1)
                if s == 0:
                    pe.wait_ge(nkv_done, 4)
                    pe.wait_ge(nk_done, 1)
                col_slot(n, 4 + 2 * s if s == 0 else 0, 5 if s == 0 else 1)
                if s == 0:
                    pe.wait_ge(gate_dve, 5)
                    mm(ps[:, 7, 64:80], tri[:, 0, :], gg[:, 0:16], start=True, stop=True)
                    mm(ps[:, 7, 80:96], tri[:, 1, :], gg[:, 16:32], start=True, stop=True)
                    mm(ps[:, 7, 96:128], ones[:], gg, start=True, stop=True).then_inc(cum_done, 1)
                    pe.wait_ge(vgelu, 4)
            for s in range(2):
                n = WIN + 10 + s
                pe.wait_ge(lo_done, n + 1)
                if s == 1:
                    pe.wait_ge(ugelu, 1)
                col_slot(n, 2 + 2 * s, 3 + 2 * s)
                if s == 0:
                    pe.wait_ge(ln_done, 1)
                    pe.wait_ge(ugelu, 2)
                    pe.wait_ge(col_act, 1)
                    pe.wait_ge(col_dve, 1)
                    for h in range(HD):
                        for c in range(TT):
                            last = mm(ps[:, (0, 1, 6, 7)[h], c * P:(c + 1) * P], vg[:, c, h * P:(h + 1) * P], wsT[:, h], start=True, stop=True)
                        last.then_inc(sv_done, 1)

            for pr in range(TT):
                chunk = (pr, TT - 1 - pr)
                for x in range(2):
                    c, it = chunk[x], 2 * pr + x
                    tok = slice(c * P, (c + 1) * P)
                    if pr == 0 and x == 0:
                        pe.wait_ge(gm_done, 4)
                        pe.wait_ge(zg_done, 2)
                        pe.wait_ge(col_dve, 6)
                    if pr:
                        pe.wait_ge(r_done, it - 1)
                    for h in range(HD):
                        col = x * 16 + c * 4 + h
                        last = mm(ps[:, x, h * P:(h + 1) * P], Gc[:, col:col + 1].broadcast_to([P, P]), ident[:], start=True, stop=True)
                    last.then_inc(grow_done, 1)
                    if pr:
                        pe.wait_ge(vs_done, it - 1)
                    for h in range(HD):
                        last = mm(ps[:, 2 + x, h * P:(h + 1) * P], kT[:, h, tok], kT[:, h, tok], start=True, stop=True)
                    last.then_inc(kk_done, 1)
                    if pr:
                        pe.wait_ge(o_acc, it - 1)
                    for h in range(HD):
                        last = mm(ps[:, 4 + x, h * P:(h + 1) * P], kT[:, h, tok], qT[:, h, tok], start=True, stop=True)
                    last.then_inc(kq_done, 1)
                for x in range(2):
                    it = 2 * pr + x
                    pe.wait_ge(y1_done, it + 1)
                    pe.wait_ge(em_done, it + 1)
                    for h in range(HD):
                        last = nc.tensor.transpose(ps[:, x, h * P:(h + 1) * P], Ym[:, x, h], ident[:])
                    last.then_inc(xtr2, 1)
                for li in range(len(LEVELS)):
                    fin = li == len(LEVELS) - 1
                    for x in range(2):
                        it = 2 * pr + x
                        lv = (pr * len(LEVELS) + li) * 2 + x
                        if li == 0:
                            pe.wait_ge(x1_done, it + 1)
                            pe.wait_ge(pm_done, it + 1)
                            pe.wait_ge(nt_done, it + 1)
                        else:
                            pe.wait_ge(xy_done, lv - 1)
                        for h in range(HD):
                            last = mm(ps[:, x, h * P:(h + 1) * P], NTm[:, x, h], Xm[:, x, h], start=True, stop=True)
                        last.then_inc(t_mm, 1)
                    for x in range(2):
                        lv = (pr * len(LEVELS) + li) * 2 + x
                        pe.wait_ge(t_copy, lv + 1)
                        if not fin:
                            for h in range(HD):
                                last = mm(ps[:, 2 + x, h * P:(h + 1) * P], Ym[:, x, h], Tm[:, x, h], start=True, stop=True)
                            last.then_inc(w_mm, 1)
                        for h in range(HD):
                            last = mm(ps[:, 4 + x, h * P:(h + 1) * P], Tm[:, x, h], Ym[:, x, h], start=True, stop=True)
                        last.then_inc(wt_mm, 1)
                for x in range(2):
                    c, it = chunk[x], 2 * pr + x
                    tok = slice(c * P, (c + 1) * P)
                    pe.wait_ge(s_upd, it - 1) if pr else pe.wait_ge(s_zero, 1)
                    for h in range(HD):
                        last = mm(ps[:, x, h * P:(h + 1) * P], kT[:, h, tok], St[:, x, h], start=True, stop=True)
                    last.then_inc(ks_mm, 1)
                for x in range(2):
                    it = 2 * pr + x
                    pe.wait_ge(xy_done, ((pr + 1) * len(LEVELS) - 1) * 2 + x + 1)
                    pe.wait_ge(r_done, it + 1)
                    for h in range(HD):
                        last = mm(ps[:, 2 + x, h * P:(h + 1) * P], Ym[:, x, h], Dm[:, x, h], start=True, stop=True)
                    last.then_inc(v_mm, 1)
                for x in range(2):
                    c, it = chunk[x], 2 * pr + x
                    pe.wait_ge(qd_done, it + 1)
                    pe.wait_ge(vn_done, it + 1)
                    for h in range(HD):
                        mm(ps[:, 4 + x, h * P:(h + 1) * P], St[:, x, h], qd[:, x, h], start=True, stop=False)
                        last = mm(ps[:, 4 + x, h * P:(h + 1) * P], Em[:, x, h], Pm[:, x, h], start=False, stop=True)
                    last.then_inc(o_mm, 1)
                    if pr < TT - 1:
                        pe.wait_ge(vs_done, it + 1)
                        if pr:
                            pe.wait_ge(s_upd, it - 1)
                        for h in range(HD):
                            last = mm(ps[:, 6 + x, h * P:(h + 1) * P], ktok[:, c, h], Tm[:, x, h], start=True, stop=True)
                        last.then_inc(s_mm, 1)
            for h in range(HD):
                pe.wait_ge(osq, h + 1)
                for c in range(TT):
                    last = mm(ps[:, 6, h * 4 + c:h * 4 + c + 1], tmp[:, h, c * P:(c + 1) * P], ones[:, 0:1], start=True, stop=True)
            last.then_inc(ost, 1)
            pe.wait_ge(oscale, 1)
            for h in range(HD):
                for c in range(TT):
                    last = mm(ps[:, h, c * P:(c + 1) * P], misc[:, h * 4 + c:h * 4 + c + 1].broadcast_to([P, P]), ident[:], start=True, stop=True)
                last.then_inc(orow, 1)
            for s in range(4):
                n = WOUT + s
                pe.wait_ge(lo_done, n + 1)
                if s == 2:
                    pe.wait_ge(y_step, 8)
                for k in range(KT):
                    if s == 0:
                        pe.wait_ge(y_ready, k + 1)
                    for f in range(2):
                        o = 2 * s + f
                        last = three(ps[:, BANK[o], :], wcol(whi, n)[:, k, f * P:(f + 1) * P], wcol(wlo, n)[:, k, f * P:(f + 1) * P],
                                     xhi[:, k, :], xlo[:, k, :], k == 0, k == KT - 1)
                last.then_inc(w_done, 1)
            norm_stats(2)
            norm_bcast(2)
            ffn(1, F2)

            norm_stats(3)
            pe.wait_ge(p_in, 16)
            for kk in range(2):
                for t in range(TT):
                    last = nc.tensor.transpose(ps[:, 6 + kk, t * P:(t + 1) * P], ptok[:, t, kk * P:(kk + 1) * P], ident[:])
            last.then_inc(p_tr, 1)
            norm_bcast(3)
            pe.wait_ge(pt_lo, 1)
            pe.wait_ge(lo_done, PROJ + 1)
            for o in range(KT):
                b = (0, 1, 2, 3)[o % 4]
                if o >= 4:
                    pe.wait_ge(e_sq, o - 3)
                for kk in range(2):
                    last = three(ps[:, b, :], wrow(whi, PROJ, D)[:, kk, o * P:(o + 1) * P], wrow(wlo, PROJ, D)[:, kk, o * P:(o + 1) * P],
                                 pThi[:, kk, :], pTlo[:, kk, :], kk == 0, kk == 1)
                last.then_inc(e_mm if o < KT - 1 else w_done, 1)
            pe.wait_ge(e_sq, 8)
            def gate_slot(s):
                n = GATE + s
                pe.wait_ge(lo_done, n + 1)
                if s >= 2:
                    pe.wait_ge(sg_done, 2 * s - 2)
                col_slot(n, (2 * s) % 4, (2 * s) % 4 + 1, xw=24 if s == 0 else None)
            gate_slot(0)
            pe.wait_ge(e_acc, 7)
            for t in range(TT):
                last = mm(ps[:, BANK[0], 4 + t:5 + t], sqsum[:, t * P:(t + 1) * P], ones[:, 0:1], start=True, stop=True)
            last.then_inc(e_stats, 1)
            gate_slot(1)
            pe.wait_ge(e_rstd, 1)
            row_bcast(6, rstd[:, 4:8], TT, e_rb)
            gate_slot(2)
            gate_slot(3)
            pe.wait_ge(hf_done, 8)
            for t in range(TT):
                if t >= 2:
                    pe.wait_ge(f_out, t - 1)
                for k in range(KT):
                    last = nc.tensor.transpose(ps[:, 4 + 2 * (t % 2) + k // 4, (k % 4) * P:(k % 4 + 1) * P], hT[:, k, t * P:(t + 1) * P], ident[:])
                last.then_inc(f_tr, 1)

        @block.scalar
        def _(act):
            A = nc.scalar.activation

            def hi(n, p, cnt=None):
                act.wait_ge(raw_in[p], cnt if cnt is not None else 16 * (n // 2 + 1))
                if not isinstance(n, int) or n >= 2:
                    act.wait_ge(w_done, n - 1)
                A(whi[p][:], raw[p][:], ACT.Copy).then_inc(hi_done, 1)

            def hir(n0, i2):
                hi(i2 * 2 + n0, n0 % 2, cnt=i2 * 16 + 16 * (n0 // 2 + 1))

            def norm_std(ni):
                if ni:
                    act.wait_ge(stats_done, ni)
                    A(std[:, 0:4], ps[:, BANK[0], 0:4], ACT.Sqrt, bias=eps[:], scale=1.0 / D).then_inc(std_done, 1)
                else:
                    act.wait_ge(ss0_done, TT)
                    A(std[:, 0:4], ss[:, 0:4], ACT.Sqrt, bias=eps[:], scale=1.0 / D).then_inc(std_done, 1)

            def norm_hi(ni):
                for k in range(KT):
                    act.wait_ge(xf_done, 8 * ni + k + 1)
                    A(xhi[:, k, :], tmp[:, k % 2, :], ACT.Copy).then_inc(xhi_done, 1)

            def squares(og):
                for o in range(KT):
                    act.wait_ge(h_done, 8 * og + o + 1)
                    if o >= 4:
                        act.wait_ge(acc_done, 7 * og + max(1, o - 4))
                    A(tmp[:, o % 4, :], hT[:, o, :], ACT.Square).then_inc(sq_done, 1)

            def ffn(u, n0):
                with act.Fori(0, FP) as i:
                    act.wait_ge(w_done, i * 2 + (n0 + 1))
                    act.wait_ge(gu_done, i + (u * FP + 1))
                    A(tmp[:, 0:2, :], ps[:, 0:2, :], ACT.Silu).then_inc(silu_done, 1)
                    hir(n0 + 2, i)
                    act.wait_ge(gu_done, i + (u * FP + 2))
                    A(guhi[:, bass.ds(i * 2, 2), :], tmp[:, 2:4, :], ACT.Copy).then_inc(guhi_done, 1)
                    hir(n0 + 3, i)
                n1 = n0 + 2 * FP
                for jj in range(2, FP):
                    hi(n1 + jj, (n1 + jj) % 2)

            act.sem_inc(silu_done, 1)
            for t in range(TT):
                act.wait_ge(x_in[t], 16)
                if t:
                    act.wait_ge(ss0_done, t)
                else:
                    act.wait_ge(const_done, 2)
                A(sqjunk[:], xtok[:, t, :], ACT.Square, accum_out=ss[:, t:t + 1]).then_inc(ss0_done, 1)
            norm_std(0)
            act.wait_ge(xtr_done, 1)
            for k in range(0, KT, 2):
                A(hT[:, k, :], ps[:, k, :], ACT.Copy).then_inc(hx_act, 1)
            act.wait_ge(vtr_done, 1)
            A(cols[:], ps[:, 0, 0:109], ACT.Copy).then_inc(cols_done, 1)
            hi(F1, F1 % 2)
            hi(F1 + 1, (F1 + 1) % 2)
            norm_hi(0)
            ffn(0, F1)
            hi(WIN, WIN % 2)
            squares(0)
            norm_std(1)
            norm_hi(1)

            hi(WIN + 1, (WIN + 1) % 2)
            act.wait_ge(ab_in, 16)
            act.wait_ge(ab_pad, 1)
            A(wabhi[:], wab[:], ACT.Copy).then_inc(wab_hi, 1)
            act.wait_ge(ws_tr, 1)
            A(wsT[:], ps[:, 7, :].rearrange("p (h n) -> p h n", h=HD), ACT.Copy).then_inc(ws_done, 1)

            def ktok_evac(jj):
                act.wait_ge(tok_tr, jj - 3)
                A(ktok[:, :, jj - 4, :], ps[:, 5 + jj % 2, :].rearrange("p (c d) -> p c d", c=TT), ACT.Copy).then_inc(ktok_done, 1)

            for s in range(6):
                if s:
                    hi(WIN + s + 1, (WIN + s + 1) % 2)
                for jj in (2 * s, 2 * s + 1):
                    act.wait_ge(conv_done, jj + 1)
                    if jj < 8:
                        A((qT if jj < 4 else kT)[:, jj % 4, :], acc[:, jj % 2, :], ACT.Silu).then_inc(zact_done, 1)
                        if jj >= 2:
                            act.wait_ge(qk_stat, jj - 1)
                        act.wait_ge(zact_done, jj + 1)
                        A(mb[:, jj % 2, :], (qT if jj < 4 else kT)[:, jj % 4, :], ACT.Square).then_inc(zsq_done, 1)
                    else:
                        act.wait_ge(qk_stat, min(jj - 1, 8))
                        if jj >= 10:
                            act.wait_ge(tok_tr, jj - 5)
                        A(mb[:, jj % 2, :], acc[:, jj % 2, :], ACT.Silu).then_inc(zact_done, 1)
                if s in (3, 4):
                    for jj in (2 * s - 2, 2 * s - 1):
                        ktok_evac(jj)
                if s == 4:
                    act.wait_ge(qk_stat, 8)
                    A(nk, ps[:, 4, 16:32], ACT.Sqrt, bias=eps[:]).then_inc(nk_done, 1)
            hi(WIN + 7, (WIN + 7) % 2)
            act.wait_ge(ab_mm, 1)
            A(abT[:], ps[0:16, 7, :], ACT.Copy).then_inc(ab_copy, 1)
            hi(WIN + 8, (WIN + 8) % 2)
            abv = ps[:, 7, 0:64].rearrange("p (c j) -> p c j", j=16)
            act.wait_ge(gate_dve, 1)
            A(ea, aa, ACT.Abs).then_inc(gate_act, 1)
            act.wait_ge(gate_act, 1)
            A(ea, ea, ACT.Exp, scale=-1.0).then_inc(gate_act, 1)
            A(be.rearrange("p (c j) -> p c j", j=8), abv[:, :, 8:16], ACT.Exp, scale=-1.0).then_inc(gate_act, 1)
            act.wait_ge(bc_in, 80)
            A(bc8[:, 16:24], bc8[:, 8:16], ACT.Exp).then_inc(gate_act, 1)
            act.wait_ge(gate_act, 2)
            A(ea, ea, ACT.Ln, bias=1.0).then_inc(gate_act, 1)
            for t in range(TT):
                act.wait_ge(w_done, WIN + 8)
                A(vg[:, t, :], ps[:, t, :], ACT.Gelu_apprx_tanh).then_inc(vgelu, 1)
            hi(WIN + 9, (WIN + 9) % 2)
            act.wait_ge(cum_done, 1)
            A(eG, ps[:, 7, 64:96], ACT.Exp)
            A(egl, ps[:, 7, 96:128], ACT.Exp).then_inc(col_act, 1)
            act.wait_ge(col_dve, 2)
            A(egd, egd, ACT.Exp).then_inc(col_act, 1)
            act.wait_ge(ln_step, 17)
            A(lsd[:], mv[:, :, 1], ACT.Sqrt, bias=eps[:]).then_inc(ln_sd, 1)
            act.wait_ge(w_done, WIN + 9)
            A(uT[:, 0:2, :], ps[:, 4:6, :], ACT.Gelu_apprx_tanh).then_inc(ugelu, 1)
            hi(WIN + 10, (WIN + 10) % 2)
            act.wait_ge(w_done, WIN + 10)
            A(uT[:, 2:4, :], ps[:, 0:2, :], ACT.Gelu_apprx_tanh).then_inc(ugelu, 1)
            hi(WIN + 11, (WIN + 11) % 2)
            act.wait_ge(w_done, WIN + 11)
            A(zg[:, 0:2, :], ps[:, 2:4, :], ACT.Silu).then_inc(zg_done, 1)
            hi(WOUT, WOUT % 2)
            act.wait_ge(w_done, WIN + 12)
            A(zg[:, 2:4, :], ps[:, 4:6, :], ACT.Silu).then_inc(zg_done, 1)
            hi(WOUT + 1, (WOUT + 1) % 2)
            for h in range(HD):
                act.wait_ge(gm_done, h + 1)
                A(xhi[:, h, :], uT[:, h, :], ACT.Copy).then_inc(yhi_done, 1)

            for pr in range(TT):
                for x in range(2):
                    it = 2 * pr + x
                    act.wait_ge(grow_done, it + 1)
                    if pr:
                        act.wait_ge(o_mm, it - 1)
                    act.wait_ge(dpre_done, it + 1)
                    A(Em[:, x], ps[:, x, :].rearrange("p (h n) -> p h n", h=HD), ACT.Exp).then_inc(em_done, 1)
                    A(Dm[:, x], Dm[:, x], ACT.Exp).then_inc(dm_done, 1)
                for x in range(2):
                    act.wait_ge(xtr2, 2 * pr + x + 1)
                    A(Xm[:, x], ps[:, x, :].rearrange("p (h n) -> p h n", h=HD), ACT.Copy).then_inc(x1_done, 1)
                for li in range(len(LEVELS)):
                    for x in range(2):
                        it = 2 * pr + x
                        lv = (pr * len(LEVELS) + li) * 2 + x
                        act.wait_ge(t_mm, lv + 1)
                        if li:
                            act.wait_ge(wt_mm, lv - 1)
                        elif pr:
                            act.wait_ge(s_mm, it - 1)
                        A(Tm[:, x], ps[:, x, :].rearrange("p (h n) -> p h n", h=HD), ACT.Copy).then_inc(t_copy, 1)
                for x in range(2):
                    c, it = (pr, TT - 1 - pr)[x], 2 * pr + x
                    act.wait_ge(v_mm, it + 1)
                    act.wait_ge(qd_done, it + 1)
                    for h in range(HD):
                        col = x * 16 + c * 4 + h
                        last = A(Em[:, x, h], ps[:, 2 + x, h * P:(h + 1) * P], ACT.Copy, scale=sk[:, col:col + 1])
                    last.then_inc(vn_done, 1)
            for h in range(HD):
                act.wait_ge(o_acc, 8)
                A(tmp[:, h, :], oT[:, h, :], ACT.Square).then_inc(osq, 1)
            act.wait_ge(ost, 1)
            act.wait_ge(osd, 1)
            A(misc[:, 0:16], misc[:, 0:16], ACT.Sqrt).then_inc(osd, 1)
            for h in range(HD):
                act.wait_ge(y_step, 2 * h + 2)
                A(xhi[:, 4 + h, :], oT[:, h, :], ACT.Copy).then_inc(yhi_done, 1)
            hi(WOUT + 2, WOUT % 2)
            hi(WOUT + 3, (WOUT + 1) % 2)
            hi(F2, F2 % 2)
            squares(1)
            norm_std(2)
            hi(F2 + 1, (F2 + 1) % 2)
            norm_hi(2)
            ffn(1, F2)
            hi(PROJ, PROJ % 2)
            squares(2)
            norm_std(3)
            act.wait_ge(p_copy, 1)
            A(pThi[:], pTf[:], ACT.Copy).then_inc(pt_hi, 1)
            norm_hi(3)
            for o in range(KT):
                act.wait_ge(e_mm, o + 1) if o < KT - 1 else act.wait_ge(w_done, PROJ + 1)
                A(eT[:, o, :], ps[:, o % 4, :], ACT.Copy).then_inc(e_copy, 1)
                if o >= 2:
                    act.wait_ge(e_acc, max(1, o - 2))
                A(tmp[:, 2 + o % 2, :], ps[:, o % 4, :], ACT.Square).then_inc(e_sq, 1)
            hi(GATE, GATE % 2)
            hi(GATE + 1, (GATE + 1) % 2)
            act.wait_ge(e_stats, 1)
            A(std[:, 4:8], ps[:, BANK[0], 4:8], ACT.Sqrt, bias=eps[:], scale=1.0 / D).then_inc(e_std, 1)
            for o in range(KT):
                if o in (0, 2):
                    hi(GATE + 2 + o // 2, (GATE + o // 2) % 2)
                act.wait_ge(w_done, GATE + o // 2 + 1)
                if o >= 2:
                    act.wait_ge(ge_done, o - 1)
                A(sgm[:, o % 2, :], ps[:, o % 4, :], ACT.Sigmoid, bias=cols[:, B_GATE + o:B_GATE + o + 1]).then_inc(sg_done, 1)
            for t in range(TT):
                act.wait_ge(f_tr, t + 1)
                if t:
                    act.wait_ge(f_ss, t)
                A(fjunk[:].rearrange("p (b n) -> p b n", b=2), ps[:, 4 + 2 * (t % 2):6 + 2 * (t % 2), :], ACT.Square,
                  accum_out=ss[:, t:t + 1]).then_inc(f_ss, 1)
                act.wait_ge(f_ss, t + 1)
                A(std[:, t:t + 1], ss[:, t:t + 1], ACT.Sqrt, bias=eps[:], scale=1.0 / D).then_inc(f_std, 1)

        @block.vector
        def _(dve):
            V = nc.vector
            stt = nc.vector.scalar_tensor_tensor

            def lo(n, p):
                dve.wait_ge(hi_done, n + 1)
                V.tensor_tensor(out=wlo[p][:], in0=raw[p][:], in1=whi[p][:].bitcast(f32), op=ALU.subtract).then_inc(lo_done, 1)

            def residual(og, n_last, factor):
                for o in range(KT + 1):
                    if o < KT:
                        if og == 1:
                            dve.wait_ge(w_done, WOUT + o // 2 + 1)
                        elif o < KT - 1:
                            dve.wait_ge(out_done, 7 * (og // 2) + o + 1)
                        else:
                            dve.wait_ge(w_done, n_last + 1)
                        stt(out=hT[:, o, :], in0=ps[:, BANK[o], :], scalar=factor, in1=hT[:, o, :], op0=ALU.mult, op1=ALU.add).then_inc(h_done, 1)
                    if o >= 2:
                        dve.wait_ge(sq_done, 8 * og + o)
                        if o == 2:
                            V.tensor_tensor(out=sqsum[:], in0=tmp[:, 0, :], in1=tmp[:, 1, :], op=ALU.add).then_inc(acc_done, 1)
                        else:
                            dve.wait_ge(acc_done, 7 * og + o - 2)
                            V.tensor_tensor(out=sqsum[:], in0=sqsum[:], in1=tmp[:, (o - 1) % 4, :], op=ALU.add).then_inc(acc_done, 1)
                    if og == 1 and o in (1, 3):
                        lo(WOUT + 3 + o // 2, (WOUT + 3 + o // 2) % 2)

            def norm_apply(ni, g0):
                dve.wait_ge(std_done, ni + 1)
                V.reciprocal(rstd[:, 0:4], std[:, 0:4]).then_inc(rstd_done, 1)
                dve.wait_ge(rb_done, ni + 1)
                for k in range(KT + 1):
                    if k < KT:
                        if k >= 2:
                            dve.wait_ge(x_ready, 8 * ni + k - 1)
                        stt(out=tmp[:, k % 2, :], in0=hT[:, k, :], scalar=cols[:, g0 + k:g0 + k + 1], in1=ps[:, BANK[1], :],
                            op0=ALU.mult, op1=ALU.mult).then_inc(xf_done, 1)
                    if k:
                        dve.wait_ge(xhi_done, 8 * ni + k)
                        V.tensor_tensor(out=xlo[:, k - 1, :], in0=tmp[:, (k - 1) % 2, :], in1=xhi[:, k - 1, :].bitcast(f32),
                                        op=ALU.subtract).then_inc(x_ready, 1)

            def ffn(u, n0):
                with dve.Fori(0, FP) as i:
                    lo(i * 2 + (n0 + 2), n0 % 2)
                    dve.wait_ge(silu_done, i + (u * FP + 1))
                    dve.wait_ge(w_done, i * 2 + (n0 + 2))
                    dve.wait_ge(gulo_done, i + (u * FP + 1))
                    V.tensor_tensor(out=tmp[:, 2:4, :], in0=ps[:, 2:4, :], in1=tmp[:, 0:2, :], op=ALU.mult).then_inc(gu_done, 1)
                    dve.wait_ge(guhi_done, i + (u * FP + 1))
                    V.tensor_tensor(out=gulo[:, bass.ds(i * 2, 2), :], in0=tmp[:, 2:4, :],
                                    in1=guhi[:, bass.ds(i * 2, 2), :].bitcast(f32), op=ALU.subtract).then_inc(gulo_done, 1)
                    lo(i * 2 + (n0 + 3), (n0 + 1) % 2)
                n1 = n0 + 2 * FP
                for jj in range(2, FP):
                    lo(n1 + jj, (n1 + jj) % 2)

            dve.sem_inc(gu_done, 1)
            dve.sem_inc(gulo_done, 1)
            dve.wait_ge(xtr_done, 1)
            for k in range(1, KT, 2):
                V.tensor_copy(hT[:, k, :], ps[:, k, :]).then_inc(hx_dve, 1)
            lo(F1, F1 % 2)
            lo(F1 + 1, (F1 + 1) % 2)
            dve.wait_ge(cols_done, 1)
            dve.wait_ge(hx_dve, 4)
            dve.wait_ge(hx_act, 4)
            norm_apply(0, G_FFN1)
            ffn(0, F1)
            lo(WIN, WIN % 2)
            residual(0, WIN - 1, 0.5)
            norm_apply(1, G_MIX)

            lo(WIN + 1, (WIN + 1) % 2)
            dve.wait_ge(wab_hi, 1)
            V.tensor_tensor(out=wablo[:], in0=wab[:], in1=wabhi[:].bitcast(f32), op=ALU.subtract).then_inc(wab_lo, 1)
            taps = [0]

            def conv(jj):
                z, a = ps[:, jj % 4, :], acc[:, jj % 2, :]
                w = lambda j: cols[:, G_CONV + j * 12 + jj:G_CONV + j * 12 + jj + 1]
                dve.wait_ge(w_done, WIN + jj // 2 + 1)
                if jj >= 2:
                    dve.wait_ge(zact_done, jj - 1)
                V.tensor_scalar(a, z, w(2), None, ALU.mult).then_inc(conv_tap, 1)
                for j in (0, 1, 3, 4):
                    taps[0] += 1
                    dve.wait_ge(conv_tap, taps[0])
                    d = j - 2
                    dst = a[:, max(0, -d):T - max(0, d)]
                    last = stt(out=dst, in0=z[:, max(0, d):T - max(0, -d)], scalar=w(j), in1=dst, op0=ALU.mult, op1=ALU.add)
                    last.then_inc(conv_done if j == 4 else conv_tap, 1)

            def nkv_evac(jj):
                dve.wait_ge(tok_tr, jj - 3)
                V.tensor_tensor(out=nkv[:, :, jj - 8, :], in0=ps[:, 5 + jj % 2, :].rearrange("p (c d) -> p c d", c=TT),
                                in1=nk[:, (jj - 8) * 4:(jj - 7) * 4].unsqueeze(2).broadcast_to([P, TT, P]), op=ALU.mult).then_inc(nkv_done, 1)

            for s in range(6):
                if s:
                    lo(WIN + s + 1, (WIN + s + 1) % 2)
                conv(2 * s)
                conv(2 * s + 1)
                if s == 5:
                    dve.wait_ge(nk_done, 1)
                    V.reciprocal(rk2, nk).then_inc(rk_step, 1)
                    dve.wait_ge(rk_step, 1)
                    V.tensor_tensor(out=rk2, in0=rk2, in1=rk2, op=ALU.mult).then_inc(rk_step, 1)
                    V.tensor_scalar(misc[:, 16:32], ps[:, 4, 0:16], EPS, float(P), ALU.add, ALU.mult).then_inc(rk_step, 1)
                    nkv_evac(8)
                    nkv_evac(9)
            lo(WIN + 7, (WIN + 7) % 2)
            nkv_evac(10)
            nkv_evac(11)
            lo(WIN + 8, (WIN + 8) % 2)
            abv = ps[:, 7, 0:64].rearrange("p (c j) -> p c j", j=16)
            dve.wait_ge(ab_tr, 1)
            dve.wait_ge(bc_in, 80)
            V.tensor_tensor(out=aa.rearrange("p (c j) -> p c j", j=8), in0=abv[:, :, 0:8],
                            in1=bc8[:, 0:8].unsqueeze(1).broadcast_to([P, TT, 8]), op=ALU.add).then_inc(gate_dve, 1)
            dve.wait_ge(gate_act, 5)
            dve.wait_ge(gate_dve, 1)
            stt(out=aa, in0=aa, scalar=0.0, in1=ea, op0=ALU.max, op1=ALU.add).then_inc(gate_dve, 1)
            V.tensor_scalar(s2, be, 1.0, None, ALU.add).then_inc(gate_dve, 1)
            dve.wait_ge(gate_dve, 3)
            V.reciprocal(be, s2).then_inc(gate_dve, 1)
            for d in range(2):
                last = stt(out=gg[:, 16 * d:16 * d + 16].rearrange("p (c h) -> p c h", c=TT),
                           in0=aa.rearrange("p (c j) -> p c j", c=TT)[:, :, 4 * d:4 * d + 4], scalar=-1.0,
                           in1=bc8[:, 16 + 4 * d:20 + 4 * d].unsqueeze(1).broadcast_to([P, TT, HD]), op0=ALU.mult, op1=ALU.mult)
            last.then_inc(gate_dve, 1)
            dve.wait_ge(vgelu, 4)
            for t in range(TT):
                for h in range(HD):
                    V.bn_stats(bns[:, t * 4 + h, :], vg[:, t, h * P:(h + 1) * P]).then_inc(ln_step, 1)
            lo(WIN + 9, (WIN + 9) % 2)
            dve.wait_ge(ln_step, 16)
            for q in range(16):
                last = V.bn_aggr(mv[:, q, :], bns[:, q, :])
            last.then_inc(ln_step, 1)
            dve.wait_ge(cum_done, 1)
            dve.wait_ge(col_act, 1)
            V.tensor_copy(Gc, ps[:, 7, 64:96]).then_inc(col_dve, 1)
            dve.wait_ge(col_dve, 1)
            V.tensor_tensor(out=egd, in0=ps[:, 7, 96:128], in1=Gc, op=ALU.subtract).then_inc(col_dve, 1)
            V.tensor_scalar(neG, eG, -1.0, None, ALU.mult).then_inc(col_dve, 1)
            dve.wait_ge(rk_step, 3)
            for d in range(2):
                last = V.tensor_tensor(out=sk[:, 16 * d:16 * d + 16].rearrange("p (c h) -> p c h", c=TT),
                                       in0=be.rearrange("p (c j) -> p c j", c=TT)[:, :, 4 * d:4 * d + 4],
                                       in1=rk2.rearrange("p (h c) -> p c h", c=TT), op=ALU.mult)
            last.then_inc(col_dve, 1)
            dve.wait_ge(col_dve, 4)
            V.tensor_scalar(nsk, sk, -1.0, None, ALU.mult).then_inc(col_dve, 1)
            dve.wait_ge(col_act, 2)
            V.tensor_tensor(out=s2, in0=sk, in1=egd, op=ALU.mult).then_inc(col_dve, 1)
            dve.wait_ge(ln_sd, 1)
            V.reciprocal(lrs[:], lsd[:]).then_inc(ln_step, 1)
            dve.wait_ge(ln_step, 18)
            for t in range(TT):
                for h in range(HD):
                    q = t * 4 + h
                    V.tensor_scalar(vg[:, t, h * P:(h + 1) * P], vg[:, t, h * P:(h + 1) * P], mv[:, q, 0:1], lrs[:, q:q + 1],
                                    ALU.subtract, ALU.mult).then_inc(ln_step, 1)
            dve.wait_ge(ln_step, 34)
            V.tensor_tensor(out=vg[:], in0=vg[:], in1=lng[:].unsqueeze(1).broadcast_to([P, TT, T]), op=ALU.mult).then_inc(ln_step, 1)
            dve.wait_ge(ln_step, 35)
            V.tensor_tensor(out=vg[:], in0=vg[:], in1=lnb[:].unsqueeze(1).broadcast_to([P, TT, T]), op=ALU.add).then_inc(ln_done, 1)
            lo(WIN + 10, (WIN + 10) % 2)
            lo(WIN + 11, (WIN + 11) % 2)
            lo(WOUT, WOUT % 2)
            dve.wait_ge(ugelu, 2)
            for h in range(HD):
                dve.wait_ge(sv_done, h + 1)
                if h:
                    dve.wait_ge(gm_done, h)
                V.tensor_tensor(out=mb[:, 0, :].rearrange("p (c i) -> p c i", c=TT), in0=ps[:, (0, 1, 6, 7)[h], :].rearrange("p (c i) -> p c i", c=TT),
                                in1=bsb[:, h * P:(h + 1) * P].unsqueeze(1).broadcast_to([P, TT, P]), op=ALU.add).then_inc(gm_step, 1)
                dve.wait_ge(gm_step, h + 1)
                V.tensor_tensor(out=uT[:, h, :], in0=uT[:, h, :], in1=mb[:, 0, :], op=ALU.mult).then_inc(gm_done, 1)
            dve.wait_ge(w_done, WOUT)
            lo(WOUT + 1, (WOUT + 1) % 2)
            for h in range(HD):
                dve.wait_ge(yhi_done, h + 1)
                V.tensor_tensor(out=xlo[:, h, :], in0=uT[:, h, :], in1=xhi[:, h, :].bitcast(f32), op=ALU.subtract).then_inc(y_ready, 1)
            V.memset(St[:], 0.0).then_inc(s_zero, 1)

            ps4 = lambda b: ps[:, b, :].rearrange("p (h n) -> p h n", h=HD)
            for pr in range(TT):
                for x in range(2):
                    c, it = (pr, TT - 1 - pr)[x], 2 * pr + x
                    dve.wait_ge(grow_done, it + 1)
                    if pr:
                        dve.wait_ge(v_mm, it - 1)
                    for h in range(HD):
                        col = x * 16 + c * 4 + h
                        last = stt(out=Dm[:, x, h], in0=ps[:, x, h * P:(h + 1) * P], scalar=Gc[:, col:col + 1], in1=negm[:, x, :],
                                   op0=ALU.subtract, op1=ALU.add)
                    last.then_inc(dpre_done, 1)
                    if pr:
                        dve.wait_ge(v_mm, it - 1)
                    V.tensor_copy(Ym[:, x], ident[:].unsqueeze(1).broadcast_to([P, HD, P])).then_inc(y_init, 1)
                for x in range(2):
                    c, it = (pr, TT - 1 - pr)[x], 2 * pr + x
                    dve.wait_ge(dm_done, it + 1)
                    dve.wait_ge(kk_done, it + 1)
                    for h in range(HD):
                        col = x * 16 + c * 4 + h
                        last = stt(out=NTm[:, x, h], in0=ps[:, 2 + x, h * P:(h + 1) * P], scalar=nsk[:, col:col + 1], in1=Dm[:, x, h],
                                   op0=ALU.mult, op1=ALU.mult)
                    last.then_inc(nt_done, 1)
                    dve.wait_ge(y_init, it + 1)
                    dve.wait_ge(nt_done, it + 1)
                    V.copy_predicated(Ym[:, x], lev[:, 0, 1 - x, :].unsqueeze(1).broadcast_to([P, HD, P]), NTm[:, x]).then_inc(y1_done, 1)
                    dve.wait_ge(kq_done, it + 1)
                    if pr:
                        dve.wait_ge(o_mm, it - 1)
                    V.tensor_tensor(out=Pm[:, x], in0=ps4(4 + x), in1=Dm[:, x], op=ALU.mult).then_inc(pm_done, 1)
                for li in range(len(LEVELS)):
                    for x in range(2):
                        lv = (pr * len(LEVELS) + li) * 2 + x
                        if li < len(LEVELS) - 1:
                            dve.wait_ge(w_mm, (pr * (len(LEVELS) - 1) + li) * 2 + x + 1)
                            V.copy_predicated(Xm[:, x], lev[:, li + 1, x, :].unsqueeze(1).broadcast_to([P, HD, P]), ps4(2 + x))
                        dve.wait_ge(wt_mm, lv + 1)
                        V.copy_predicated(Ym[:, x], lev[:, li + 1, 1 - x, :].unsqueeze(1).broadcast_to([P, HD, P]), ps4(4 + x)).then_inc(xy_done, 1)
                for x in range(2):
                    c, it = (pr, TT - 1 - pr)[x], 2 * pr + x
                    dve.wait_ge(ks_mm, it + 1)
                    dve.wait_ge(pm_done, it + 1)
                    for h in range(HD):
                        col = x * 16 + c * 4 + h
                        last = stt(out=Dm[:, x, h], in0=ps[:, x, h * P:(h + 1) * P], scalar=neG[:, col:col + 1], in1=nkv[:, c, h],
                                   op0=ALU.mult, op1=ALU.add)
                    last.then_inc(r_done, 1)
                for x in range(2):
                    c, it = (pr, TT - 1 - pr)[x], 2 * pr + x
                    dve.wait_ge(vn_done, it + 1)
                    V.tensor_tensor(out=Tm[:, x], in0=ps4(2 + x), in1=s2[:, x * 16 + c * 4:x * 16 + c * 4 + 4].unsqueeze(2).broadcast_to([P, HD, P]),
                                    op=ALU.mult).then_inc(vs_done, 1)
                for x in range(2):
                    c, it = (pr, TT - 1 - pr)[x], 2 * pr + x
                    dst = oT[:, :, c * P:(c + 1) * P]
                    dve.wait_ge(o_mm, it + 1)
                    if pr < 2:
                        V.tensor_copy(dst, ps4(4 + x)).then_inc(o_acc, 1)
                    else:
                        dve.wait_ge(o_acc, 2 * (TT - 1 - pr) + 2)
                        V.tensor_tensor(out=dst, in0=ps4(4 + x), in1=dst, op=ALU.add).then_inc(o_acc, 1)
                    if pr < TT - 1:
                        dve.wait_ge(s_mm, it + 1)
                        for h in range(HD):
                            col = x * 16 + c * 4 + h
                            last = stt(out=St[:, x, h], in0=St[:, x, h], scalar=egl[:, col:col + 1], in1=ps[:, 6 + x, h * P:(h + 1) * P],
                                       op0=ALU.mult, op1=ALU.add)
                        last.then_inc(s_upd, 1)
            dve.wait_ge(ost, 1)
            V.tensor_scalar(misc[:, 16:32], misc[:, 16:32], EPS, None, ALU.mult).then_inc(rk_step, 1)
            dve.wait_ge(rk_step, 4)
            stt(out=misc[:, 0:16], in0=ps[:, 6, 0:16], scalar=1.0 / P, in1=misc[:, 16:32], op0=ALU.mult, op1=ALU.add).then_inc(osd, 1)
            dve.wait_ge(osd, 2)
            V.reciprocal(misc[:, 0:16], misc[:, 0:16]).then_inc(oscale, 1)
            for h in range(HD):
                dve.wait_ge(orow, h + 1)
                stt(out=oT[:, h, :], in0=oT[:, h, :], scalar=cols[:, G_OUT:G_OUT + 1], in1=ps[:, h, :], op0=ALU.mult, op1=ALU.mult).then_inc(y_step, 1)
                dve.wait_ge(y_step, 2 * h + 1)
                V.tensor_tensor(out=oT[:, h, :], in0=oT[:, h, :], in1=zg[:, h, :], op=ALU.mult).then_inc(y_step, 1)
                if h:
                    dve.wait_ge(yhi_done, 4 + h)
                    V.tensor_tensor(out=xlo[:, 3 + h, :], in0=oT[:, h - 1, :], in1=xhi[:, 3 + h, :].bitcast(f32), op=ALU.subtract).then_inc(y_ready, 1)
            dve.wait_ge(yhi_done, 8)
            V.tensor_tensor(out=xlo[:, 7, :], in0=oT[:, 3, :], in1=xhi[:, 7, :].bitcast(f32), op=ALU.subtract).then_inc(y_ready, 1)
            lo(WOUT + 2, WOUT % 2)
            residual(1, None, 1.0)
            norm_apply(2, G_FFN2)
            lo(F2 + 1, (F2 + 1) % 2)
            ffn(1, F2)
            lo(PROJ, PROJ % 2)
            residual(2, PROJ - 1, 0.5)
            dve.wait_ge(p_tr, 1)
            V.tensor_copy(pTf[:], ps[:, 6:8, :]).then_inc(p_copy, 1)
            dve.wait_ge(pt_hi, 1)
            V.tensor_tensor(out=pTlo[:], in0=pTf[:], in1=pThi[:].bitcast(f32), op=ALU.subtract).then_inc(pt_lo, 1)
            norm_apply(3, G_GATE)
            for o in range(1, KT):
                dve.wait_ge(e_sq, o + 1)
                if o == 1:
                    V.tensor_tensor(out=sqsum[:], in0=tmp[:, 2, :], in1=tmp[:, 3, :], op=ALU.add).then_inc(e_acc, 1)
                else:
                    dve.wait_ge(e_acc, o - 1)
                    V.tensor_tensor(out=sqsum[:], in0=sqsum[:], in1=tmp[:, 2 + o % 2, :], op=ALU.add).then_inc(e_acc, 1)
            lo(GATE, GATE % 2)
            lo(GATE + 1, (GATE + 1) % 2)
            dve.wait_ge(e_std, 1)
            V.reciprocal(rstd[:, 4:8], std[:, 4:8]).then_inc(e_rstd, 1)
            lo(GATE + 2, GATE % 2)
            dve.wait_ge(e_rb, 1)
            for o in range(KT):
                dve.wait_ge(e_copy, 8)
                stt(out=eT[:, o, :], in0=eT[:, o, :], scalar=cols[:, G_PLE + o:G_PLE + o + 1], in1=ps[:, 6, :], op0=ALU.mult, op1=ALU.mult).then_inc(en_done, 1)
            for o in range(KT):
                if o == 2:
                    lo(GATE + 3, (GATE + 1) % 2)
                dve.wait_ge(sg_done, o + 1)
                dve.wait_ge(en_done, 8)
                V.tensor_tensor(out=eT[:, o, :], in0=eT[:, o, :], in1=sgm[:, o % 2, :], op=ALU.mult).then_inc(ge_done, 1)
                dve.wait_ge(ge_done, o + 1)
                V.tensor_tensor(out=hT[:, o, :], in0=hT[:, o, :], in1=eT[:, o, :], op=ALU.add).then_inc(hf_done, 1)
            dve.wait_ge(f_in, 16)
            for t in range(TT):
                dve.wait_ge(f_std, t + 1)
                V.reciprocal(rstd[:, t:t + 1], std[:, t:t + 1]).then_inc(f_rstd, 1)
                dve.wait_ge(f_rstd, t + 1)
                if t >= 2:
                    dve.wait_ge(stored[t % 2], 16 * (t // 2))
                stt(out=otile[:, t % 2, :].rearrange("p (b n) -> p b n", b=2), in0=ps[:, 4 + 2 * (t % 2):6 + 2 * (t % 2), :],
                    scalar=rstd[:, t:t + 1], in1=fbc[:].rearrange("p (b n) -> p b n", b=2), op0=ALU.mult, op1=ALU.mult).then_inc(f_out, 1)


_INS = ["x", "p", "ffn1_norm", "ffn1_w_gate", "ffn1_w_up", "ffn1_w_down", "mix_norm", "w_in", "gm_ln_g", "gm_ln_b", "gm_ws",
        "gm_bs", "dn_conv_w", "dn_a_log", "dn_dt_bias", "dn_out_norm", "w_out", "ffn2_norm", "ffn2_w_gate", "ffn2_w_up",
        "ffn2_w_down", "ple_proj", "ple_norm", "ple_gate_norm", "ple_gate_w", "ple_gate_b", "final_norm"]


def kernel(**inputs):
    import numpy as np
    import concourse.bacc as bacc
    from concourse.bass_utils import run_bass_kernel_spmd as run

    nc = bacc.Bacc("TRN2", target_bir_lowering=False, num_devices=1)
    arrays, io = {}, {}
    for name in _INS:
        a = np.ascontiguousarray(inputs[name])
        arrays[f"in_{name}"] = a
        io[name] = nc.dram_tensor(f"in_{name}", a.shape, mybir.dt.from_np(a.dtype), kind="ExternalInput").ap()
    io["out"] = nc.dram_tensor("out_0", (1, T, D), mybir.dt.float32, kind="ExternalOutput").ap()
    build(nc, io)
    r = run(nc, [arrays], core_ids=[0])
    return r.results[0]["out_0"]
```

```python
import concourse.bass as bass
from concourse import mybir
from contextlib import ExitStack

P = 128
D = 1024
KT = D // P
T = 512
TT = T // P
FF = 2816
FP = FF // (2 * P)
HD = 4
NJ = 16
PLE = 256
EPS = 1e-6
CONV = 5
NEG = -1e30

F1 = 0
WIN = F1 + 3 * FP
WOUT = WIN + 12
F2 = WOUT + 4
PROJ = F2 + 3 * FP
GATE = PROJ + 1
NSLOT = GATE + 4
B = 32
NB = P // B
NI = 2 * TT * HD * NB
assert NI == P


def build(nc, io):
    f32, f32r, i8 = mybir.dt.float32, mybir.dt.float32r, mybir.dt.int8
    ALU, ACT = mybir.AluOpType, mybir.ActivationFunctionType
    ctx = ExitStack()
    with ctx:
        cursor = [(nc.sbuf_base + 63) // 64 * 64]

        def sb(name, shape, dt=f32, offset=None):
            n = 1 if dt == i8 else 4
            for s in shape[1:]:
                n *= s
            if offset is None:
                offset = cursor[0]
                cursor[0] += (n + 63) // 64 * 64
            return nc.alloc_sbuf_tensor_at(name, shape, dt, offset=offset)

        def sem(name):
            return ctx.enter_context(nc.semaphore(name))

        hT = sb("hT", [P, KT, T])
        x_at = cursor[0]
        xhi = sb("xhi", [P, KT, T], f32r)
        xlo = sb("xlo", [P, KT, T], f32r)
        raw = [sb(f"raw{i}", [P, 2048]) for i in range(2)]
        whi = [sb(f"whi{i}", [P, 2048], f32r) for i in range(2)]
        wlo = [sb(f"wlo{i}", [P, 2048], f32r) for i in range(2)]
        ident = sb("ident", [P, P])
        ones = sb("ones", [P, P])
        eps = sb("eps", [P, 1])
        cols = sb("cols", [P, 109])
        tri = sb("tri", [P, 2, P])
        negm = sb("negm", [P, 2, P])
        lev = sb("lev", [P, 2, 2, P], i8)
        sgn = sb("sgn", [P, 1])
        ss = sb("ss", [P, 8])
        std = sb("std", [P, 8])
        rstd = sb("rstd", [P, 8])
        ptok = sb("ptok", [P, TT, PLE])
        sqsum = sb("sqsum", [P, T])
        tmp_at = cursor[0]
        tmp = sb("tmp", [P, 4, T])
        arena = cursor[0]
        G_FFN1, G_MIX, G_FFN2, G_GATE, G_PLE, B_GATE, G_CONV, G_OUT = 0, 8, 16, 24, 32, 40, 48, 108

        guhi = sb("guhi", [P, 2 * FP, T], f32r)
        gulo = sb("gulo", [P, 2 * FP, T], f32r)
        end = cursor[0]
        assert end <= nc.sbuf_usable_end, (end, nc.sbuf_usable_end)
        cursor[0] = arena
        xtok = sb("xtok", [P, TT, D])
        vrows = sb("vrows", [109, P])
        sqjunk = sb("sqjunk", [P, D])
        cursor[0] = arena
        qT = sb("qT", [P, HD, T])
        kT = sb("kT", [P, HD, T])
        ktok = sb("ktok", [P, TT, HD, P])
        nkv = sb("nkv", [P, TT, HD, P])
        zg_at = cursor[0]
        zg = sb("zg", [P, HD, T])
        uT_at = cursor[0]
        uT = sb("uT", [P, HD, T])
        oT_at = cursor[0]
        oT = sb("oT", [P, HD, T])
        St = sb("St", [P, 2, HD, P])
        nx_at = cursor[0]
        NTm = sb("NTm", [P, 2, HD, P])
        vn = sb("vn", [P, 2, HD, P])
        vg = sb("vg", [P, TT, T], offset=nx_at)
        d_at = cursor[0]
        Dm = sb("Dm", [P, 2, HD, P])
        Em = sb("Em", [P, 2, HD, P])
        wab = sb("wab", [P, 240], offset=d_at)
        wabhi = sb("wabhi", [P, 240], f32r, offset=d_at + 960)
        wablo = sb("wablo", [P, 240], f32r, offset=d_at + 1920)
        abT = sb("abT", [16, T], offset=d_at + 2880)
        bns = sb("bns", [P, 16, 6], offset=d_at + 4928)
        mv = sb("mv", [P, 16, 2], offset=d_at + 5312)
        lsd = sb("lsd", [P, 16], offset=d_at + 5440)
        lrs = sb("lrs", [P, 16], offset=d_at + 5504)
        t_at = cursor[0]
        Tm = sb("Tm", [P, 2, HD, P])
        wsraw = sb("wsraw", [P, HD, P], offset=t_at)
        wsT = sb("wsT", [P, HD, P])
        xb_at = cursor[0]
        lng = sb("lng", [P, T])
        lnb = sb("lnb", [P, T])
        xb = sb("xb", [P, 2, TT, HD, B], offset=xb_at)
        bsb = sb("bsb", [P, T])
        kkd = sb("kkd", [P, TT, HD, B], offset=uT_at)
        gsT = sb("gsT", [32, 2, P], offset=uT_at + 2048)
        Xi = sb("Xi", [P, B, B], offset=oT_at)
        Zi = sb("Zi", [P, B, B], offset=oT_at + 4096)
        prod = sb("prod", [P, 256], offset=zg_at)
        gsi = sb("gsi", [P, 2, B], offset=zg_at + 1024)
        gi, si = gsi[:, 0, :], gsi[:, 1, :]
        Ei = sb("Ei", [P, B, B], offset=zg_at + 2048)
        assert cursor[0] <= end
        Pm = sb("Pm", [P, 2, 2, HD, P], offset=x_at)
        qd = sb("qd", [P, 2, 2, HD, P], offset=x_at + 8192)
        Rm = sb("Rm", [P, 2, 2, HD, P], offset=x_at + 16384)
        Om = sb("Om", [P, 2, 2, HD, P], offset=x_at + 24576)
        acc = sb("acc", [P, 2, T], offset=tmp_at)
        mb = sb("mb", [P, 2, T], offset=tmp_at + 4096)
        rhs = sb("rhs", [P, 2, HD, P], offset=tmp_at)
        vs = sb("vs", [P, 2, HD, P], offset=tmp_at + 4096)
        small = sb("small", [P, 15, 32], offset=tmp_at - 2048)
        (aa, ea, gg, be, Gc, nsk, eG, neG, egl, egd, sk, s2, misc, bc8, misc2) = [small[:, i, :] for i in range(15)]
        nk = misc2[:, 0:16]
        rk2 = misc2[:, 16:32]
        cursor[0] = arena
        eT = sb("eT", [P, KT, T])
        pThi = sb("pThi", [P, 2, T], f32r)
        pTlo = sb("pTlo", [P, 2, T], f32r)
        fbc = sb("fbc", [P, D])
        otile = sb("otile", [P, 2, D])
        fjunk = sb("fjunk", [P, D])
        sgm = sb("sgm", [P, 2, T])
        pTf = sb("pTf", [P, 2, T])
        assert cursor[0] <= end

        ps = ctx.enter_context(nc.psum_tensor("ps", [P, 8, T], f32))

        raw_in = [sem("raw_in0"), sem("raw_in1")]
        hi_done, lo_done, w_done = sem("hi_done"), sem("lo_done"), sem("w_done")
        x_in = [sem(f"x_in{t}") for t in range(TT)]
        vec_in, bc_in, ab_in, ws_in, p_in, f_in = [sem(s) for s in ("vec_in", "bc_in", "ab_in", "ws_in", "p_in", "f_in")]
        const_step, const_done = sem("const_step"), sem("const_done")
        xtr_done, vtr_done, hx_act, hx_dve, cols_done, ss0_done = [
            sem(s) for s in ("xtr_done", "vtr_done", "hx_act", "hx_dve", "cols_done", "ss0_done")]
        silu_done, gu_done, guhi_done, gulo_done = [sem(s) for s in ("silu_done", "gu_done", "guhi_done", "gulo_done")]
        out_done, h_done, sq_done, acc_done = [sem(s) for s in ("out_done", "h_done", "sq_done", "acc_done")]
        stats_done, std_done, rstd_done, rb_done = [sem(s) for s in ("stats_done", "std_done", "rstd_done", "rb_done")]
        xf_done, xhi_done, x_ready = sem("xf_done"), sem("xhi_done"), sem("x_ready")
        conv_tap, conv_done, zact_done, zsq_done, qk_stat, tok_tr, ktok_done, nkv_done = [
            sem(s) for s in ("conv_tap", "conv_done", "zact_done", "zsq_done", "qk_stat", "tok_tr", "ktok_done", "nkv_done")]
        nk_done, rk_step = sem("nk_done"), sem("rk_step")
        ab_pad = sem("ab_pad")
        wab_hi, wab_lo, ab_mm, ab_copy, ab_tr = [sem(s) for s in ("wab_hi", "wab_lo", "ab_mm", "ab_copy", "ab_tr")]
        gate_act, gate_dve, cum_done, col_act, col_dve = [sem(s) for s in ("gate_act", "gate_dve", "cum_done", "col_act", "col_dve")]
        vgelu, ln_step, ln_sd, ln_done, ws_tr, ws_done, ugelu, sv_done, gm_step, gm_done = [
            sem(s) for s in ("vgelu", "ln_step", "ln_sd", "ln_done", "ws_tr", "ws_done", "ugelu", "sv_done", "gm_step", "gm_done")]
        zg_done = sem("zg_done")
        tap0 = sem("tap0")
        kkd_mm, kkd_done, gs_tr, gs_done, kin_in, gin_in, zi_dve, zi_exp, xi_init, xi_step, xi_done = [
            sem(s) for s in ("kkd_mm", "kkd_done", "gs_tr", "gs_done", "kin_in", "gin_in", "zi_dve", "zi_exp", "xi_init", "xi_step", "xi_done")]
        kk_stored, inv_stored = sem("kk_stored"), sem("inv_stored")
        xb_in, r_zero, r_init = sem("xb_in"), sem("r_zero"), sem("r_init")
        grow_done, kk_done, kq_done, dpre_done, dm_done, em_done, pm_done, nt_done = [
            sem(s) for s in ("grow_done", "kk_done", "kq_done", "dpre_done", "dm_done", "em_done", "pm_done", "nt_done")]
        qd_done, o_tr, o_init = sem("qd_done"), sem("o_transposed"), sem("o_init")
        t_mm, t_copy, w_mm, x_upd, wt_mm, y_upd = [sem(s) for s in ("t_mm", "t_copy", "w_mm", "x_upd", "wt_mm", "y_upd")]
        s_zero, ks_mm, r_done, v_mm, vn_done, vs_done, o_mm, s_mm, s_upd, o_acc = [
            sem(s) for s in ("s_zero", "ks_mm", "r_done", "v_mm", "vn_done", "vs_done", "o_mm", "s_mm", "s_upd", "o_acc")]
        osq, ost, osd, oscale, orow, y_step, yhi_done, y_ready = [
            sem(s) for s in ("osq", "ost", "osd", "oscale", "orow", "y_step", "yhi_done", "y_ready")]
        p_tr, p_copy, pt_hi, pt_lo, e_mm, e_copy, e_sq, e_acc = [
            sem(s) for s in ("p_tr", "p_copy", "pt_hi", "pt_lo", "e_mm", "e_copy", "e_sq", "e_acc")]
        e_stats, e_std, e_rstd, e_rb, en_done = [sem(s) for s in ("e_stats", "e_std", "e_rstd", "e_rb", "en_done")]
        g_mm, sg_done, ge_done, hf_done, f_tr, f_ss, f_std, f_rstd, f_out, *stored = [
            sem(s) for s in ("g_mm", "sg_done", "ge_done", "hf_done", "f_tr", "f_ss", "f_std", "f_rstd", "f_out", "stored0")] + [sem("stored1")]

        block = ctx.enter_context(nc.Block())
        own = lambda d, b: slice(64 * d + 16 * b, 64 * d + 16 * b + 16)
        ch = lambda jj: jj if jj >= 8 else (jj + 4) % 8
        BANK = [(o + 4) % 8 for o in range(KT)]

        def wcol(w, n):
            return w[n % 2][:].rearrange("p (k n) -> p k n", n=256)

        def wrow(w, n, c):
            return w[n % 2][:].rearrange("p (k n) -> p k n", n=c)

        @block.sync
        def _(sp):
            def load(n, p, src, dst=None):
                if not isinstance(n, int) or n >= 2:
                    sp.wait_ge(lo_done, n - 1)
                sp.dma_start(raw[p][:].rearrange("p (k n) -> p k n", n=dst or 256), src).then_inc(raw_in[p], 16)

            def col_pair(w, i):
                return w[:, bass.ds(i * 256, 256)].rearrange("(k p) n -> p k n", p=P)

            def row_pair(w, j):
                return w[bass.ds(j * 256, 256), :].rearrange("(f p) n -> p f n", p=P)

            def ffn(n0, wg, wu, wd):
                load(n0, n0 % 2, col_pair(wg, 0))
                load(n0 + 1, (n0 + 1) % 2, col_pair(wu, 0))
                with sp.Fori(1, FP) as i:
                    load(i * 2 + n0, n0 % 2, col_pair(wg, i))
                    load(i * 2 + (n0 + 1), (n0 + 1) % 2, col_pair(wu, i))
                n1 = n0 + 2 * FP
                with sp.Fori(0, FP - 1, 2) as j:
                    load(j + n1, n1 % 2, row_pair(wd, j), D)
                    load(j + (n1 + 1), (n1 + 1) % 2, row_pair(wd, j + 1), D)
                load(n1 + FP - 1, (n1 + FP - 1) % 2, row_pair(wd, FP - 1), D)

            xv = io["x"][0].rearrange("(t p) n -> p t n", p=P)
            for t in range(TT):
                sp.dma_start(xtok[:, t, :], xv[:, t, :]).then_inc(x_in[t], 16)
            ffn(F1, io["ffn1_w_gate"][0], io["ffn1_w_up"][0], io["ffn1_w_down"][0])
            wi = io["w_in"][0]
            for s, c0 in enumerate((1536, 1792, 1024, 1280, 2048, 2304)):
                load(WIN + s, (WIN + s) % 2, wi[:, c0:c0 + 256].rearrange("(k p) n -> p k n", p=P))
            for s in range(2):
                load(WIN + 6 + s, (WIN + 6 + s) % 2, wi[512 * s:512 * (s + 1), 512:1024].rearrange("(k p) n -> p k n", p=P), 512)
            for s, c0 in enumerate((0, 256, 2560, 2816)):
                load(WIN + 8 + s, (WIN + 8 + s) % 2, wi[:, c0:c0 + 256].rearrange("(k p) n -> p k n", p=P))
            for s in range(4):
                load(WOUT + s, (WOUT + s) % 2, col_pair(io["w_out"][0], s))
            ffn(F2, io["ffn2_w_gate"][0], io["ffn2_w_up"][0], io["ffn2_w_down"][0])
            load(PROJ, PROJ % 2, row_pair(io["ple_proj"][0], 0), D)
            for s in range(4):
                load(GATE + s, (GATE + s) % 2, col_pair(io["ple_gate_w"][0], s))
            ov = io["out"][0].rearrange("(t p) n -> p t n", p=P)
            for t in range(TT):
                sp.wait_ge(f_out, t + 1)
                sp.dma_start(ov[:, t, :], otile[:, t % 2, :]).then_inc(stored[t % 2], 16)
            for half in stored:
                sp.wait_ge(half, 16 * (TT // 2))

        @block.gpsimd
        def _(pool):
            step = [0]

            def fill(ap, v):
                nc.gpsimd.memset(ap, v).then_inc(const_step, 1)
                step[0] += 1

            def sel(ap, pattern, base, cm, op, fillv):
                pool.wait_ge(const_step, step[0])
                nc.gpsimd.affine_select(out=ap, in_=ap, pattern=pattern, compare_op=op, fill=fillv, base=base,
                                        channel_multiplier=cm).then_inc(const_step, 1)
                step[0] += 1

            fill(ones[:], 1.0)
            fill(eps[:], EPS)
            fill(sgn[:], -1.0)
            fill(ident[:], 0.0)
            sel(ident[:], [[-1, P]], 0, 1, ALU.not_equal, 1.0)
            pool.wait_ge(const_step, step[0])
            nc.gpsimd.memset(sgn[0:64, :], 1.0).then_inc(const_done, 1)
            pool.wait_ge(const_done, 1)
            fill(tri[:], 1.0)
            fill(negm[:], 0.0)
            for d, sg in ((0, 1), (1, -1)):
                sel(tri[:, d, :], [[sg, P]], 0, -sg, ALU.is_ge, 0.0)
                sel(negm[:, d, :], [[sg, P]], 0, -sg, ALU.is_ge, NEG)
            fill(lev[:], 0.0)
            for l in range(2):
                s = B << l
                v = lev[:, l, :, :].rearrange("p d (b e r) -> p d b e r", e=2, r=s)
                for d in range(2):
                    part = v[:, d, :, d, :]
                    pool.wait_ge(const_step, step[0])
                    fill(part, 1.0)
                    lo = s if d == 0 else 0
                    sel(part, [[-2 * s, P // (2 * s)], [0, s]], -lo, 1, ALU.is_ge, 0.0)
                    sel(part, [[2 * s, P // (2 * s)], [0, s]], lo + s - 1, -1, ALU.is_ge, 0.0)
            pool.wait_ge(const_step, step[0])
            pool.sem_inc(const_done, 1)
            pool.dma_start(ptok[:], io["p"][0, 0].rearrange("(t p) n -> p t n", p=P)).then_inc(p_in, 16)
            pool.wait_ge(w_done, WIN)
            pool.wait_ge(gulo_done, FP + 1)
            pool.dma_start(lng[:], io["gm_ln_g"].rearrange("a h d -> a (h d)").broadcast_to([P, T])).then_inc(bc_in, 16)
            pool.dma_start(lnb[:], io["gm_ln_b"].rearrange("a h d -> a (h d)").broadcast_to([P, T])).then_inc(bc_in, 16)
            pool.dma_start(bsb[:], io["gm_bs"].rearrange("a h d -> a (h d)").broadcast_to([P, T])).then_inc(bc_in, 16)
            pool.dma_start(wab[:, 0:128].rearrange("p (k n) -> p k n", n=16),
                           io["w_in"][0][:, 3072:3088].rearrange("(k p) n -> p k n", p=P)).then_inc(ab_in, 16)
            pool.dma_start(wsraw[:], io["gm_ws"][0].rearrange("h i j -> i h j")).then_inc(ws_in, 16)
            nc.gpsimd.memset(wab[:, 128:240], 0.0).then_inc(ab_pad, 1)
            pool.wait_ge(stats_done, 1)
            pool.dma_start(bc8[:, 0:8], io["dn_dt_bias"].rearrange("a h d -> a (h d)").broadcast_to([P, 8])).then_inc(bc_in, 16)
            pool.dma_start(bc8[:, 8:16], io["dn_a_log"].rearrange("a h d -> a (h d)").broadcast_to([P, 8])).then_inc(bc_in, 16)
            pool.wait_ge(kkd_done, 16)
            pool.dma_start(io["kk_rows"], kkd[:].rearrange("p c h i -> p (c h) i")).then_inc(kk_stored, 16)
            pool.wait_ge(kk_stored, 16)
            for d in range(2):
                for b in range(NB):
                    pool.dma_start(Zi[own(d, b)], io["kk_rows"][b * B:(b + 1) * B].rearrange("j q i -> q j i")).then_inc(kin_in, 16)
            pool.wait_ge(xi_done, 1)
            pool.dma_start(io["inv_rows"], Xi[:]).then_inc(inv_stored, 16)
            pool.wait_ge(inv_stored, 16)
            pool.wait_ge(ln_done, 1)
            for d in range(2):
                for b in range(NB):
                    pool.dma_start(xb[b * B:(b + 1) * B, d].rearrange("j c h i -> j (c h) i"),
                                   io["inv_rows"][own(d, b)].rearrange("q j i -> j q i")).then_inc(xb_in, 16)
            pool.wait_ge(w_done, WOUT)
            pool.wait_ge(zsq_done, 8)

            def blocks(pr):
                for x in range(2):
                    c, it = (pr, TT - 1 - pr)[x], 2 * pr + x
                    if it:
                        pool.wait_ge(r_init, it)
                    if pr >= 2:
                        pool.wait_ge(v_mm, it - 3)
                    nc.gpsimd.memset(Rm[:, pr % 2, x], 0.0).then_inc(r_zero, 1)
                    if pr == 0 and x == 0:
                        pool.wait_ge(xb_in, 16 * 8)
                    pool.wait_ge(r_zero, it + 1)
                    for b in range(NB):
                        last = nc.gpsimd.tensor_copy(Rm[b * B:(b + 1) * B, pr % 2, x, :, b * B:(b + 1) * B], xb[b * B:(b + 1) * B, x, c])
                    last.then_inc(r_init, 1)

            blocks(0)
            for pr in range(TT):
                if pr < TT - 1:
                    blocks(pr + 1)
                pool.wait_ge(r_init, min(2 * pr + 4, 8))
                for x in range(2):
                    c = pr if x == 0 else TT - 1 - pr
                    it = 2 * pr + x
                    pool.wait_ge(em_done, it + 1)
                    if pr >= 2:
                        pool.wait_ge(o_mm, it - 3)
                    nc.gpsimd.tensor_tensor(out=qd[:, pr % 2, x], in0=qT[:, :, c * P:(c + 1) * P], in1=Em[:, x], op=ALU.mult).then_inc(qd_done, 1)
            pool.wait_ge(w_done, PROJ)
            pool.dma_start(fbc[:], io["final_norm"].rearrange("(a n) -> a n", a=1).broadcast_to([P, D])).then_inc(f_in, 16)

        @block.tensor
        def _(pe):
            mm = nc.tensor.matmul

            def three(out, whi_, wlo_, hi_, lo_, start, stop):
                mm(out, whi_, hi_, start=start, stop=False)
                mm(out, whi_, lo_, start=False, stop=False)
                return mm(out, wlo_, hi_, start=False, stop=stop)

            def col_slot(n, b0, b1, xw=None):
                for k in range(KT):
                    if xw is not None:
                        pe.wait_ge(x_ready, xw + k + 1)
                    for f, b in enumerate((b0, b1)):
                        last = three(ps[:, b, :], wcol(whi, n)[:, k, f * P:(f + 1) * P], wcol(wlo, n)[:, k, f * P:(f + 1) * P],
                                     xhi[:, k, :], xlo[:, k, :], k == 0, k == KT - 1)
                last.then_inc(w_done, 1)

            def row_bcast(bank, src, n, done):
                for t in range(n):
                    last = mm(ps[:, bank, t * P:(t + 1) * P], src[:, t:t + 1].broadcast_to([P, P]), ident[:], start=True, stop=True)
                last.then_inc(done, 1)

            def norm_stats(ni):
                pe.wait_ge(acc_done, 7 * ni)
                for t in range(TT):
                    last = mm(ps[:, BANK[0], t:t + 1], sqsum[:, t * P:(t + 1) * P], ones[:, 0:1], start=True, stop=True)
                last.then_inc(stats_done, 1)

            def norm_bcast(ni):
                pe.wait_ge(rstd_done, ni + 1)
                row_bcast(BANK[1], rstd, TT, rb_done)

            def ffn(u, n0):
                with pe.Fori(0, FP) as i:
                    pe.wait_ge(lo_done, i * 2 + (n0 + 1))
                    pe.wait_ge(silu_done, i + (u * FP + 1))
                    col_slot(n0, 0, 1, xw=(0 if u == 0 else 16))
                    pe.wait_ge(lo_done, i * 2 + (n0 + 2))
                    pe.wait_ge(gu_done, i + (u * FP + 1))
                    col_slot(n0 + 1, 2, 3)
                n1 = n0 + 2 * FP

                def down(n, j, first=False, last_slot=False, jn=0):
                    pe.wait_ge(lo_done, j + (n1 + 1))
                    pe.wait_ge(gulo_done, j + (u * FP + 2))
                    for o in range(KT):
                        if first and o == 4:
                            pe.wait_ge(silu_done, (u + 1) * FP + 1)
                            pe.wait_ge(gu_done, (u + 1) * FP + 1)
                        for fl in range(2):
                            g = bass.ds(j * 2 + fl, 1)
                            last = three(ps[:, BANK[o], :], wrow(whi, n, D)[:, fl, o * P:(o + 1) * P], wrow(wlo, n, D)[:, fl, o * P:(o + 1) * P],
                                         guhi[:, g, :], gulo[:, g, :], first and fl == 0, last_slot and fl == 1)
                        if last_slot and o < KT - 1:
                            last.then_inc(out_done, 1)
                    last.then_inc(w_done, 1)

                down(n1, 0, first=True)
                with pe.Fori(1, FP - 2, 2) as j:
                    down(n1 + 1, j)
                    down(n1 + 2, j + 1)
                down(n1 + FP - 2, FP - 2)
                down(n1 + FP - 1, FP - 1, last_slot=True)

            pe.wait_ge(const_done, 1)
            for t in range(TT):
                pe.wait_ge(x_in[t], 16)
                for k in range(KT):
                    last = nc.tensor.transpose(ps[:, k, t * P:(t + 1) * P], xtok[:, t, k * P:(k + 1) * P], ident[:])
            last.then_inc(xtr_done, 1)
            pe.wait_ge(vec_in, 8 * 16)
            pe.wait_ge(hx_act, 1)
            nc.tensor.transpose(ps[:, 0, 0:109], vrows[:], ident[0:109, 0:109]).then_inc(vtr_done, 1)
            pe.wait_ge(hx_dve, 1)
            pe.wait_ge(hx_act, 4)
            pe.wait_ge(hx_dve, 4)
            norm_bcast(0)
            ffn(0, F1)
            norm_stats(1)
            norm_bcast(1)

            def qkv_post(s):
                for jj in (2 * s, 2 * s + 1):
                    if jj < 8:
                        pe.wait_ge(zsq_done, jj + 1)
                        if jj == 6:
                            pe.wait_ge(nk_done, 1)
                        for c in range(TT):
                            last = mm(ps[:, 4, jj * 4 + c:jj * 4 + c + 1], mb[:, jj % 2, c * P:(c + 1) * P], ones[:, 0:1], start=True, stop=True)
                        last.then_inc(qk_stat, 1)
                    if jj < 4 or jj >= 8:
                        src = kT[:, jj] if jj < 4 else mb[:, jj % 2]
                        pe.wait_ge(zact_done, jj + 1)
                        if jj in (2, 3):
                            pe.wait_ge(ktok_done, jj - 1)
                        elif jj in (8, 9):
                            pe.wait_ge(kkd_done, 16)
                        elif jj in (10, 11):
                            pe.wait_ge(nkv_done, jj - 9)
                        for c in range(TT):
                            last = nc.tensor.transpose(ps[:, 5 + jj % 2, c * P:(c + 1) * P], src[:, c * P:(c + 1) * P], ident[:])
                        last.then_inc(tok_tr, 1)

            for s in range(6):
                n = WIN + s
                pe.wait_ge(lo_done, n + 1)
                if s >= 2:
                    pe.wait_ge(conv_done, 2 * s - 2)
                col_slot(n, (2 * s) % 4, (2 * s) % 4 + 1, xw=8 if s == 0 else None)
                if s == 0:
                    pe.wait_ge(ws_in, 16)
                    for h in range(HD):
                        last = nc.tensor.transpose(ps[:, 7, h * P:(h + 1) * P], wsraw[:, h], ident[:])
                    last.then_inc(ws_tr, 1)
                if s == 1:
                    pe.wait_ge(wab_lo, 1)
                    pe.wait_ge(ws_done, 1)
                    for k in range(KT):
                        last = three(ps[:, 7, :], wabhi[:, k * 16:k * 16 + P], wablo[:, k * 16:k * 16 + P], xhi[:, k, :], xlo[:, k, :], k == 0, k == KT - 1)
                    last.then_inc(ab_mm, 1)
                if s >= 1:
                    qkv_post(s - 1)
                if s == 2:
                    pe.wait_ge(ab_copy, 1)
                    for c in range(TT):
                        last = nc.tensor.transpose(ps[:, 7, c * 16:(c + 1) * 16], abT[:, c * P:(c + 1) * P], ident[0:16, 0:16])
                    last.then_inc(ab_tr, 1)
                    pe.wait_ge(ktok_done, 4)
                if s in (2, 3):
                    for c in (2 * s - 4, 2 * s - 3):
                        if c >= 2:
                            pe.wait_ge(kkd_done, 4 * (c - 1))
                        for h in range(HD):
                            last = mm(ps[:, 5 + c % 2, h * P:(h + 1) * P], kT[:, h, c * P:(c + 1) * P], kT[:, h, c * P:(c + 1) * P], start=True, stop=True)
                        last.then_inc(kkd_mm, 1)
                if s == 3:
                    pe.wait_ge(gate_dve, 5)
                    mm(ps[:, 7, 64:80], tri[:, 0, :], gg[:, 0:16], start=True, stop=True)
                    mm(ps[:, 7, 80:96], tri[:, 1, :], gg[:, 16:32], start=True, stop=True)
                    mm(ps[:, 7, 96:128], ones[:], gg, start=True, stop=True).then_inc(cum_done, 1)
                if s == 4:
                    pe.wait_ge(col_dve, 5)
                    nc.tensor.transpose(ps[0:32, 7, 128:256], Gc, ident[:])
                    nc.tensor.transpose(ps[0:32, 7, 256:384], nsk, ident[:]).then_inc(gs_tr, 1)
            for s in range(2):
                n = WIN + 6 + s
                pe.wait_ge(lo_done, n + 1)
                if s == 0:
                    pe.wait_ge(conv_done, 12)
                for t in range(TT):
                    tok = slice(t * P, (t + 1) * P)
                    for kl in range(4):
                        k = 4 * s + kl
                        wh, wl = wrow(whi, n, 512)[:, kl], wrow(wlo, n, 512)[:, kl]
                        mm(ps[:, t, :], xhi[:, k, tok], wh, start=(k == 0), stop=False)
                        mm(ps[:, t, :], xlo[:, k, tok], wh, start=False, stop=False)
                        last = mm(ps[:, t, :], xhi[:, k, tok], wl, start=False, stop=(k == KT - 1))
                last.then_inc(w_done, 1)
                if s == 0:
                    qkv_post(5)
            for s in range(2):
                n = WIN + 8 + s
                pe.wait_ge(lo_done, n + 1)
                if s == 0:
                    pe.wait_ge(nkv_done, 4)
                    pe.wait_ge(rk_step, 3)
                else:
                    pe.wait_ge(vgelu, 4)
                col_slot(n, 4 if s == 0 else 0, 5 if s == 0 else 1)
            for s in range(2):
                n = WIN + 10 + s
                pe.wait_ge(lo_done, n + 1)
                if s == 1:
                    pe.wait_ge(ugelu, 1)
                col_slot(n, 2 + 2 * s, 3 + 2 * s)
            pe.wait_ge(ln_done, 1)
            pe.wait_ge(ugelu, 2)
            pe.wait_ge(gs_done, 1)
            for h in range(HD):
                for c in range(TT):
                    last = mm(ps[:, (0, 1, 6, 7)[h], c * P:(c + 1) * P], vg[:, c, h * P:(h + 1) * P], wsT[:, h], start=True, stop=True)
                last.then_inc(sv_done, 1)

            def heads(bank, lhs, rhs_, done, start=True, stop=True):
                for h in range(HD):
                    last = mm(ps[:, bank, h * P:(h + 1) * P], lhs(h), rhs_(h), start=start, stop=stop)
                last.then_inc(done, 1)

            def toks(pr, x):
                c = (pr, TT - 1 - pr)[x]
                return c, slice(c * P, (c + 1) * P)

            def X(pr, x):
                return (Rm, Om)[x][:, pr % 2, x]

            def Y(pr, x):
                return (Om, Rm)[x][:, pr % 2, x]

            def grow(pr, x):
                c, tok = toks(pr, x)
                if pr:
                    pe.wait_ge(t_copy, 4 * (pr - 1) + 3 + x)
                heads(x, lambda h: Gc[:, x * 16 + c * 4 + h:x * 16 + c * 4 + h + 1].broadcast_to([P, P]), lambda h: ident[:], grow_done)

            def kk(pr, x):
                c, tok = toks(pr, x)
                if pr:
                    pe.wait_ge(y_upd, 4 * (pr - 1) + 3 + x)
                heads(2 + x, lambda h: kT[:, h, tok], lambda h: kT[:, h, tok], kk_done)

            def kq(pr, x):
                c, tok = toks(pr, x)
                pe.wait_ge(nt_done, 2 * pr + x + 1)
                heads(2 + x, lambda h: kT[:, h, tok], lambda h: qT[:, h, tok], kq_done)

            def transpose_blocks(pr, x):
                pe.wait_ge(r_init, 2 * pr + x + 1)
                pe.wait_ge(em_done, 2 * pr + x + 1)
                for h in range(HD):
                    last = nc.tensor.transpose(ps[:, x, h * P:(h + 1) * P], Rm[:, pr % 2, x, h], ident[:])
                last.then_inc(o_tr, 1)

            def t_step(pr, li, x):
                if li == 0:
                    pe.wait_ge(o_init, 2 * pr + x + 1)
                else:
                    pe.wait_ge(x_upd, 2 * pr + x + 1)
                heads(x, lambda h: NTm[:, x, h], lambda h: X(pr, x)[:, h], t_mm)

            def w_step(pr, x):
                pe.wait_ge(t_copy, 4 * pr + x + 1)
                pe.wait_ge(pm_done, 2 * pr + x + 1)
                heads(2 + x, lambda h: Y(pr, x)[:, h], lambda h: Tm[:, x, h], w_mm)

            def wt_step(pr, li, x):
                if li == 0:
                    pe.wait_ge(x_upd, 2 * pr + x + 1)
                else:
                    pe.wait_ge(t_copy, 4 * pr + 3 + x)
                    pe.wait_ge(y_upd, 4 * pr + x + 1)
                heads(2 + x, lambda h: Tm[:, x, h], lambda h: Y(pr, x)[:, h], wt_mm)

            def ks_step(pr, x):
                c, tok = toks(pr, x)
                pe.wait_ge(s_upd, 2 * pr - 1 + x) if pr else pe.wait_ge(s_zero, 1)
                heads(6 + x, lambda h: kT[:, h, tok], lambda h: St[:, x, h], ks_mm)

            def v_step(pr, x):
                pe.wait_ge(y_upd, 4 * pr + 3 + x)
                pe.wait_ge(r_done, 2 * pr + x + 1)
                heads(6 + x, lambda h: Y(pr, x)[:, h], lambda h: rhs[:, x, h], v_mm)

            def s_step(pr, x):
                c, tok = toks(pr, x)
                pe.wait_ge(vs_done, 2 * pr + x + 1)
                heads(6 + x, lambda h: ktok[:, c, h], lambda h: vs[:, x, h], s_mm)

            def o_step(pr, x):
                it = 2 * pr + x
                pe.wait_ge(qd_done, it + 1)
                pe.wait_ge(vn_done, it + 1)
                if pr:
                    pe.wait_ge(o_acc, it - 1)
                for h in range(HD):
                    mm(ps[:, 4 + x, h * P:(h + 1) * P], St[:, x, h], qd[:, pr % 2, x, h], start=True, stop=False)
                    last = mm(ps[:, 4 + x, h * P:(h + 1) * P], vn[:, x, h], Pm[:, pr % 2, x, h], start=False, stop=True)
                last.then_inc(o_mm, 1)

            both = (0, 1)
            for pr in range(TT + 1):
                sc, iv = pr - 1, pr < TT
                if pr == 0:
                    pe.wait_ge(gm_done, 4)
                    pe.wait_ge(zg_done, 2)
                    pe.wait_ge(col_dve, 6)
                if iv:
                    for x in both:
                        grow(pr, x)
                    for x in both:
                        kk(pr, x)
                if sc >= 0:
                    for x in both:
                        ks_step(sc, x)
                if iv:
                    for x in both:
                        transpose_blocks(pr, x)
                if sc >= 0:
                    for x in both:
                        v_step(sc, x)
                if iv:
                    for x in both:
                        kq(pr, x)
                    for x in both:
                        t_step(pr, 0, x)
                if sc >= 0:
                    for x in both:
                        o_step(sc, x)
                        if sc < TT - 1:
                            s_step(sc, x)
                if iv:
                    for x in both:
                        w_step(pr, x)
                    for x in both:
                        wt_step(pr, 0, x)
                    for x in both:
                        t_step(pr, 1, x)
                    for x in both:
                        wt_step(pr, 1, x)
            for h in range(HD):
                pe.wait_ge(osq, h + 1)
                for c in range(TT):
                    last = mm(ps[:, 6, h * 4 + c:h * 4 + c + 1], tmp[:, h, c * P:(c + 1) * P], ones[:, 0:1], start=True, stop=True)
            last.then_inc(ost, 1)
            pe.wait_ge(oscale, 1)
            for h in range(HD):
                for c in range(TT):
                    last = mm(ps[:, h, c * P:(c + 1) * P], misc[:, h * 4 + c:h * 4 + c + 1].broadcast_to([P, P]), ident[:], start=True, stop=True)
                last.then_inc(orow, 1)
            for s in range(4):
                n = WOUT + s
                pe.wait_ge(lo_done, n + 1)
                if s == 2:
                    pe.wait_ge(y_step, 8)
                for k in range(KT):
                    if s == 0:
                        pe.wait_ge(y_ready, k + 1)
                    for f in range(2):
                        o = 2 * s + f
                        last = three(ps[:, BANK[o], :], wcol(whi, n)[:, k, f * P:(f + 1) * P], wcol(wlo, n)[:, k, f * P:(f + 1) * P],
                                     xhi[:, k, :], xlo[:, k, :], k == 0, k == KT - 1)
                last.then_inc(w_done, 1)
            norm_stats(2)
            norm_bcast(2)
            ffn(1, F2)

            norm_stats(3)
            pe.wait_ge(p_in, 16)
            for kk in range(2):
                for t in range(TT):
                    last = nc.tensor.transpose(ps[:, 6 + kk, t * P:(t + 1) * P], ptok[:, t, kk * P:(kk + 1) * P], ident[:])
            last.then_inc(p_tr, 1)
            norm_bcast(3)
            pe.wait_ge(pt_lo, 1)
            pe.wait_ge(lo_done, PROJ + 1)
            for o in range(KT):
                b = (0, 1, 2, 3)[o % 4]
                if o >= 4:
                    pe.wait_ge(e_sq, o - 3)
                for kk in range(2):
                    last = three(ps[:, b, :], wrow(whi, PROJ, D)[:, kk, o * P:(o + 1) * P], wrow(wlo, PROJ, D)[:, kk, o * P:(o + 1) * P],
                                 pThi[:, kk, :], pTlo[:, kk, :], kk == 0, kk == 1)
                last.then_inc(e_mm if o < KT - 1 else w_done, 1)
            pe.wait_ge(e_sq, 8)
            def gate_slot(s):
                n = GATE + s
                pe.wait_ge(lo_done, n + 1)
                if s >= 2:
                    pe.wait_ge(sg_done, 2 * s - 2)
                col_slot(n, (2 * s) % 4, (2 * s) % 4 + 1, xw=24 if s == 0 else None)
            gate_slot(0)
            pe.wait_ge(e_acc, 7)
            for t in range(TT):
                last = mm(ps[:, BANK[0], 4 + t:5 + t], sqsum[:, t * P:(t + 1) * P], ones[:, 0:1], start=True, stop=True)
            last.then_inc(e_stats, 1)
            gate_slot(1)
            pe.wait_ge(e_rstd, 1)
            row_bcast(6, rstd[:, 4:8], TT, e_rb)
            gate_slot(2)
            gate_slot(3)
            pe.wait_ge(hf_done, 8)
            for t in range(TT):
                if t >= 2:
                    pe.wait_ge(f_out, t - 1)
                for k in range(KT):
                    last = nc.tensor.transpose(ps[:, 4 + 2 * (t % 2) + k // 4, (k % 4) * P:(k % 4 + 1) * P], hT[:, k, t * P:(t + 1) * P], ident[:])
                last.then_inc(f_tr, 1)

        @block.scalar
        def _(act):
            A = nc.scalar.activation

            def hi(n, p, cnt=None):
                act.wait_ge(raw_in[p], cnt if cnt is not None else 16 * (n // 2 + 1))
                if not isinstance(n, int) or n >= 2:
                    act.wait_ge(w_done, n - 1)
                A(whi[p][:], raw[p][:], ACT.Copy).then_inc(hi_done, 1)

            def hir(n0, i2):
                hi(i2 * 2 + n0, n0 % 2, cnt=i2 * 16 + 16 * (n0 // 2 + 1))

            def norm_std(ni):
                if ni:
                    act.wait_ge(stats_done, ni)
                    A(std[:, 0:4], ps[:, BANK[0], 0:4], ACT.Sqrt, bias=eps[:], scale=1.0 / D).then_inc(std_done, 1)
                else:
                    act.wait_ge(ss0_done, TT)
                    A(std[:, 0:4], ss[:, 0:4], ACT.Sqrt, bias=eps[:], scale=1.0 / D).then_inc(std_done, 1)

            def norm_hi(ni):
                for k in range(KT):
                    act.wait_ge(xf_done, 8 * ni + k + 1)
                    A(xhi[:, k, :], tmp[:, k % 2, :], ACT.Copy).then_inc(xhi_done, 1)

            def squares(og):
                for o in range(KT):
                    act.wait_ge(h_done, 8 * og + o + 1)
                    if o >= 4:
                        act.wait_ge(acc_done, 7 * og + max(1, o - 4))
                    A(tmp[:, o % 4, :], hT[:, o, :], ACT.Square).then_inc(sq_done, 1)

            def ffn(u, n0):
                with act.Fori(0, FP) as i:
                    act.wait_ge(w_done, i * 2 + (n0 + 1))
                    act.wait_ge(gu_done, i + (u * FP + 1))
                    A(tmp[:, 0:2, :], ps[:, 0:2, :], ACT.Silu).then_inc(silu_done, 1)
                    hir(n0 + 2, i)
                    act.wait_ge(gu_done, i + (u * FP + 2))
                    A(guhi[:, bass.ds(i * 2, 2), :], tmp[:, 2:4, :], ACT.Copy).then_inc(guhi_done, 1)
                    hir(n0 + 3, i)
                n1 = n0 + 2 * FP
                for jj in range(2, FP):
                    hi(n1 + jj, (n1 + jj) % 2)

            act.sem_inc(silu_done, 1)
            rows = [("ffn1_norm", 0), ("mix_norm", 8), ("ffn2_norm", 16), ("ple_gate_norm", 24), ("ple_norm", 32), ("ple_gate_b", 40)]
            for name, r in rows:
                act.dma_start(vrows[r:r + 8, :], io[name][0].rearrange("(k p) -> k p", p=P)).then_inc(vec_in, 16)
            act.dma_start(vrows[48:108, :], io["dn_conv_w"][0].rearrange("j (t p) -> (j t) p", p=P)).then_inc(vec_in, 16)
            act.dma_start(vrows[108:109, :], io["dn_out_norm"]).then_inc(vec_in, 16)
            for t in range(TT):
                act.wait_ge(x_in[t], 16)
                if t:
                    act.wait_ge(ss0_done, t)
                else:
                    act.wait_ge(const_done, 1)
                A(sqjunk[:], xtok[:, t, :], ACT.Square, accum_out=ss[:, t:t + 1]).then_inc(ss0_done, 1)
            norm_std(0)
            act.wait_ge(xtr_done, 1)
            for k in range(0, KT, 2):
                A(hT[:, k, :], ps[:, k, :], ACT.Copy).then_inc(hx_act, 1)
            act.wait_ge(vtr_done, 1)
            A(cols[:], ps[:, 0, 0:109], ACT.Copy).then_inc(cols_done, 1)
            hi(F1, F1 % 2)
            hi(F1 + 1, (F1 + 1) % 2)
            norm_hi(0)
            ffn(0, F1)
            hi(WIN, WIN % 2)
            squares(0)
            norm_std(1)
            norm_hi(1)

            hi(WIN + 1, (WIN + 1) % 2)
            act.wait_ge(ab_in, 16)
            act.wait_ge(ab_pad, 1)
            A(wabhi[:], wab[:], ACT.Copy).then_inc(wab_hi, 1)
            act.wait_ge(ws_tr, 1)
            A(wsT[:], ps[:, 7, :].rearrange("p (h n) -> p h n", h=HD), ACT.Copy).then_inc(ws_done, 1)

            def ktok_evac(jj):
                act.wait_ge(tok_tr, jj + 1)
                A(ktok[:, :, jj, :], ps[:, 5 + jj % 2, :].rearrange("p (c d) -> p c d", c=TT), ACT.Copy).then_inc(ktok_done, 1)

            def kkd_evac(c):
                act.wait_ge(kkd_mm, c + 1)
                for b in range(NB):
                    A(kkd[b * B:(b + 1) * B, c], ps[b * B:(b + 1) * B, 5 + c % 2, :].rearrange("p (h n) -> p h n", h=HD)[:, :, b * B:(b + 1) * B],
                      ACT.Copy).then_inc(kkd_done, 1)

            for s in range(6):
                for jj in (2 * s, 2 * s + 1):
                    act.wait_ge(w_done, WIN + s + 1)
                    if jj >= 2:
                        act.wait_ge(zact_done, jj - 1)
                    A(acc[:, jj % 2, :], ps[:, jj % 4, :], ACT.Copy, scale=cols[:, G_CONV + 24 + ch(jj):G_CONV + 25 + ch(jj)]).then_inc(tap0, 1)
                hi(WIN + s + 2, (WIN + s) % 2)
                if s == 3:
                    kkd_evac(0)
                    kkd_evac(1)
                if s == 2:
                    act.wait_ge(ab_mm, 1)
                    A(abT[:], ps[0:16, 7, :], ACT.Copy).then_inc(ab_copy, 1)
                for jj in (2 * s, 2 * s + 1):
                    act.wait_ge(conv_done, jj + 1)
                    if jj < 8:
                        z = (kT if jj < 4 else qT)[:, jj % 4, :]
                        A(z, acc[:, jj % 2, :], ACT.Silu).then_inc(zact_done, 1)
                        if jj >= 2:
                            act.wait_ge(qk_stat, jj - 1)
                        act.wait_ge(zact_done, jj + 1)
                        A(mb[:, jj % 2, :], z, ACT.Square).then_inc(zsq_done, 1)
                    else:
                        act.wait_ge(qk_stat, min(jj - 1, 8))
                        if jj >= 10:
                            act.wait_ge(tok_tr, jj - 5)
                        A(mb[:, jj % 2, :], acc[:, jj % 2, :], ACT.Silu).then_inc(zact_done, 1)
                if s in (1, 2):
                    for jj in (2 * s - 2, 2 * s - 1):
                        ktok_evac(jj)
                if s == 3:
                    kkd_evac(2)
                    kkd_evac(3)
                    abv = ps[:, 7, 0:64].rearrange("p (c j) -> p c j", j=16)
                    act.wait_ge(gate_dve, 1)
                    A(ea, aa, ACT.Abs).then_inc(gate_act, 1)
                    act.wait_ge(gate_act, 1)
                    A(ea, ea, ACT.Exp, scale=-1.0).then_inc(gate_act, 1)
                    A(be.rearrange("p (c j) -> p c j", j=8), abv[:, :, 8:16], ACT.Exp, scale=-1.0).then_inc(gate_act, 1)
                    A(bc8[:, 16:24], bc8[:, 8:16], ACT.Exp).then_inc(gate_act, 1)
                    act.wait_ge(gate_act, 2)
                    A(ea, ea, ACT.Ln, bias=1.0).then_inc(gate_act, 1)
                    act.wait_ge(qk_stat, 6)
                    A(nk, ps[:, 4, 0:16], ACT.Sqrt, bias=eps[:]).then_inc(nk_done, 1)
                if s == 4:
                    act.wait_ge(cum_done, 1)
                    A(eG, ps[:, 7, 64:96], ACT.Exp)
                    A(egl, ps[:, 7, 96:128], ACT.Exp).then_inc(col_act, 1)
                    act.wait_ge(col_dve, 2)
                    A(egd, egd, ACT.Exp).then_inc(col_act, 1)
                if s == 5:
                    act.wait_ge(gs_tr, 1)
                    A(gsT[:], ps[0:32, 7, 128:384].rearrange("p (a n) -> p a n", a=2), ACT.Copy).then_inc(gs_done, 1)
                    act.wait_ge(gs_done, 1)
                    for d in range(2):
                        for b in range(NB):
                            act.dma_start(gsi[own(d, b)], gsT[16 * d:16 * d + 16, :, b * B:(b + 1) * B]).then_inc(gin_in, 16)
            act.wait_ge(zi_dve, 3)
            A(Ei[:], Ei[:], ACT.Exp).then_inc(zi_exp, 1)
            hi(WIN + 8, (WIN + 8) % 2)
            for t in range(TT):
                act.wait_ge(w_done, WIN + 8)
                A(vg[:, t, :], ps[:, t, :], ACT.Gelu_apprx_tanh).then_inc(vgelu, 1)
            hi(WIN + 9, (WIN + 9) % 2)
            hi(WIN + 10, (WIN + 10) % 2)
            act.wait_ge(w_done, WIN + 9)
            A(uT[:, 0:2, :], ps[:, 4:6, :], ACT.Gelu_apprx_tanh).then_inc(ugelu, 1)
            hi(WIN + 11, (WIN + 11) % 2)
            act.wait_ge(w_done, WIN + 10)
            A(uT[:, 2:4, :], ps[:, 0:2, :], ACT.Gelu_apprx_tanh).then_inc(ugelu, 1)
            act.wait_ge(ln_step, 17)
            A(lsd[:], mv[:, :, 1], ACT.Sqrt, bias=eps[:]).then_inc(ln_sd, 1)
            hi(WOUT, WOUT % 2)
            act.wait_ge(w_done, WIN + 11)
            act.wait_ge(xi_done, 1)
            A(zg[:, 0:2, :], ps[:, 2:4, :], ACT.Silu).then_inc(zg_done, 1)
            hi(WOUT + 1, (WOUT + 1) % 2)
            act.wait_ge(w_done, WIN + 12)
            A(zg[:, 2:4, :], ps[:, 4:6, :], ACT.Silu).then_inc(zg_done, 1)

            def ps4(b):
                return ps[:, b, :].rearrange("p (h n) -> p h n", h=HD)

            def decays(pr):
                for x in range(2):
                    it = 2 * pr + x
                    act.wait_ge(dpre_done, it + 1)
                    if pr:
                        act.wait_ge(qd_done, it - 1)
                    A(Em[:, x], ps4(x), ACT.Exp).then_inc(em_done, 1)
                    A(Dm[:, x], Dm[:, x], ACT.Exp).then_inc(dm_done, 1)

            def others(pr):
                for x in range(2):
                    act.wait_ge(o_tr, 2 * pr + x + 1)
                    A(Om[:, pr % 2, x], ps4(x), ACT.Copy).then_inc(o_init, 1)

            def t_evac(pr, li):
                for x in range(2):
                    tn = 4 * pr + 2 * li + x
                    act.wait_ge(t_mm, tn + 1)
                    if tn >= 2:
                        act.wait_ge(wt_mm, tn - 1)
                    A(Tm[:, x], ps4(x), ACT.Copy).then_inc(t_copy, 1)

            def v_evac(pr):
                for x in range(2):
                    c, it = (pr, TT - 1 - pr)[x], 2 * pr + x
                    act.wait_ge(v_mm, it + 1)
                    if pr:
                        act.wait_ge(o_mm, it - 1)
                    for h in range(HD):
                        col = x * 16 + c * 4 + h
                        last = A(vn[:, x, h], ps[:, 6 + x, h * P:(h + 1) * P], ACT.Copy, scale=sk[:, col:col + 1])
                    last.then_inc(vn_done, 1)

            for pr in range(TT + 1):
                if pr < TT:
                    decays(pr)
                    others(pr)
                if pr:
                    v_evac(pr - 1)
                if pr < TT:
                    t_evac(pr, 0)
                    t_evac(pr, 1)
            act.wait_ge(o_mm, 8)
            act.wait_ge(r_init, 8)
            for h in range(HD):
                A(xhi[:, h, :], uT[:, h, :], ACT.Copy).then_inc(yhi_done, 1)
            for h in range(HD):
                act.wait_ge(o_acc, 8)
                A(tmp[:, h, :], oT[:, h, :], ACT.Square).then_inc(osq, 1)
            act.wait_ge(ost, 1)
            act.wait_ge(osd, 1)
            A(misc[:, 0:16], misc[:, 0:16], ACT.Sqrt).then_inc(osd, 1)
            for h in range(HD):
                act.wait_ge(y_step, 2 * h + 2)
                A(xhi[:, 4 + h, :], oT[:, h, :], ACT.Copy).then_inc(yhi_done, 1)
            hi(WOUT + 2, WOUT % 2)
            hi(WOUT + 3, (WOUT + 1) % 2)
            hi(F2, F2 % 2)
            squares(1)
            norm_std(2)
            hi(F2 + 1, (F2 + 1) % 2)
            norm_hi(2)
            ffn(1, F2)
            hi(PROJ, PROJ % 2)
            squares(2)
            norm_std(3)
            act.wait_ge(p_copy, 1)
            A(pThi[:], pTf[:], ACT.Copy).then_inc(pt_hi, 1)
            norm_hi(3)
            for o in range(KT):
                act.wait_ge(e_mm, o + 1) if o < KT - 1 else act.wait_ge(w_done, PROJ + 1)
                A(eT[:, o, :], ps[:, o % 4, :], ACT.Copy).then_inc(e_copy, 1)
                if o >= 2:
                    act.wait_ge(e_acc, max(1, o - 2))
                A(tmp[:, 2 + o % 2, :], ps[:, o % 4, :], ACT.Square).then_inc(e_sq, 1)
            hi(GATE, GATE % 2)
            hi(GATE + 1, (GATE + 1) % 2)
            act.wait_ge(e_stats, 1)
            A(std[:, 4:8], ps[:, BANK[0], 4:8], ACT.Sqrt, bias=eps[:], scale=1.0 / D).then_inc(e_std, 1)
            for o in range(KT):
                if o in (0, 2):
                    hi(GATE + 2 + o // 2, (GATE + o // 2) % 2)
                act.wait_ge(w_done, GATE + o // 2 + 1)
                if o >= 2:
                    act.wait_ge(ge_done, o - 1)
                A(sgm[:, o % 2, :], ps[:, o % 4, :], ACT.Sigmoid, bias=cols[:, B_GATE + o:B_GATE + o + 1]).then_inc(sg_done, 1)
            for t in range(TT):
                act.wait_ge(f_tr, t + 1)
                if t:
                    act.wait_ge(f_ss, t)
                A(fjunk[:].rearrange("p (b n) -> p b n", b=2), ps[:, 4 + 2 * (t % 2):6 + 2 * (t % 2), :], ACT.Square,
                  accum_out=ss[:, t:t + 1]).then_inc(f_ss, 1)
                act.wait_ge(f_ss, t + 1)
                A(std[:, t:t + 1], ss[:, t:t + 1], ACT.Sqrt, bias=eps[:], scale=1.0 / D).then_inc(f_std, 1)

        @block.vector
        def _(dve):
            V = nc.vector
            stt = nc.vector.scalar_tensor_tensor

            def lo(n, p):
                dve.wait_ge(hi_done, n + 1)
                V.tensor_tensor(out=wlo[p][:], in0=raw[p][:], in1=whi[p][:].bitcast(f32), op=ALU.subtract).then_inc(lo_done, 1)

            def residual(og, n_last, factor):
                for o in range(KT + 1):
                    if o < KT:
                        if og == 1:
                            dve.wait_ge(w_done, WOUT + o // 2 + 1)
                        elif o < KT - 1:
                            dve.wait_ge(out_done, 7 * (og // 2) + o + 1)
                        else:
                            dve.wait_ge(w_done, n_last + 1)
                        stt(out=hT[:, o, :], in0=ps[:, BANK[o], :], scalar=factor, in1=hT[:, o, :], op0=ALU.mult, op1=ALU.add).then_inc(h_done, 1)
                    if o >= 2:
                        dve.wait_ge(sq_done, 8 * og + o)
                        if o == 2:
                            V.tensor_tensor(out=sqsum[:], in0=tmp[:, 0, :], in1=tmp[:, 1, :], op=ALU.add).then_inc(acc_done, 1)
                        else:
                            dve.wait_ge(acc_done, 7 * og + o - 2)
                            V.tensor_tensor(out=sqsum[:], in0=sqsum[:], in1=tmp[:, (o - 1) % 4, :], op=ALU.add).then_inc(acc_done, 1)
                    if og == 1 and o in (1, 3):
                        lo(WOUT + 3 + o // 2, (WOUT + 3 + o // 2) % 2)

            def norm_apply(ni, g0):
                dve.wait_ge(std_done, ni + 1)
                V.reciprocal(rstd[:, 0:4], std[:, 0:4]).then_inc(rstd_done, 1)
                dve.wait_ge(rb_done, ni + 1)
                for k in range(KT + 1):
                    if k < KT:
                        if k >= 2:
                            dve.wait_ge(x_ready, 8 * ni + k - 1)
                        stt(out=tmp[:, k % 2, :], in0=hT[:, k, :], scalar=cols[:, g0 + k:g0 + k + 1], in1=ps[:, BANK[1], :],
                            op0=ALU.mult, op1=ALU.mult).then_inc(xf_done, 1)
                    if k:
                        dve.wait_ge(xhi_done, 8 * ni + k)
                        V.tensor_tensor(out=xlo[:, k - 1, :], in0=tmp[:, (k - 1) % 2, :], in1=xhi[:, k - 1, :].bitcast(f32),
                                        op=ALU.subtract).then_inc(x_ready, 1)

            def ffn(u, n0):
                with dve.Fori(0, FP) as i:
                    lo(i * 2 + (n0 + 2), n0 % 2)
                    dve.wait_ge(silu_done, i + (u * FP + 1))
                    dve.wait_ge(w_done, i * 2 + (n0 + 2))
                    dve.wait_ge(gulo_done, i + (u * FP + 1))
                    V.tensor_tensor(out=tmp[:, 2:4, :], in0=ps[:, 2:4, :], in1=tmp[:, 0:2, :], op=ALU.mult).then_inc(gu_done, 1)
                    dve.wait_ge(guhi_done, i + (u * FP + 1))
                    V.tensor_tensor(out=gulo[:, bass.ds(i * 2, 2), :], in0=tmp[:, 2:4, :],
                                    in1=guhi[:, bass.ds(i * 2, 2), :].bitcast(f32), op=ALU.subtract).then_inc(gulo_done, 1)
                    lo(i * 2 + (n0 + 3), (n0 + 1) % 2)
                n1 = n0 + 2 * FP
                for jj in range(2, FP):
                    lo(n1 + jj, (n1 + jj) % 2)

            dve.sem_inc(gu_done, 1)
            dve.sem_inc(gulo_done, 1)
            dve.wait_ge(xtr_done, 1)
            for k in range(1, KT, 2):
                V.tensor_copy(hT[:, k, :], ps[:, k, :]).then_inc(hx_dve, 1)
            lo(F1, F1 % 2)
            lo(F1 + 1, (F1 + 1) % 2)
            dve.wait_ge(cols_done, 1)
            dve.wait_ge(hx_dve, 4)
            dve.wait_ge(hx_act, 4)
            norm_apply(0, G_FFN1)
            ffn(0, F1)
            lo(WIN, WIN % 2)
            residual(0, WIN - 1, 0.5)
            norm_apply(1, G_MIX)

            lo(WIN + 1, (WIN + 1) % 2)
            dve.wait_ge(wab_hi, 1)
            V.tensor_tensor(out=wablo[:], in0=wab[:], in1=wabhi[:].bitcast(f32), op=ALU.subtract).then_inc(wab_lo, 1)
            taps = [0]

            def conv(jj):
                z, a = ps[:, jj % 4, :], acc[:, jj % 2, :]
                dve.wait_ge(tap0, jj + 1)
                for j in (0, 1, 3, 4):
                    if j:
                        taps[0] += 1
                        dve.wait_ge(conv_tap, taps[0])
                    d = j - 2
                    w = cols[:, G_CONV + j * 12 + ch(jj):G_CONV + j * 12 + ch(jj) + 1]
                    dst = a[:, max(0, -d):T - max(0, d)]
                    last = stt(out=dst, in0=z[:, max(0, d):T - max(0, -d)], scalar=w, in1=dst, op0=ALU.mult, op1=ALU.add)
                    last.then_inc(conv_done if j == 4 else conv_tap, 1)

            def nkv_evac(jj):
                dve.wait_ge(tok_tr, jj - 3)
                V.tensor_tensor(out=nkv[:, :, jj - 8, :], in0=ps[:, 5 + jj % 2, :].rearrange("p (c d) -> p c d", c=TT),
                                in1=nk[:, (jj - 8) * 4:(jj - 7) * 4].unsqueeze(2).broadcast_to([P, TT, P]), op=ALU.mult).then_inc(nkv_done, 1)

            for s in range(6):
                conv(2 * s)
                lo(WIN + s + 2, (WIN + s) % 2)
                conv(2 * s + 1)
                if s == 3:
                    abv = ps[:, 7, 0:64].rearrange("p (c j) -> p c j", j=16)
                    dve.wait_ge(gate_act, 5)
                    stt(out=aa, in0=aa, scalar=0.0, in1=ea, op0=ALU.max, op1=ALU.add).then_inc(gate_dve, 1)
                    V.tensor_scalar(s2, be, 1.0, None, ALU.add).then_inc(gate_dve, 1)
                    dve.wait_ge(gate_dve, 3)
                    V.reciprocal(be, s2).then_inc(gate_dve, 1)
                    for d in range(2):
                        last = stt(out=gg[:, 16 * d:16 * d + 16].rearrange("p (c h) -> p c h", c=TT),
                                   in0=aa.rearrange("p (c j) -> p c j", c=TT)[:, :, 4 * d:4 * d + 4], scalar=-1.0,
                                   in1=bc8[:, 16 + 4 * d:20 + 4 * d].unsqueeze(1).broadcast_to([P, TT, HD]), op0=ALU.mult, op1=ALU.mult)
                    last.then_inc(gate_dve, 1)
                    dve.wait_ge(nk_done, 1)
                    V.reciprocal(rk2, nk).then_inc(rk_step, 1)
                    dve.wait_ge(rk_step, 1)
                    V.tensor_tensor(out=rk2, in0=rk2, in1=rk2, op=ALU.mult).then_inc(rk_step, 1)
                if s == 2:
                    abv = ps[:, 7, 0:64].rearrange("p (c j) -> p c j", j=16)
                    dve.wait_ge(ab_tr, 1)
                    dve.wait_ge(bc_in, 80)
                    V.tensor_tensor(out=aa.rearrange("p (c j) -> p c j", j=8), in0=abv[:, :, 0:8],
                                    in1=bc8[:, 0:8].unsqueeze(1).broadcast_to([P, TT, 8]), op=ALU.add).then_inc(gate_dve, 1)
                if s == 4:
                    dve.wait_ge(cum_done, 1)
                    dve.wait_ge(col_act, 1)
                    V.tensor_copy(Gc, ps[:, 7, 64:96]).then_inc(col_dve, 1)
                    dve.wait_ge(col_dve, 1)
                    V.tensor_tensor(out=egd, in0=ps[:, 7, 96:128], in1=Gc, op=ALU.subtract).then_inc(col_dve, 1)
                    V.tensor_scalar(neG, eG, -1.0, None, ALU.mult).then_inc(col_dve, 1)
                    dve.wait_ge(rk_step, 2)
                    for d in range(2):
                        last = V.tensor_tensor(out=sk[:, 16 * d:16 * d + 16].rearrange("p (c h) -> p c h", c=TT),
                                               in0=be.rearrange("p (c j) -> p c j", c=TT)[:, :, 4 * d:4 * d + 4],
                                               in1=rk2.rearrange("p (h c) -> p c h", c=TT), op=ALU.mult)
                    last.then_inc(col_dve, 1)
                    dve.wait_ge(col_dve, 4)
                    V.tensor_scalar(nsk, sk, -1.0, None, ALU.mult).then_inc(col_dve, 1)
                    dve.wait_ge(col_act, 2)
                    V.tensor_tensor(out=s2, in0=sk, in1=egd, op=ALU.mult).then_inc(col_dve, 1)
                    dve.wait_ge(qk_stat, 8)
                    V.tensor_scalar(misc[:, 16:32], ps[:, 4, 16:32], EPS, float(P), ALU.add, ALU.mult).then_inc(rk_step, 1)
                if s == 5:
                    nkv_evac(8)
                    nkv_evac(9)
            dve.wait_ge(gin_in, 8 * 16)
            V.tensor_scalar(gi, gi, sgn[:], None, ALU.mult).then_inc(zi_dve, 1)
            dve.wait_ge(zi_dve, 1)
            row = lambda a: a.unsqueeze(2).broadcast_to([P, B, B])
            col = lambda a: a.unsqueeze(1).broadcast_to([P, B, B])
            V.tensor_tensor(out=Ei[:], in0=row(gi), in1=col(gi), op=ALU.subtract).then_inc(zi_dve, 1)
            dve.wait_ge(zi_dve, 2)
            V.tensor_scalar(Ei[:], Ei[:], 0.0, None, ALU.min).then_inc(zi_dve, 1)
            dve.wait_ge(kin_in, 8 * 16)
            V.tensor_tensor(out=Zi[0:64], in0=Zi[0:64], in1=col(si)[0:64], op=ALU.mult)
            V.tensor_tensor(out=Zi[64:P], in0=Zi[64:P], in1=row(si)[64:P], op=ALU.mult).then_inc(zi_dve, 1)
            V.memset(Xi[:], 0.0).then_inc(xi_init, 1)
            dve.wait_ge(xi_init, 1)
            V.memset(Xi[:].rearrange("p r c -> p (r c)")[:, 0:B * B:B + 1], 1.0).then_inc(xi_init, 1)
            dve.wait_ge(zi_exp, 1)
            dve.wait_ge(zi_dve, 4)
            V.tensor_tensor(out=Zi[:], in0=Zi[:], in1=Ei[:], op=ALU.mult).then_inc(zi_dve, 1)
            nkv_evac(10)
            nkv_evac(11)
            dve.wait_ge(zi_dve, 5)
            dve.wait_ge(xi_init, 2)

            def substitute(m0, m1):
                for m in range(m0, m1):
                    nr, ncol = B - 1 - m, m + 1
                    if m:
                        dve.wait_ge(xi_step, 2 * m)
                    w = prod[:, 0:nr * ncol].rearrange("p (r c) -> p r c", r=nr)
                    V.tensor_tensor(out=w, in0=Zi[:, m + 1:B, m:m + 1].broadcast_to([P, nr, ncol]),
                                    in1=Xi[:, m:m + 1, 0:ncol].broadcast_to([P, nr, ncol]), op=ALU.mult).then_inc(xi_step, 1)
                    dve.wait_ge(xi_step, 2 * m + 1)
                    V.tensor_tensor(out=Xi[:, m + 1:B, 0:ncol], in0=Xi[:, m + 1:B, 0:ncol], in1=w, op=ALU.add).then_inc(
                        xi_step if m < B - 2 else xi_done, 1)

            substitute(0, 10)
            lo(WIN + 8, (WIN + 8) % 2)
            substitute(10, 20)
            lo(WIN + 9, (WIN + 9) % 2)
            substitute(20, B - 1)
            dve.wait_ge(vgelu, 4)
            for t in range(TT):
                for h in range(HD):
                    V.bn_stats(bns[:, t * 4 + h, :], vg[:, t, h * P:(h + 1) * P]).then_inc(ln_step, 1)
            dve.wait_ge(ln_step, 16)
            for q in range(16):
                last = V.bn_aggr(mv[:, q, :], bns[:, q, :])
            last.then_inc(ln_step, 1)
            lo(WIN + 10, (WIN + 10) % 2)
            dve.wait_ge(ln_sd, 1)
            V.reciprocal(lrs[:], lsd[:]).then_inc(ln_step, 1)
            dve.wait_ge(ln_step, 18)
            for t in range(TT):
                for h in range(HD):
                    q = t * 4 + h
                    V.tensor_scalar(vg[:, t, h * P:(h + 1) * P], vg[:, t, h * P:(h + 1) * P], mv[:, q, 0:1], lrs[:, q:q + 1],
                                    ALU.subtract, ALU.mult).then_inc(ln_step, 1)
            lo(WIN + 11, (WIN + 11) % 2)
            dve.wait_ge(ln_step, 34)
            V.tensor_tensor(out=vg[:], in0=vg[:], in1=lng[:].unsqueeze(1).broadcast_to([P, TT, T]), op=ALU.mult).then_inc(ln_step, 1)
            dve.wait_ge(ln_step, 35)
            V.tensor_tensor(out=vg[:], in0=vg[:], in1=lnb[:].unsqueeze(1).broadcast_to([P, TT, T]), op=ALU.add).then_inc(ln_done, 1)
            V.memset(St[:], 0.0).then_inc(s_zero, 1)
            lo(WOUT, WOUT % 2)
            lo(WOUT + 1, (WOUT + 1) % 2)
            dve.wait_ge(ugelu, 2)
            for h in range(HD):
                dve.wait_ge(sv_done, h + 1)
                if h:
                    dve.wait_ge(gm_done, h)
                V.tensor_tensor(out=mb[:, 0, :].rearrange("p (c i) -> p c i", c=TT), in0=ps[:, (0, 1, 6, 7)[h], :].rearrange("p (c i) -> p c i", c=TT),
                                in1=bsb[:, h * P:(h + 1) * P].unsqueeze(1).broadcast_to([P, TT, P]), op=ALU.add).then_inc(gm_step, 1)
                dve.wait_ge(gm_step, h + 1)
                V.tensor_tensor(out=uT[:, h, :], in0=uT[:, h, :], in1=mb[:, 0, :], op=ALU.mult).then_inc(gm_done, 1)

            ps4 = lambda b: ps[:, b, :].rearrange("p (h n) -> p h n", h=HD)
            both = (0, 1)

            def cell(pr, x):
                c = (pr, TT - 1 - pr)[x]
                return c, 2 * pr + x, x * 16 + c * 4

            def decay_args(pr, x):
                c, it, q = cell(pr, x)
                dve.wait_ge(grow_done, it + 1)
                if pr:
                    dve.wait_ge(pm_done, it - 1)
                for h in range(HD):
                    last = stt(out=Dm[:, x, h], in0=ps[:, x, h * P:(h + 1) * P], scalar=Gc[:, q + h:q + h + 1], in1=negm[:, x, :],
                               op0=ALU.subtract, op1=ALU.add)
                last.then_inc(dpre_done, 1)

            def nt(pr, x):
                c, it, q = cell(pr, x)
                dve.wait_ge(dm_done, it + 1)
                dve.wait_ge(kk_done, it + 1)
                if pr:
                    dve.wait_ge(t_mm, 4 * (pr - 1) + 3 + x)
                for h in range(HD):
                    last = stt(out=NTm[:, x, h], in0=ps[:, 2 + x, h * P:(h + 1) * P], scalar=nsk[:, q + h:q + h + 1], in1=Dm[:, x, h],
                               op0=ALU.mult, op1=ALU.mult)
                last.then_inc(nt_done, 1)

            def p_mul(pr, x):
                c, it, q = cell(pr, x)
                dve.wait_ge(kq_done, it + 1)
                if pr >= 2:
                    dve.wait_ge(o_mm, it - 3)
                V.tensor_tensor(out=Pm[:, pr % 2, x], in0=ps4(2 + x), in1=Dm[:, x], op=ALU.mult).then_inc(pm_done, 1)

            def level_mask(l, d):
                return lev[:, l, d, :].unsqueeze(1).broadcast_to([P, HD, P])

            def x_update(pr, x):
                dve.wait_ge(w_mm, 2 * pr + x + 1)
                V.copy_predicated((Rm, Om)[x][:, pr % 2, x], level_mask(0, x), ps4(2 + x)).then_inc(x_upd, 1)

            def y_update(pr, li, x):
                dve.wait_ge(wt_mm, 4 * pr + 2 * li + x + 1)
                V.copy_predicated((Om, Rm)[x][:, pr % 2, x], level_mask(li, 1 - x), ps4(2 + x)).then_inc(y_upd, 1)

            def r_step(pr, x):
                c, it, q = cell(pr, x)
                dve.wait_ge(ks_mm, it + 1)
                if pr:
                    dve.wait_ge(v_mm, it - 1)
                for h in range(HD):
                    last = stt(out=rhs[:, x, h], in0=ps[:, 6 + x, h * P:(h + 1) * P], scalar=neG[:, q + h:q + h + 1], in1=nkv[:, c, h],
                               op0=ALU.mult, op1=ALU.add)
                last.then_inc(r_done, 1)

            def vs_step(pr, x):
                c, it, q = cell(pr, x)
                dve.wait_ge(vn_done, it + 1)
                if pr:
                    dve.wait_ge(s_mm, it - 1)
                V.tensor_tensor(out=vs[:, x], in0=ps4(6 + x), in1=s2[:, q:q + 4].unsqueeze(2).broadcast_to([P, HD, P]),
                                op=ALU.mult).then_inc(vs_done, 1)

            def o_out(pr, x):
                c, it, q = cell(pr, x)
                dst = oT[:, :, c * P:(c + 1) * P]
                dve.wait_ge(o_mm, it + 1)
                if pr < 2:
                    V.tensor_copy(dst, ps4(4 + x)).then_inc(o_acc, 1)
                else:
                    dve.wait_ge(o_acc, 2 * (TT - 1 - pr) + 2)
                    V.tensor_tensor(out=dst, in0=ps4(4 + x), in1=dst, op=ALU.add).then_inc(o_acc, 1)

            def s_update(pr, x):
                c, it, q = cell(pr, x)
                dve.wait_ge(s_mm, it + 1)
                for h in range(HD):
                    last = stt(out=St[:, x, h], in0=St[:, x, h], scalar=egl[:, q + h:q + h + 1], in1=ps[:, 6 + x, h * P:(h + 1) * P],
                               op0=ALU.mult, op1=ALU.add)
                last.then_inc(s_upd, 1)

            for pr in range(TT + 1):
                sc, iv = pr - 1, pr < TT
                if iv:
                    for x in both:
                        decay_args(pr, x)
                if sc >= 0:
                    for x in both:
                        r_step(sc, x)
                if iv:
                    for x in both:
                        nt(pr, x)
                if sc >= 0:
                    for x in both:
                        vs_step(sc, x)
                if iv:
                    for x in both:
                        p_mul(pr, x)
                if sc >= 0:
                    for x in both:
                        if sc < TT - 1:
                            s_update(sc, x)
                        o_out(sc, x)
                if iv:
                    for x in both:
                        x_update(pr, x)
                    for x in both:
                        y_update(pr, 0, x)
                    for x in both:
                        y_update(pr, 1, x)
            for h in range(HD):
                dve.wait_ge(yhi_done, h + 1)
                V.tensor_tensor(out=xlo[:, h, :], in0=uT[:, h, :], in1=xhi[:, h, :].bitcast(f32), op=ALU.subtract).then_inc(y_ready, 1)
            dve.wait_ge(ost, 1)
            V.tensor_scalar(misc[:, 16:32], misc[:, 16:32], EPS, None, ALU.mult).then_inc(rk_step, 1)
            dve.wait_ge(rk_step, 4)
            stt(out=misc[:, 0:16], in0=ps[:, 6, 0:16], scalar=1.0 / P, in1=misc[:, 16:32], op0=ALU.mult, op1=ALU.add).then_inc(osd, 1)
            dve.wait_ge(osd, 2)
            V.reciprocal(misc[:, 0:16], misc[:, 0:16]).then_inc(oscale, 1)
            for h in range(HD):
                dve.wait_ge(orow, h + 1)
                stt(out=oT[:, h, :], in0=oT[:, h, :], scalar=cols[:, G_OUT:G_OUT + 1], in1=ps[:, h, :], op0=ALU.mult, op1=ALU.mult).then_inc(y_step, 1)
                dve.wait_ge(y_step, 2 * h + 1)
                V.tensor_tensor(out=oT[:, h, :], in0=oT[:, h, :], in1=zg[:, h, :], op=ALU.mult).then_inc(y_step, 1)
                if h:
                    dve.wait_ge(yhi_done, 4 + h)
                    V.tensor_tensor(out=xlo[:, 3 + h, :], in0=oT[:, h - 1, :], in1=xhi[:, 3 + h, :].bitcast(f32), op=ALU.subtract).then_inc(y_ready, 1)
            dve.wait_ge(yhi_done, 8)
            V.tensor_tensor(out=xlo[:, 7, :], in0=oT[:, 3, :], in1=xhi[:, 7, :].bitcast(f32), op=ALU.subtract).then_inc(y_ready, 1)
            lo(WOUT + 2, WOUT % 2)
            residual(1, None, 1.0)
            norm_apply(2, G_FFN2)
            lo(F2 + 1, (F2 + 1) % 2)
            ffn(1, F2)
            lo(PROJ, PROJ % 2)
            residual(2, PROJ - 1, 0.5)
            dve.wait_ge(p_tr, 1)
            V.tensor_copy(pTf[:], ps[:, 6:8, :]).then_inc(p_copy, 1)
            dve.wait_ge(pt_hi, 1)
            V.tensor_tensor(out=pTlo[:], in0=pTf[:], in1=pThi[:].bitcast(f32), op=ALU.subtract).then_inc(pt_lo, 1)
            norm_apply(3, G_GATE)
            for o in range(1, KT):
                dve.wait_ge(e_sq, o + 1)
                if o == 1:
                    V.tensor_tensor(out=sqsum[:], in0=tmp[:, 2, :], in1=tmp[:, 3, :], op=ALU.add).then_inc(e_acc, 1)
                else:
                    dve.wait_ge(e_acc, o - 1)
                    V.tensor_tensor(out=sqsum[:], in0=sqsum[:], in1=tmp[:, 2 + o % 2, :], op=ALU.add).then_inc(e_acc, 1)
            lo(GATE, GATE % 2)
            lo(GATE + 1, (GATE + 1) % 2)
            dve.wait_ge(e_std, 1)
            V.reciprocal(rstd[:, 4:8], std[:, 4:8]).then_inc(e_rstd, 1)
            lo(GATE + 2, GATE % 2)
            dve.wait_ge(e_rb, 1)
            for o in range(KT):
                dve.wait_ge(e_copy, 8)
                stt(out=eT[:, o, :], in0=eT[:, o, :], scalar=cols[:, G_PLE + o:G_PLE + o + 1], in1=ps[:, 6, :], op0=ALU.mult, op1=ALU.mult).then_inc(en_done, 1)
            for o in range(KT):
                if o == 2:
                    lo(GATE + 3, (GATE + 1) % 2)
                dve.wait_ge(sg_done, o + 1)
                dve.wait_ge(en_done, 8)
                V.tensor_tensor(out=eT[:, o, :], in0=eT[:, o, :], in1=sgm[:, o % 2, :], op=ALU.mult).then_inc(ge_done, 1)
                dve.wait_ge(ge_done, o + 1)
                V.tensor_tensor(out=hT[:, o, :], in0=hT[:, o, :], in1=eT[:, o, :], op=ALU.add).then_inc(hf_done, 1)
            dve.wait_ge(f_in, 16)
            for t in range(TT):
                dve.wait_ge(f_std, t + 1)
                V.reciprocal(rstd[:, t:t + 1], std[:, t:t + 1]).then_inc(f_rstd, 1)
                dve.wait_ge(f_rstd, t + 1)
                if t >= 2:
                    dve.wait_ge(stored[t % 2], 16 * (t // 2))
                stt(out=otile[:, t % 2, :].rearrange("p (b n) -> p b n", b=2), in0=ps[:, 4 + 2 * (t % 2):6 + 2 * (t % 2), :],
                    scalar=rstd[:, t:t + 1], in1=fbc[:].rearrange("p (b n) -> p b n", b=2), op0=ALU.mult, op1=ALU.mult).then_inc(f_out, 1)


_INS = ["x", "p", "ffn1_norm", "ffn1_w_gate", "ffn1_w_up", "ffn1_w_down", "mix_norm", "w_in", "gm_ln_g", "gm_ln_b", "gm_ws",
        "gm_bs", "dn_conv_w", "dn_a_log", "dn_dt_bias", "dn_out_norm", "w_out", "ffn2_norm", "ffn2_w_gate", "ffn2_w_up",
        "ffn2_w_down", "ple_proj", "ple_norm", "ple_gate_norm", "ple_gate_w", "ple_gate_b", "final_norm"]


def kernel(**inputs):
    import numpy as np
    import concourse.bacc as bacc
    from concourse.bass_utils import run_bass_kernel_spmd as run

    nc = bacc.Bacc("TRN2", target_bir_lowering=False, num_devices=1)
    arrays, io = {}, {}
    for name in _INS:
        a = np.ascontiguousarray(inputs[name])
        arrays[f"in_{name}"] = a
        io[name] = nc.dram_tensor(f"in_{name}", a.shape, mybir.dt.from_np(a.dtype), kind="ExternalInput").ap()
    io["out"] = nc.dram_tensor("out_0", (1, T, D), mybir.dt.float32, kind="ExternalOutput").ap()
    io["kk_rows"] = nc.dram_tensor("kk_rows", (P, TT * HD, B), mybir.dt.float32, kind="Internal").ap()
    io["inv_rows"] = nc.dram_tensor("inv_rows", (P, B, B), mybir.dt.float32, kind="Internal").ap()
    build(nc, io)
    r = run(nc, [arrays], core_ids=[0])
    return r.results[0]["out_0"]
```

```python
import concourse.bass as bass
from concourse import mybir
from contextlib import ExitStack

P = 128
D = 1024
KT = D // P
T = 512
TT = T // P
FF = 2816
FP = FF // (2 * P)
HD = 4
PLE = 256
EPS = 1e-6
NEG = -1e30

F1 = 0
WIN = F1 + 3 * FP
WOUT = WIN + 12
F2 = WOUT + 4
PROJ = F2 + 3 * FP
GATE = PROJ + 1
B = 32
NB = P // B
NI = 2 * TT * HD * NB
assert NI == P


def build(nc, io):
    f32, f32r, i8 = mybir.dt.float32, mybir.dt.float32r, mybir.dt.int8
    ALU, ACT = mybir.AluOpType, mybir.ActivationFunctionType
    ctx = ExitStack()
    with ctx:
        cursor = [(nc.sbuf_base + 63) // 64 * 64]

        def sb(name, shape, dt=f32, offset=None):
            n = 1 if dt == i8 else 4
            for s in shape[1:]:
                n *= s
            if offset is None:
                offset = cursor[0]
                cursor[0] += (n + 63) // 64 * 64
            return nc.alloc_sbuf_tensor_at(name, shape, dt, offset=offset)

        def sem(name):
            return ctx.enter_context(nc.semaphore(name))

        hT = sb("hT", [P, KT, T])
        x_at = cursor[0]
        xhi = sb("xhi", [P, KT, T], f32r)
        xlo = sb("xlo", [P, KT, T], f32r)
        raw = [sb(f"raw{i}", [P, 2048]) for i in range(2)]
        whi = [sb(f"whi{i}", [P, 2048], f32r) for i in range(2)]
        wlo = [sb(f"wlo{i}", [P, 2048], f32r) for i in range(2)]
        ident = sb("ident", [P, P])
        ones = sb("ones", [P, P])
        eps = sb("eps", [P, 1])
        cols = sb("cols", [P, 109])
        tri = sb("tri", [P, 2, P])
        negm = sb("negm", [P, 2, P])
        lev = sb("lev", [P, 2, 2, P], i8)
        sgn = sb("sgn", [P, 1])
        ss = sb("ss", [P, 8])
        std = sb("std", [P, 8])
        rstd = sb("rstd", [P, 8])
        pTf = sb("pTf", [P, 2, T])
        sqsum = sb("sqsum", [P, T])
        small = sb("small", [P, 15, 32])
        mv = sb("mv", [P, 16, 2])
        lsd = sb("lsd", [P, 16])
        lrs = sb("lrs", [P, 16])
        rrow = sqsum
        tmp_at = cursor[0]
        tmp = sb("tmp", [P, 4, T])
        arena = cursor[0]
        G_FFN1, G_MIX, G_FFN2, G_GATE, G_PLE, B_GATE, G_CONV, G_OUT = 0, 8, 16, 24, 32, 40, 48, 108

        guhi = sb("guhi", [P, 2 * FP, T], f32r)
        gulo = sb("gulo", [P, 2 * FP, T], f32r)
        end = cursor[0]
        assert end <= nc.sbuf_usable_end, (end, nc.sbuf_usable_end)
        cursor[0] = arena
        xtok = sb("xtok", [P, TT, D])
        g1rows = sb("g1rows", [8, P])
        vrows = sb("vrows", [101, P])
        sqjunk = sb("sqjunk", [P, D])
        ptok = sb("ptok", [P, TT, PLE])
        cursor[0] = arena
        qT = sb("qT", [P, HD, T])
        kT = sb("kT", [P, HD, T])
        ktok = sb("ktok", [P, TT, HD, P])
        nkv = sb("nkv", [P, TT, HD, P])
        zg_at = cursor[0]
        zg = sb("zg", [P, HD, T])
        uT_at = cursor[0]
        uT = sb("uT", [P, HD, T])
        oT_at = cursor[0]
        oT = sb("oT", [P, HD, T])
        St = sb("St", [P, 2, HD, P])
        nx_at = cursor[0]
        NTm = sb("NTm", [P, 2, HD, P])
        vn = sb("vn", [P, 2, HD, P])
        svb = sb("svb", [P, 2, T], offset=nx_at + 4096)
        d_at = cursor[0]
        Dm = sb("Dm", [P, 2, HD, P])
        Em = sb("Em", [P, 2, HD, P])
        wab = sb("wab", [P, 240], offset=d_at)
        wabhi = sb("wabhi", [P, 240], f32r, offset=d_at + 960)
        wablo = sb("wablo", [P, 240], f32r, offset=d_at + 1920)
        abT = sb("abT", [16, T], offset=d_at + 2880)
        bns = sb("bns", [P, 16, 6], offset=d_at + 4928)
        t_at = cursor[0]
        Tm = sb("Tm", [P, 2, HD, P])
        wsraw = sb("wsraw", [P, HD, P], offset=t_at)
        lng = sb("lng", [P, T], offset=nx_at + 4096)
        lnb = sb("lnb", [P, T], offset=nx_at + 6144)
        wsT = sb("wsT", [P, HD, P])
        xb = sb("xb", [P, 2, TT, HD, B])
        bsb = sb("bsb", [P, T])
        kkd = sb("kkd", [P, TT, HD, B], offset=uT_at)
        gsT = sb("gsT", [32, 2, P], offset=uT_at + 2048)
        Xi = sb("Xi", [P, B, B], offset=oT_at)
        Zi = sb("Zi", [P, B, B], offset=oT_at + 4096)
        prod = sb("prod", [P, 256], offset=zg_at)
        gsi = sb("gsi", [P, 2, B], offset=zg_at + 1024)
        gi, si = gsi[:, 0, :], gsi[:, 1, :]
        Ei = sb("Ei", [P, B, B], offset=zg_at + 2048)
        assert cursor[0] <= end
        Pm = sb("Pm", [P, 2, 2, HD, P], offset=x_at)
        qd = sb("qd", [P, 2, 2, HD, P], offset=x_at + 8192)
        Rm = sb("Rm", [P, 2, 2, HD, P], offset=x_at + 16384)
        Om = sb("Om", [P, 2, 2, HD, P], offset=x_at + 24576)
        acc = sb("acc", [P, 2, T], offset=tmp_at)
        mb = sb("mb", [P, 2, T], offset=tmp_at + 4096)
        vg = sb("vg", [P, TT, T], offset=tmp_at)
        rhs = sb("rhs", [P, 2, HD, P], offset=tmp_at)
        vs = sb("vs", [P, 2, HD, P], offset=tmp_at + 4096)
        (aa, ea, gg, be, Gc, nsk, eG, neG, egl, egd, sk, s2, misc, bc8, misc2) = [small[:, i, :] for i in range(15)]
        nk = misc2[:, 0:16]
        rk2 = misc2[:, 16:32]
        cursor[0] = arena
        pThi = sb("pThi", [P, 2, T], f32r)
        pTlo = sb("pTlo", [P, 2, T], f32r)
        eT = sb("eT", [P, KT, T])
        fbc = sb("fbc", [P, D])
        otile = sb("otile", [P, TT, D])
        fjunk = sb("fjunk", [P, TT, T])
        fb = sb("fb", [P, TT])
        sgm = sb("sgm", [P, 2, T])
        assert cursor[0] <= end

        ps = ctx.enter_context(nc.psum_tensor("ps", [P, 8, T], f32))

        raw_in = [sem("raw_in0"), sem("raw_in1")]
        hi_done, lo_done, w_done = sem("hi_done"), sem("lo_done"), sem("w_done")
        x_in = [sem(f"x_in{t}") for t in range(TT)]
        vec_in, bc_in, ab_in, ws_in, p_in, f_in = [sem(s) for s in ("vec_in", "bc_in", "ab_in", "ws_in", "p_in", "f_in")]
        g1_in, g1_tr, g1_done = sem("g1_in"), sem("g1_tr"), sem("g1_done")
        const_step, const_done = sem("const_step"), sem("const_done")
        xtr_done, vtr_done, hx_act, hx_dve, cols_done, ss0_done = [
            sem(s) for s in ("xtr_done", "vtr_done", "hx_act", "hx_dve", "cols_done", "ss0_done")]
        gr_done, silu_done, ur_done, gu_done, guhi_done, gulo_done = [
            sem(s) for s in ("gr_done", "silu_done", "ur_done", "gu_done", "guhi_done", "gulo_done")]
        rr_done, y_used = sem("rr_done"), sem("y_used")
        z_scaled, ab_scaled, pair_scaled = sem("z_scaled"), sem("ab_scaled"), sem("pair_scaled")
        out_done, h_done, sq_done, acc_done = [sem(s) for s in ("out_done", "h_done", "sq_done", "acc_done")]
        stats_done, std_done, rstd_done, rb_done = [sem(s) for s in ("stats_done", "std_done", "rstd_done", "rb_done")]
        xhi_done, x_ready = sem("xhi_done"), sem("x_ready")
        conv_tap, conv_done, zact_done, zsq_done, qk_stat, tok_tr, ktok_done, nkv_done = [
            sem(s) for s in ("conv_tap", "conv_done", "zact_done", "zsq_done", "qk_stat", "tok_tr", "ktok_done", "nkv_done")]
        nk_done, rk_step = sem("nk_done"), sem("rk_step")
        wab_hi, wab_step, ab_mm, ab_tr = [sem(s) for s in ("wab_hi", "wab_step", "ab_mm", "ab_tr")]
        gate_act, gate_dve, cum_done, col_act, col_dve = [sem(s) for s in ("gate_act", "gate_dve", "cum_done", "col_act", "col_dve")]
        vgelu, ln_step, ln_sd, ln_done, ws_tr, ws_done, ugelu, sv_done, gm_step, gm_done = [
            sem(s) for s in ("vgelu", "ln_step", "ln_sd", "ln_done", "ws_tr", "ws_done", "ugelu", "sv_done", "gm_step", "gm_done")]
        zg_done = sem("zg_done")
        tap0 = sem("tap0")
        kkd_mm, kkd_done, gs_tr, gs_done, kin_in, gin_in, zi_dve, zi_exp, xi_step, xi_done = [
            sem(s) for s in ("kkd_mm", "kkd_done", "gs_tr", "gs_done", "kin_in", "gin_in", "zi_dve", "zi_exp", "xi_step", "xi_done")]
        kk_stored, inv_stored = sem("kk_stored"), sem("inv_stored")
        xb_in, r_zero, r_init = sem("xb_in"), sem("r_zero"), sem("r_init")
        grow_done, kk_done, kq_done, dpre_done, dm_done, em_done, pm_done, nt_done = [
            sem(s) for s in ("grow_done", "kk_done", "kq_done", "dpre_done", "dm_done", "em_done", "pm_done", "nt_done")]
        qd_done, o_tr, o_init = sem("qd_done"), sem("o_transposed"), sem("o_init")
        t_mm, t_copy, w_mm, x_upd, wt_mm, y_upd = [sem(s) for s in ("t_mm", "t_copy", "w_mm", "x_upd", "wt_mm", "y_upd")]
        s_zero, ks_mm, r_done, v_mm, vn_done, vs_done, o_mm, s_mm, s_upd, o_acc = [
            sem(s) for s in ("s_zero", "ks_mm", "r_done", "v_mm", "vn_done", "vs_done", "o_mm", "s_mm", "s_upd", "o_acc")]
        osq, ost, osd, oscale, orow, y_step, yhi_done, y_ready = [
            sem(s) for s in ("osq", "ost", "osd", "oscale", "orow", "y_step", "yhi_done", "y_ready")]
        p_tr, p_copy, pt_hi, pt_lo, e_mm, e_sq, e_acc = [
            sem(s) for s in ("p_tr", "p_copy", "pt_hi", "pt_lo", "e_mm", "e_sq", "e_acc")]
        e_stats, e_std, e_rstd, e_rb, en_done, gs_scaled = [sem(s) for s in ("e_stats", "e_std", "e_rstd", "e_rb", "en_done", "gs_scaled")]
        f_first, g_six, f_mul, f_bias, f_half = [sem(s) for s in ("f_first", "g_six", "f_mul", "f_bias", "f_half")]
        sg_done, ge_done, hf_done, f_tr, f_ss, f_std, f_rstd, f_out, stored = [
            sem(s) for s in ("sg_done", "ge_done", "hf_done", "f_tr", "f_ss", "f_std", "f_rstd", "f_out", "stored")]

        block = ctx.enter_context(nc.Block())
        own = lambda d, b: slice(64 * d + 16 * b, 64 * d + 16 * b + 16)
        ch = lambda jj: jj if jj >= 8 else (jj + 4) % 8
        BANK = [(o + 4) % 8 for o in range(KT)]

        def square_sum(eng, E, og, o):
            eng.wait_ge(sq_done, 8 * og + o + 1)
            if o > 1:
                eng.wait_ge(acc_done, 7 * og + o - 1)
            E.tensor_tensor(out=sqsum[:], in0=tmp[:, 0, :] if o == 1 else sqsum[:], in1=tmp[:, o % 4, :], op=ALU.add).then_inc(acc_done, 1)

        def wcol(w, n):
            return w[n % 2][:].rearrange("p (k n) -> p k n", n=256)

        def wrow(w, n, c):
            return w[n % 2][:].rearrange("p (k n) -> p k n", n=c)

        @block.sync
        def _(sp):
            def load(n, p, src, dst=None):
                if not isinstance(n, int) or n >= 2:
                    sp.wait_ge(lo_done, n - 1)
                sp.dma_start(raw[p][:].rearrange("p (k n) -> p k n", n=dst or 256), src).then_inc(raw_in[p], 16)

            def col_pair(w, i):
                return w[:, bass.ds(i * 256, 256)].rearrange("(k p) n -> p k n", p=P)

            def row_pair(w, j):
                return w[bass.ds(j * 256, 256), :].rearrange("(f p) n -> p f n", p=P)

            def ffn(n0, wg, wu, wd):
                load(n0, n0 % 2, col_pair(wg, 0))
                load(n0 + 1, (n0 + 1) % 2, col_pair(wu, 0))
                if n0 == F1:
                    rows = [("mix_norm", 0), ("ffn2_norm", 8), ("ple_gate_norm", 16), ("ple_norm", 24), ("ple_gate_b", 32)]
                    for name, r in rows:
                        sp.dma_start(vrows[r:r + 8, :], io[name][0].rearrange("(k p) -> k p", p=P)).then_inc(vec_in, 16)
                    sp.dma_start(vrows[40:100, :], io["dn_conv_w"][0].rearrange("j (t p) -> (j t) p", p=P)).then_inc(vec_in, 16)
                    sp.dma_start(vrows[100:101, :], io["dn_out_norm"]).then_inc(vec_in, 16)
                with sp.Fori(1, FP) as i:
                    load(i * 2 + n0, n0 % 2, col_pair(wg, i))
                    load(i * 2 + (n0 + 1), (n0 + 1) % 2, col_pair(wu, i))
                n1 = n0 + 2 * FP
                with sp.Fori(0, FP - 1, 2) as j:
                    load(j + n1, n1 % 2, row_pair(wd, j), D)
                    load(j + (n1 + 1), (n1 + 1) % 2, row_pair(wd, j + 1), D)
                load(n1 + FP - 1, (n1 + FP - 1) % 2, row_pair(wd, FP - 1), D)

            sp.dma_start(g1rows[:], io["ffn1_norm"][0].rearrange("(k p) -> k p", p=P)).then_inc(g1_in, 16)
            xv = io["x"][0].rearrange("(t p) n -> p t n", p=P)
            for t in range(TT):
                sp.dma_start(xtok[:, t, :], xv[:, t, :]).then_inc(x_in[t], 16)
            ffn(F1, io["ffn1_w_gate"][0], io["ffn1_w_up"][0], io["ffn1_w_down"][0])
            wi = io["w_in"][0]
            for s, c0 in enumerate((1536, 1792, 1024, 1280, 2048, 2304)):
                load(WIN + s, (WIN + s) % 2, wi[:, c0:c0 + 256].rearrange("(k p) n -> p k n", p=P))
            for s, c0 in enumerate((0, 256)):
                load(WIN + 6 + s, (WIN + 6 + s) % 2, wi[:, c0:c0 + 256].rearrange("(k p) n -> p k n", p=P))
            for s in range(2):
                load(WIN + 8 + s, (WIN + 8 + s) % 2, wi[512 * s:512 * (s + 1), 512:1024].rearrange("(k p) n -> p k n", p=P), 512)
            for s, c0 in enumerate((2560, 2816)):
                load(WIN + 10 + s, (WIN + 10 + s) % 2, wi[:, c0:c0 + 256].rearrange("(k p) n -> p k n", p=P))
            for s in range(4):
                load(WOUT + s, (WOUT + s) % 2, col_pair(io["w_out"][0], s))
                if s == 1:
                    sp.wait_ge(xi_done, 1)
                    sp.dma_start(io["inv_rows"], Xi[:]).then_inc(inv_stored, 16)
                    sp.wait_ge(inv_stored, 16)
                    for d in range(2):
                        for b in range(NB):
                            sp.dma_start(xb[b * B:(b + 1) * B, d].rearrange("j c h i -> j (c h) i"),
                                         io["inv_rows"][own(d, b)].rearrange("q j i -> j q i")).then_inc(xb_in, 16)
            ffn(F2, io["ffn2_w_gate"][0], io["ffn2_w_up"][0], io["ffn2_w_down"][0])
            load(PROJ, PROJ % 2, row_pair(io["ple_proj"][0], 0), D)
            for s in range(4):
                load(GATE + s, (GATE + s) % 2, col_pair(io["ple_gate_w"][0], s))
            ov = io["out"][0].rearrange("(t p) n -> p t n", p=P)
            for t in range(TT):
                sp.wait_ge(f_out, t + 1)
                sp.wait_ge(f_half, t + 1)
                sp.dma_start(ov[:, t, :], otile[:, t, :]).then_inc(stored, 16)
            sp.wait_ge(stored, 16 * TT)

        @block.gpsimd
        def _(pool):
            step = [0]

            def fill(ap, v):
                nc.gpsimd.memset(ap, v).then_inc(const_step, 1)
                step[0] += 1

            def sel(ap, pattern, base, cm, op, fillv):
                pool.wait_ge(const_step, step[0])
                nc.gpsimd.affine_select(out=ap, in_=ap, pattern=pattern, compare_op=op, fill=fillv, base=base,
                                        channel_multiplier=cm).then_inc(const_step, 1)
                step[0] += 1

            fill(ones[:], 1.0)
            fill(eps[:], EPS)
            fill(sgn[:], -1.0)
            fill(ident[:], 0.0)
            sel(ident[:], [[-1, P]], 0, 1, ALU.not_equal, 1.0)
            pool.dma_start(ptok[:], io["p"][0, 0].rearrange("(t p) n -> p t n", p=P)).then_inc(p_in, 16)
            pool.wait_ge(const_step, step[0])
            nc.gpsimd.memset(sgn[0:64, :], 1.0).then_inc(const_done, 1)
            pool.wait_ge(const_done, 1)
            fill(tri[:], 1.0)
            fill(negm[:], 0.0)
            for d, sg in ((0, 1), (1, -1)):
                sel(tri[:, d, :], [[sg, P]], 0, -sg, ALU.is_ge, 0.0)
                sel(negm[:, d, :], [[sg, P]], 0, -sg, ALU.is_ge, NEG)
            fill(lev[:], 0.0)
            for l in range(2):
                s = B << l
                v = lev[:, l, :, :].rearrange("p d (b e r) -> p d b e r", e=2, r=s)
                for d in range(2):
                    part = v[:, d, :, d, :]
                    pool.wait_ge(const_step, step[0])
                    fill(part, 1.0)
                    lo = s if d == 0 else 0
                    sel(part, [[-2 * s, P // (2 * s)], [0, s]], -lo, 1, ALU.is_ge, 0.0)
                    sel(part, [[2 * s, P // (2 * s)], [0, s]], lo + s - 1, -1, ALU.is_ge, 0.0)
            pool.wait_ge(const_step, step[0])
            pool.sem_inc(const_done, 1)
            for o in range(1, KT):
                square_sum(pool, nc.gpsimd, 0, o)
            pool.wait_ge(w_done, WIN)
            pool.wait_ge(gulo_done, FP)
            pool.dma_start(wsraw[:], io["gm_ws"][0].rearrange("h i j -> i h j")).then_inc(ws_in, 16)
            pool.dma_start(wab[:, 0:128].rearrange("p (k n) -> p k n", n=16),
                           io["w_in"][0][:, 3072:3088].rearrange("(k p) n -> p k n", p=P)).then_inc(ab_in, 16)
            pool.dma_start(bc8[:, 0:8], io["dn_dt_bias"].rearrange("a h d -> a (h d)").broadcast_to([P, 8])).then_inc(bc_in, 16)
            pool.dma_start(bc8[:, 8:16], io["dn_a_log"].rearrange("a h d -> a (h d)").broadcast_to([P, 8])).then_inc(bc_in, 16)
            pool.dma_start(bsb[:], io["gm_bs"].rearrange("a h d -> a (h d)").broadcast_to([P, T])).then_inc(bc_in, 16)
            pool.dma_start(lng[:], io["gm_ln_g"].rearrange("a h d -> a (h d)").broadcast_to([P, T])).then_inc(bc_in, 16)
            pool.dma_start(lnb[:], io["gm_ln_b"].rearrange("a h d -> a (h d)").broadcast_to([P, T])).then_inc(bc_in, 16)
            nc.gpsimd.memset(St[:], 0.0).then_inc(s_zero, 1)
            pool.wait_ge(kkd_done, 16)
            pool.dma_start(io["kk_rows"], kkd[:].rearrange("p c h i -> p (c h) i")).then_inc(kk_stored, 16)
            pool.wait_ge(kk_stored, 16)
            for d in range(2):
                for b in range(NB):
                    pool.dma_start(Zi[own(d, b)], io["kk_rows"][b * B:(b + 1) * B].rearrange("j q i -> q j i")).then_inc(kin_in, 16)
            pool.wait_ge(w_done, WOUT)
            pool.wait_ge(zsq_done, 8)

            def zero_blocks(pr):
                for x in range(2):
                    if pr >= 2:
                        pool.wait_ge(v_mm, 2 * pr + x - 3)
                    nc.gpsimd.memset(Rm[:, pr % 2, x], 0.0).then_inc(r_zero, 1)

            zero_blocks(0)
            zero_blocks(1)
            pool.wait_ge(ln_step, 34)
            nc.gpsimd.tensor_tensor(out=vg[:], in0=vg[:], in1=lng[:].unsqueeze(1).broadcast_to([P, TT, T]), op=ALU.mult).then_inc(ln_step, 1)
            pool.wait_ge(ln_step, 35)
            nc.gpsimd.tensor_tensor(out=vg[:], in0=vg[:], in1=lnb[:].unsqueeze(1).broadcast_to([P, TT, T]), op=ALU.add).then_inc(ln_done, 1)
            for pr in range(TT):
                if 0 < pr < TT - 1:
                    zero_blocks(pr + 1)
                for x in range(2):
                    c = pr if x == 0 else TT - 1 - pr
                    it = 2 * pr + x
                    pool.wait_ge(em_done, it + 1)
                    if pr >= 2:
                        pool.wait_ge(o_mm, it - 3)
                    nc.gpsimd.tensor_tensor(out=qd[:, pr % 2, x], in0=qT[:, :, c * P:(c + 1) * P], in1=Em[:, x], op=ALU.mult).then_inc(qd_done, 1)
            for og in (1, 2):
                for o in range(1, KT):
                    square_sum(pool, nc.gpsimd, og, o)
            pool.wait_ge(w_done, PROJ)
            pool.dma_start(fbc[:], io["final_norm"].rearrange("(a n) -> a n", a=1).broadcast_to([P, D])).then_inc(f_in, 16)

        @block.tensor
        def _(pe):
            mm = nc.tensor.matmul

            def three(out, whi_, wlo_, hi_, lo_, start, stop):
                mm(out, whi_, hi_, start=start, stop=False)
                mm(out, whi_, lo_, start=False, stop=False)
                return mm(out, wlo_, hi_, start=False, stop=stop)

            def col_slot(n, b0, b1, xw=None, before={}):
                for k in range(KT):
                    if k in before:
                        before[k]()
                    if xw is not None:
                        pe.wait_ge(x_ready, xw + k + 1)
                    for f, b in enumerate((b0, b1)):
                        last = three(ps[:, b, :], wcol(whi, n)[:, k, f * P:(f + 1) * P], wcol(wlo, n)[:, k, f * P:(f + 1) * P],
                                     xhi[:, k, :], xlo[:, k, :], k == 0, k == KT - 1)
                last.then_inc(w_done, 1)

            def row_bcast(bank, src, n, done):
                for t in range(n):
                    last = mm(ps[:, bank, t * P:(t + 1) * P], src[:, t:t + 1].broadcast_to([P, P]), ident[:], start=True, stop=True)
                last.then_inc(done, 1)

            def norm_stats(ni, bank=BANK[0]):
                pe.wait_ge(acc_done, 7 * ni)
                for t in range(TT):
                    last = mm(ps[:, bank, t:t + 1], sqsum[:, t * P:(t + 1) * P], ones[:, 0:1], start=True, stop=True)
                last.then_inc(stats_done, 1)

            def first_slot(n, b0, b1, xw, ni):
                col_slot(n, b0, b1, xw=xw, before={6: (lambda: norm_stats(ni)) if ni else start_rest})

            def start_rest():
                pe.wait_ge(hx_act, 4)
                pe.wait_ge(hx_dve, 4)
                pe.wait_ge(vec_in, 7 * 16)
                nc.tensor.transpose(ps[:, 4, 0:101], vrows[:], ident[0:101, 0:101]).then_inc(vtr_done, 1)
                pe.wait_ge(p_in, 16)
                for kk in range(2):
                    for t in range(TT):
                        last = nc.tensor.transpose(ps[:, 6 + kk, t * P:(t + 1) * P], ptok[:, t, kk * P:(kk + 1) * P], ident[:])
                last.then_inc(p_tr, 1)

            def norm_bcast(ni, bank=BANK[1]):
                pe.wait_ge(rstd_done, ni + 1)
                row_bcast(bank, rstd, TT, rb_done)

            def ffn(u, n0):
                pe.wait_ge(lo_done, n0 + 1)
                if u:
                    pe.wait_ge(h_done, 8 * u + 6)
                else:
                    pe.wait_ge(hx_act, 1)
                    pe.wait_ge(hx_dve, 1)
                first_slot(n0, 0, 1, 0 if u == 0 else 16, 2 * u)
                pe.wait_ge(lo_done, n0 + 2)
                if u:
                    pe.wait_ge(h_done, 8 * u + 8)
                col_slot(n0 + 1, 2, 3, before={3: lambda: norm_bcast(2 * u)})
                with pe.Fori(1, FP) as i:
                    pe.wait_ge(lo_done, i * 2 + (n0 + 1))
                    pe.wait_ge(gr_done, i + u * FP)
                    col_slot(n0, 0, 1)
                    pe.wait_ge(lo_done, i * 2 + (n0 + 2))
                    pe.wait_ge(ur_done, i + u * FP)
                    col_slot(n0 + 1, 2, 3)
                n1 = n0 + 2 * FP

                def down(n, j, first=False, last_slot=False):
                    pe.wait_ge(lo_done, j + (n1 + 1))
                    pe.wait_ge(gulo_done, j + (u * FP + 1))
                    for o in range(KT):
                        if first and o == 4:
                            pe.wait_ge(ur_done, (u + 1) * FP)
                        for fl in range(2):
                            g = bass.ds(j * 2 + fl, 1)
                            last = three(ps[:, BANK[o], :], wrow(whi, n, D)[:, fl, o * P:(o + 1) * P], wrow(wlo, n, D)[:, fl, o * P:(o + 1) * P],
                                         guhi[:, g, :], gulo[:, g, :], first and fl == 0, last_slot and fl == 1)
                        if last_slot and o < KT - 1:
                            last.then_inc(out_done, 1)
                    last.then_inc(w_done, 1)

                down(n1, 0, first=True)
                with pe.Fori(1, FP - 2, 2) as j:
                    down(n1 + 1, j)
                    down(n1 + 2, j + 1)
                down(n1 + FP - 2, FP - 2)
                down(n1 + FP - 1, FP - 1, last_slot=True)

            pe.wait_ge(const_done, 1)
            pe.wait_ge(g1_in, 16)
            nc.tensor.transpose(ps[:, 0, 0:8], g1rows[:], ident[0:8, 0:8]).then_inc(g1_tr, 1)
            pe.wait_ge(g1_done, 1)
            for t in range(TT):
                pe.wait_ge(x_in[t], 16)
                for k in range(KT):
                    last = nc.tensor.transpose(ps[:, k, t * P:(t + 1) * P], xtok[:, t, k * P:(k + 1) * P], ident[:])
            last.then_inc(xtr_done, 1)
            ffn(0, F1)

            def qkv_post(s):
                for jj in (2 * s, 2 * s + 1):
                    if jj < 8:
                        pe.wait_ge(zsq_done, jj + 1)
                        if jj == 6:
                            pe.wait_ge(nk_done, 1)
                        for c in range(TT):
                            last = mm(ps[:, 4, jj * 4 + c:jj * 4 + c + 1], mb[:, jj % 2, c * P:(c + 1) * P], ones[:, 0:1], start=True, stop=True)
                        last.then_inc(qk_stat, 1)
                    if jj < 4 or jj >= 8:
                        src = kT[:, jj] if jj < 4 else mb[:, jj % 2]
                        pe.wait_ge(zact_done, jj + 1)
                        if jj in (2, 3):
                            pe.wait_ge(ktok_done, jj - 1)
                        elif jj in (8, 9):
                            pe.wait_ge(kkd_done, 16)
                        elif jj in (10, 11):
                            pe.wait_ge(nkv_done, jj - 9)
                        for c in range(TT):
                            last = nc.tensor.transpose(ps[:, 5 + jj % 2, c * P:(c + 1) * P], src[:, c * P:(c + 1) * P], ident[:])
                        last.then_inc(tok_tr, 1)

            for s in range(6):
                n = WIN + s
                pe.wait_ge(lo_done, n + 1)
                if s == 0:
                    pe.wait_ge(h_done, 6)
                    first_slot(n, 0, 1, 8, 1)
                elif s == 1:
                    pe.wait_ge(h_done, 8)
                    col_slot(n, 2, 3, before={1: lambda: norm_bcast(1)})
                    pe.wait_ge(rr_done, 2)
                else:
                    pe.wait_ge(conv_done, 2 * s - 2)
                    col_slot(n, (2 * s) % 4, (2 * s) % 4 + 1)
                if s == 0:
                    pe.wait_ge(ws_in, 16)
                    for h in range(HD):
                        last = nc.tensor.transpose(ps[:, 7, h * P:(h + 1) * P], wsraw[:, h], ident[:])
                    last.then_inc(ws_tr, 1)
                if s == 1:
                    pe.wait_ge(wab_step, 2)
                    pe.wait_ge(ws_done, 1)
                    for k in range(KT):
                        last = three(ps[:, 7, :], wabhi[:, k * 16:k * 16 + P], wablo[:, k * 16:k * 16 + P], xhi[:, k, :], xlo[:, k, :], k == 0, k == KT - 1)
                    last.then_inc(ab_mm, 1)
                if s >= 1:
                    qkv_post(s - 1)
                if s == 2:
                    pe.wait_ge(ab_scaled, 1)
                    for c in range(TT):
                        last = nc.tensor.transpose(ps[:, 7, c * 16:(c + 1) * 16], abT[:, c * P:(c + 1) * P], ident[0:16, 0:16])
                    last.then_inc(ab_tr, 1)
                if s in (3, 4):
                    pe.wait_ge(ktok_done, 4)
                    for c in (2 * s - 6, 2 * s - 5):
                        if c >= 2:
                            pe.wait_ge(kkd_done, 4 * (c - 1))
                        for h in range(HD):
                            last = mm(ps[:, 5 + c % 2, h * P:(h + 1) * P], kT[:, h, c * P:(c + 1) * P], kT[:, h, c * P:(c + 1) * P], start=True, stop=True)
                        last.then_inc(kkd_mm, 1)
                if s == 4:
                    pe.wait_ge(gate_dve, 5)
                    mm(ps[:, 7, 64:80], tri[:, 0, :], gg[:, 0:16], start=True, stop=True)
                    mm(ps[:, 7, 80:96], tri[:, 1, :], gg[:, 16:32], start=True, stop=True)
                    mm(ps[:, 7, 96:128], ones[:], gg, start=True, stop=True).then_inc(cum_done, 1)
                if s == 5:
                    pe.wait_ge(col_dve, 5)
                    nc.tensor.transpose(ps[0:32, 7, 128:256], Gc, ident[:])
                    nc.tensor.transpose(ps[0:32, 7, 256:384], nsk, ident[:]).then_inc(gs_tr, 1)
            for s in range(2):
                n = WIN + 6 + s
                pe.wait_ge(lo_done, n + 1)
                pe.wait_ge(conv_done, 10 + 2 * s)
                col_slot(n, 2 * s, 2 * s + 1)
                if s == 0:
                    qkv_post(5)
            for s in range(2):
                n = WIN + 8 + s
                pe.wait_ge(lo_done, n + 1)
                if s == 0:
                    pe.wait_ge(rk_step, 3)
                    pe.wait_ge(nkv_done, 4)
                    pe.wait_ge(gs_done, 1)
                for t in range(TT):
                    tok = slice(t * P, (t + 1) * P)
                    for kl in range(4):
                        k = 4 * s + kl
                        wh, wl = wrow(whi, n, 512)[:, kl], wrow(wlo, n, 512)[:, kl]
                        mm(ps[:, 4 + t, :], xhi[:, k, tok], wh, start=(k == 0), stop=False)
                        mm(ps[:, 4 + t, :], xlo[:, k, tok], wh, start=False, stop=False)
                        last = mm(ps[:, 4 + t, :], xhi[:, k, tok], wl, start=False, stop=(k == KT - 1))
                last.then_inc(w_done, 1)
            for s in range(2):
                n = WIN + 10 + s
                pe.wait_ge(lo_done, n + 1)
                pe.wait_ge(ugelu, s + 1)
                col_slot(n, 2 * s, 2 * s + 1)

            def spatial():
                pe.wait_ge(ln_done, 1)
                for h in (2, 3, 0, 1):
                    for c in range(TT):
                        last = mm(ps[:, 4 + h, c * P:(c + 1) * P], vg[:, c, h * P:(h + 1) * P], wsT[:, h], start=True, stop=True)
                    last.then_inc(sv_done, 1)

            def heads(bank, lhs, rhs_, done, start=True, stop=True):
                for h in range(HD):
                    last = mm(ps[:, bank, h * P:(h + 1) * P], lhs(h), rhs_(h), start=start, stop=stop)
                last.then_inc(done, 1)

            def toks(pr, x):
                c = (pr, TT - 1 - pr)[x]
                return c, slice(c * P, (c + 1) * P)

            def X(pr, x):
                return (Rm, Om)[x][:, pr % 2, x]

            def Y(pr, x):
                return (Om, Rm)[x][:, pr % 2, x]

            def grow(pr, x):
                c, tok = toks(pr, x)
                if pr:
                    pe.wait_ge(t_copy, 4 * (pr - 1) + 3 + x)
                heads(x, lambda h: Gc[:, x * 16 + c * 4 + h:x * 16 + c * 4 + h + 1].broadcast_to([P, P]), lambda h: ident[:], grow_done)

            def kk(pr, x):
                c, tok = toks(pr, x)
                if pr:
                    pe.wait_ge(y_upd, 4 * (pr - 1) + 3 + x)
                heads(2 + x, lambda h: kT[:, h, tok], lambda h: kT[:, h, tok], kk_done)

            def kq(pr, x):
                c, tok = toks(pr, x)
                pe.wait_ge(nt_done, 2 * pr + x + 1)
                heads(2 + x, lambda h: kT[:, h, tok], lambda h: qT[:, h, tok], kq_done)

            def transpose_blocks(pr, x):
                pe.wait_ge(r_init, 2 * pr + x + 1)
                pe.wait_ge(em_done, 2 * pr + x + 1)
                for h in range(HD):
                    last = nc.tensor.transpose(ps[:, x, h * P:(h + 1) * P], Rm[:, pr % 2, x, h], ident[:])
                last.then_inc(o_tr, 1)

            def t_step(pr, li, x):
                if li == 0:
                    pe.wait_ge(o_init, 2 * pr + x + 1)
                else:
                    pe.wait_ge(x_upd, 2 * pr + x + 1)
                heads(x, lambda h: NTm[:, x, h], lambda h: X(pr, x)[:, h], t_mm)

            def w_step(pr, x):
                pe.wait_ge(t_copy, 4 * pr + x + 1)
                pe.wait_ge(pm_done, 2 * pr + x + 1)
                heads(2 + x, lambda h: Y(pr, x)[:, h], lambda h: Tm[:, x, h], w_mm)

            def wt_step(pr, li, x):
                if li == 0:
                    pe.wait_ge(x_upd, 2 * pr + x + 1)
                else:
                    pe.wait_ge(t_copy, 4 * pr + 3 + x)
                    pe.wait_ge(y_upd, 4 * pr + x + 1)
                heads(2 + x, lambda h: Tm[:, x, h], lambda h: Y(pr, x)[:, h], wt_mm)

            def ks_step(pr, x):
                c, tok = toks(pr, x)
                pe.wait_ge(s_upd, 2 * pr - 1 + x) if pr else pe.wait_ge(s_zero, 1)
                heads(6 + x, lambda h: kT[:, h, tok], lambda h: St[:, x, h], ks_mm)

            def v_step(pr, x):
                pe.wait_ge(y_upd, 4 * pr + 3 + x)
                pe.wait_ge(r_done, 2 * pr + x + 1)
                heads(6 + x, lambda h: Y(pr, x)[:, h], lambda h: rhs[:, x, h], v_mm)

            def s_step(pr, x):
                c, tok = toks(pr, x)
                pe.wait_ge(vs_done, 2 * pr + x + 1)
                heads(6 + x, lambda h: ktok[:, c, h], lambda h: vs[:, x, h], s_mm)

            def o_step(pr, x):
                it = 2 * pr + x
                pe.wait_ge(qd_done, it + 1)
                pe.wait_ge(vn_done, it + 1)
                if pr:
                    pe.wait_ge(o_acc, it - 1)
                for h in range(HD):
                    mm(ps[:, 4 + x, h * P:(h + 1) * P], St[:, x, h], qd[:, pr % 2, x, h], start=True, stop=False)
                    last = mm(ps[:, 4 + x, h * P:(h + 1) * P], vn[:, x, h], Pm[:, pr % 2, x, h], start=False, stop=True)
                last.then_inc(o_mm, 1)

            both = (0, 1)
            for pr in range(TT + 1):
                sc, iv = pr - 1, pr < TT
                if pr == 0:
                    pe.wait_ge(zg_done, 1)
                    pe.wait_ge(col_dve, 6)
                if iv:
                    for x in both:
                        grow(pr, x)
                    if pr == 0:
                        pe.wait_ge(zg_done, 2)
                    for x in both:
                        kk(pr, x)
                if pr == 1:
                    pe.wait_ge(gm_done, 2)
                if sc >= 0:
                    for x in both:
                        ks_step(sc, x)
                if iv:
                    for x in both:
                        transpose_blocks(pr, x)
                if sc >= 0:
                    for x in both:
                        v_step(sc, x)
                if iv:
                    for x in both:
                        kq(pr, x)
                    for x in both:
                        t_step(pr, 0, x)
                if 0 <= sc < TT - 1:
                    for x in both:
                        s_step(sc, x)
                if iv:
                    for x in both:
                        w_step(pr, x)
                if pr == 1:
                    pe.wait_ge(gm_done, 4)
                if sc >= 0:
                    for x in both:
                        o_step(sc, x)
                if iv:
                    for x in both:
                        wt_step(pr, 0, x)
                    for x in both:
                        t_step(pr, 1, x)
                    for x in both:
                        wt_step(pr, 1, x)
                if pr == 0:
                    spatial()
            def out_part(s, k0, k1):
                n = WOUT + s
                pe.wait_ge(lo_done, n + 1)
                for k in range(k0, k1):
                    pe.wait_ge(y_ready, k + 1)
                    for f in range(2):
                        last = three(ps[:, BANK[2 * s + f], :], wcol(whi, n)[:, k, f * P:(f + 1) * P], wcol(wlo, n)[:, k, f * P:(f + 1) * P],
                                     xhi[:, k, :], xlo[:, k, :], k == 0, k == KT - 1)
                    if s == 3 and k < KT - 1:
                        last.then_inc(y_used, 1)
                if k1 == KT:
                    last.then_inc(w_done, 1)

            pe.wait_ge(vn_done, 8)
            out_part(1, 0, 4)
            for h in range(HD):
                pe.wait_ge(osq, h + 1)
                for c in range(TT):
                    last = mm(ps[:, 0, h * 4 + c:h * 4 + c + 1], tmp[:, h, c * P:(c + 1) * P], ones[:, 0:1], start=True, stop=True)
            last.then_inc(ost, 1)
            pe.wait_ge(o_acc, 8)
            out_part(0, 0, 4)
            pe.wait_ge(oscale, 1)
            for h in range(HD):
                for c in range(TT):
                    last = mm(ps[:, h, c * P:(c + 1) * P], misc[:, h * 4 + c:h * 4 + c + 1].broadcast_to([P, P]), ident[:], start=True, stop=True)
                last.then_inc(orow, 1)
            out_part(0, 4, KT)
            out_part(1, 4, KT)
            pe.wait_ge(y_step, 8)
            out_part(2, 0, KT)
            out_part(3, 0, KT)
            ffn(1, F2)

            pe.wait_ge(pt_lo, 1)
            pe.wait_ge(lo_done, PROJ + 1)
            for o in range(KT):
                pe.wait_ge(h_done, 16 + o + 1)
                for kk in range(2):
                    last = three(ps[:, BANK[o], :], wrow(whi, PROJ, D)[:, kk, o * P:(o + 1) * P], wrow(wlo, PROJ, D)[:, kk, o * P:(o + 1) * P],
                                 pThi[:, kk, :], pTlo[:, kk, :], kk == 0, kk == 1)
                last.then_inc(e_mm if o < KT - 1 else w_done, 1)

            def gate_sums():
                pe.wait_ge(e_sq, 8)
                norm_stats(3, bank=0)

            def gate_rows():
                norm_bcast(3, bank=1)

            def e_sums():
                pe.wait_ge(e_acc, 7)
                for t in range(TT):
                    last = mm(ps[:, 2, t:t + 1], pTf[:, 0, t * P:(t + 1) * P], ones[:, 0:1], start=True, stop=True)
                last.then_inc(e_stats, 1)

            def e_rows():
                pe.wait_ge(e_rstd, 1)
                row_bcast(3, rstd[:, 4:8], TT, e_rb)

            for s in range(4):
                n = GATE + s
                pe.wait_ge(lo_done, n + 1)
                if s < 2:
                    pe.wait_ge(e_sq, 2 * s + 2)
                elif s == 2:
                    pe.wait_ge(rr_done, 4)
                else:
                    pe.wait_ge(en_done, 8)
                if s < 3:
                    col_slot(n, BANK[2 * s], BANK[2 * s + 1], xw=24 if s == 0 else None,
                             before=({6: gate_sums}, {0: e_sums, 3: gate_rows, 6: e_rows}, {})[s])
            for f in range(2):
                if f:
                    pe.wait_ge(hf_done, 4)
                    for t in range(TT):
                        for k in range(4):
                            last = nc.tensor.transpose(ps[:, 4 + t, k * P:(k + 1) * P], hT[:, k, t * P:(t + 1) * P], ident[:])
                    last.then_inc(f_first, 1)
                for k in range(KT):
                    last = three(ps[:, 2 + f, :], wcol(whi, n)[:, k, f * P:(f + 1) * P], wcol(wlo, n)[:, k, f * P:(f + 1) * P],
                                 xhi[:, k, :], xlo[:, k, :], k == 0, k == KT - 1)
                last.then_inc(g_six if f == 0 else w_done, 1)
            for k in range(4, KT):
                pe.wait_ge(hf_done, k + 1)
                pe.wait_ge(gs_scaled, 8)
                for t in range(TT):
                    last = nc.tensor.transpose(ps[:, t, (k - 4) * P:(k - 3) * P], hT[:, k, t * P:(t + 1) * P], ident[:])
                    if k == KT - 1:
                        last.then_inc(f_tr, 1)

        @block.scalar
        def _(act):
            A = nc.scalar.activation

            def hi(n, p, cnt=None):
                act.wait_ge(raw_in[p], cnt if cnt is not None else 16 * (n // 2 + 1))
                if not isinstance(n, int) or n >= 2:
                    act.wait_ge(w_done, n - 1)
                A(whi[p][:], raw[p][:], ACT.Copy).then_inc(hi_done, 1)

            def norm_std(ni, bank=BANK[0]):
                if ni:
                    act.wait_ge(stats_done, ni)
                    A(std[:, 0:4], ps[:, bank, 0:4], ACT.Sqrt, bias=eps[:], scale=1.0 / D).then_inc(std_done, 1)
                else:
                    act.wait_ge(ss0_done, TT)
                    A(std[:, 0:4], ss[:, 0:4], ACT.Sqrt, bias=eps[:], scale=1.0 / D).then_inc(std_done, 1)

            def rows_copy(ni, bank=BANK[1]):
                act.wait_ge(rb_done, ni + 1)
                A(rrow[:], ps[:, bank, :], ACT.Copy).then_inc(rr_done, 1)

            def squares(og, g0=None):
                for o in range(KT):
                    act.wait_ge(h_done, 8 * og + o + 1)
                    if g0 is not None:
                        if og == 1:
                            act.wait_ge(y_used, o + 1) if o < KT - 1 else act.wait_ge(w_done, WOUT + 4)
                        A(xhi[:, o, :], hT[:, o, :], ACT.Copy, scale=cols[:, g0 + o:g0 + o + 1]).then_inc(xhi_done, 1)
                    if o >= 4:
                        act.wait_ge(acc_done, 7 * og + max(1, o - 4))
                    A(tmp[:, o % 4, :], hT[:, o, :], ACT.Square).then_inc(sq_done, 1)

            def ffn(u, n0):
                def pair(i):
                    hi(i * 2 + n0 + 2, n0 % 2, cnt=i * 16 + 16 * (n0 // 2 + 2))
                    act.wait_ge(gr_done, i + (u * FP + 1))
                    A(tmp[:, 0:2, :], tmp[:, 0:2, :], ACT.Silu).then_inc(silu_done, 1)
                    hi(i * 2 + n0 + 3, (n0 + 1) % 2, cnt=i * 16 + 16 * ((n0 + 3) // 2 + 1))
                    act.wait_ge(gu_done, i + (u * FP + 1))
                    A(guhi[:, bass.ds(i * 2, 2), :], tmp[:, 2:4, :], ACT.Copy).then_inc(guhi_done, 1)

                if u:
                    norm_std(2)
                rows_copy(2 * u)
                pair(0)
                with act.Fori(1, FP) as i:
                    pair(i)
                n1 = n0 + 2 * FP
                for jj in range(2, FP):
                    hi(n1 + jj, (n1 + jj) % 2)

            def token_square(t):
                act.wait_ge(x_in[t], 16)
                act.wait_ge(ss0_done, t) if t else act.wait_ge(const_done, 1)
                A(sqjunk[:], xtok[:, t, :], ACT.Square, accum_out=ss[:, t:t + 1]).then_inc(ss0_done, 1)

            def x_hi(k):
                act.wait_ge(hx_act, min(k // 2 + 1, 4)) if k % 2 == 0 else act.wait_ge(hx_dve, k // 2 + 1)
                A(xhi[:, k, :], hT[:, k, :], ACT.Copy, scale=cols[:, G_FFN1 + k:G_FFN1 + k + 1]).then_inc(xhi_done, 1)

            act.wait_ge(g1_tr, 1)
            A(cols[:, 0:8], ps[:, 0, 0:8], ACT.Copy).then_inc(g1_done, 1)
            token_square(0)
            token_square(1)
            token_square(2)
            hi(F1, F1 % 2)
            act.wait_ge(xtr_done, 1)
            act.wait_ge(g1_done, 1)
            A(hT[:, 0, :], ps[:, 0, :], ACT.Copy).then_inc(hx_act, 1)
            x_hi(0)
            for k in range(2, KT, 2):
                A(hT[:, k, :], ps[:, k, :], ACT.Copy).then_inc(hx_act, 1)
            for k in range(1, KT):
                x_hi(k)
            token_square(3)
            norm_std(0)
            hi(F1 + 1, (F1 + 1) % 2)
            act.wait_ge(vtr_done, 1)
            A(cols[:, 8:109], ps[:, 4, 0:101], ACT.Copy).then_inc(cols_done, 1)
            act.wait_ge(p_tr, 1)
            A(pTf[:], ps[:, 6:8, :], ACT.Copy).then_inc(p_copy, 1)
            ffn(0, F1)
            hi(WIN, WIN % 2)
            squares(0, G_MIX)

            hi(WIN + 1, (WIN + 1) % 2)
            norm_std(1)
            act.wait_ge(ab_in, 16)
            act.wait_ge(wab_step, 1)
            A(wabhi[:], wab[:], ACT.Copy).then_inc(wab_hi, 1)
            act.wait_ge(ws_tr, 1)
            A(wsT[:], ps[:, 7, :].rearrange("p (h n) -> p h n", h=HD), ACT.Copy).then_inc(ws_done, 1)
            rows_copy(1)

            def ktok_evac(jj):
                act.wait_ge(tok_tr, jj + 1)
                A(ktok[:, :, jj, :], ps[:, 5 + jj % 2, :].rearrange("p (c d) -> p c d", c=TT), ACT.Copy).then_inc(ktok_done, 1)

            def kkd_evac(c):
                act.wait_ge(kkd_mm, c + 1)
                for b in range(NB):
                    A(kkd[b * B:(b + 1) * B, c], ps[b * B:(b + 1) * B, 5 + c % 2, :].rearrange("p (h n) -> p h n", h=HD)[:, :, b * B:(b + 1) * B],
                      ACT.Copy).then_inc(kkd_done, 1)

            for s in range(6):
                for jj in (2 * s, 2 * s + 1):
                    act.wait_ge(z_scaled, jj + 1)
                    if jj >= 2:
                        act.wait_ge(zact_done, jj - 1)
                    A(acc[:, jj % 2, :], ps[:, jj % 4, :], ACT.Copy, scale=cols[:, G_CONV + 24 + ch(jj):G_CONV + 25 + ch(jj)]).then_inc(tap0, 1)
                hi(WIN + s + 2, (WIN + s) % 2)
                for jj in (2 * s, 2 * s + 1):
                    act.wait_ge(conv_done, jj + 1)
                    if jj < 8:
                        z = (kT if jj < 4 else qT)[:, jj % 4, :]
                        A(z, acc[:, jj % 2, :], ACT.Silu).then_inc(zact_done, 1)
                        if jj >= 2:
                            act.wait_ge(qk_stat, jj - 1)
                        act.wait_ge(zact_done, jj + 1)
                        A(mb[:, jj % 2, :], z, ACT.Square).then_inc(zsq_done, 1)
                    else:
                        act.wait_ge(qk_stat, min(jj - 1, 8))
                        if jj >= 10:
                            act.wait_ge(tok_tr, jj - 5)
                        A(mb[:, jj % 2, :], acc[:, jj % 2, :], ACT.Silu).then_inc(zact_done, 1)
                if s in (1, 2):
                    for jj in (2 * s - 2, 2 * s - 1):
                        ktok_evac(jj)
                if s == 3:
                    abv = ps[:, 7, 0:64].rearrange("p (c j) -> p c j", j=16)
                    act.wait_ge(gate_dve, 1)
                    A(ea, aa, ACT.Abs).then_inc(gate_act, 1)
                    act.wait_ge(gate_act, 1)
                    A(ea, ea, ACT.Exp, scale=-1.0).then_inc(gate_act, 1)
                    A(be.rearrange("p (c j) -> p c j", j=8), abv[:, :, 8:16], ACT.Exp, scale=-1.0).then_inc(gate_act, 1)
                    A(bc8[:, 16:24], bc8[:, 8:16], ACT.Exp).then_inc(gate_act, 1)
                    act.wait_ge(gate_act, 2)
                    A(ea, ea, ACT.Ln, bias=1.0).then_inc(gate_act, 1)
                    act.wait_ge(qk_stat, 6)
                    A(nk, ps[:, 4, 0:16], ACT.Sqrt, bias=eps[:]).then_inc(nk_done, 1)
                if s in (3, 4):
                    kkd_evac(2 * s - 6)
                    kkd_evac(2 * s - 5)
                if s == 4:
                    act.wait_ge(cum_done, 1)
                    A(eG, ps[:, 7, 64:96], ACT.Exp)
                    A(egl, ps[:, 7, 96:128], ACT.Exp).then_inc(col_act, 1)
                    act.wait_ge(col_dve, 2)
                    A(egd, egd, ACT.Exp).then_inc(col_act, 1)
                if s == 5:
                    act.wait_ge(gs_tr, 1)
                    A(gsT[:], ps[0:32, 7, 128:384].rearrange("p (a n) -> p a n", a=2), ACT.Copy).then_inc(gs_done, 1)
                    act.wait_ge(gs_done, 1)
                    for d in range(2):
                        for b in range(NB):
                            act.dma_start(gsi[own(d, b)], gsT[16 * d:16 * d + 16, :, b * B:(b + 1) * B]).then_inc(gin_in, 16)
            hi(WIN + 8, (WIN + 8) % 2)
            act.wait_ge(zi_dve, 3)
            A(Ei[:], Ei[:], ACT.Exp).then_inc(zi_exp, 1)
            act.wait_ge(kk_stored, 16)
            act.wait_ge(gin_in, 8 * 16)
            act.wait_ge(pair_scaled, 1)
            A(uT[:, 0:2, :], ps[:, 0:2, :], ACT.Gelu_apprx_tanh).then_inc(ugelu, 1)
            hi(WIN + 9, (WIN + 9) % 2)
            act.wait_ge(pair_scaled, 2)
            A(uT[:, 2:4, :], ps[:, 2:4, :], ACT.Gelu_apprx_tanh).then_inc(ugelu, 1)
            hi(WIN + 10, (WIN + 10) % 2)
            act.wait_ge(w_done, WIN + 10)
            act.wait_ge(tok_tr, 8)
            hi(WIN + 11, (WIN + 11) % 2)
            for t in range(TT):
                A(vg[:, t, :], ps[:, 4 + t, :], ACT.Gelu_apprx_tanh, scale=rstd[:, t:t + 1]).then_inc(vgelu, 1)
            hi(WOUT, WOUT % 2)
            act.wait_ge(xi_done, 1)
            act.wait_ge(pair_scaled, 3)
            A(zg[:, 0:2, :], ps[:, 0:2, :], ACT.Silu).then_inc(zg_done, 1)
            act.wait_ge(pair_scaled, 4)
            A(zg[:, 2:4, :], ps[:, 2:4, :], ACT.Silu).then_inc(zg_done, 1)
            act.wait_ge(ln_step, 17)
            A(lsd[:], mv[:, :, 1], ACT.Sqrt, bias=eps[:]).then_inc(ln_sd, 1)

            def ps4(b):
                return ps[:, b, :].rearrange("p (h n) -> p h n", h=HD)

            def decays(pr):
                for x in range(2):
                    it = 2 * pr + x
                    act.wait_ge(dpre_done, it + 1)
                    if pr:
                        act.wait_ge(qd_done, it - 1)
                    A(Em[:, x], ps4(x), ACT.Exp).then_inc(em_done, 1)
                    A(Dm[:, x], Dm[:, x], ACT.Exp).then_inc(dm_done, 1)

            def others(pr):
                for x in range(2):
                    act.wait_ge(o_tr, 2 * pr + x + 1)
                    A(Om[:, pr % 2, x], ps4(x), ACT.Copy).then_inc(o_init, 1)

            def t_evac(pr, li):
                for x in range(2):
                    tn = 4 * pr + 2 * li + x
                    act.wait_ge(t_mm, tn + 1)
                    if tn >= 2:
                        act.wait_ge(wt_mm, tn - 1)
                    A(Tm[:, x], ps4(x), ACT.Copy).then_inc(t_copy, 1)

            def v_evac(pr):
                for x in range(2):
                    c, it = (pr, TT - 1 - pr)[x], 2 * pr + x
                    act.wait_ge(v_mm, it + 1)
                    if pr:
                        act.wait_ge(o_mm, it - 1)
                    for h in range(HD):
                        col = x * 16 + c * 4 + h
                        last = A(vn[:, x, h], ps[:, 6 + x, h * P:(h + 1) * P], ACT.Copy, scale=sk[:, col:col + 1])
                    last.then_inc(vn_done, 1)

            for pr in range(TT + 1):
                if pr < TT:
                    decays(pr)
                    if pr == 0:
                        hi(WOUT + 1, (WOUT + 1) % 2)
                    others(pr)
                if pr:
                    v_evac(pr - 1)
                if pr < TT:
                    t_evac(pr, 0)
                    t_evac(pr, 1)
                if pr == TT - 1:
                    act.wait_ge(o_mm, 6)
                    for h in (0, 1):
                        A(xhi[:, h, :], uT[:, h, :], ACT.Copy).then_inc(yhi_done, 1)
            act.wait_ge(o_mm, 8)
            for h in (2, 3):
                A(xhi[:, h, :], uT[:, h, :], ACT.Copy).then_inc(yhi_done, 1)
            for h in range(HD):
                act.wait_ge(o_acc, 8)
                A(tmp[:, h, :], oT[:, h, :], ACT.Square).then_inc(osq, 1)
            act.wait_ge(ost, 1)
            act.wait_ge(osd, 1)
            A(misc[:, 0:16], misc[:, 0:16], ACT.Sqrt).then_inc(osd, 1)
            for h in range(HD):
                act.wait_ge(y_step, HD + h + 1)
                A(xhi[:, 4 + h, :], oT[:, h, :], ACT.Copy).then_inc(yhi_done, 1)
            hi(WOUT + 2, WOUT % 2)
            hi(WOUT + 3, (WOUT + 1) % 2)
            hi(F2, F2 % 2)
            squares(1, G_FFN2)
            hi(F2 + 1, (F2 + 1) % 2)
            ffn(1, F2)
            act.wait_ge(p_copy, 1)
            act.wait_ge(w_done, PROJ - 2)
            A(pThi[:], pTf[:], ACT.Copy).then_inc(pt_hi, 1)
            hi(PROJ, PROJ % 2)
            squares(2, G_GATE)
            hi(GATE, GATE % 2)
            for o in range(KT):
                act.wait_ge(e_mm, o + 1) if o < KT - 1 else act.wait_ge(w_done, PROJ + 1)
                A(eT[:, o, :], ps[:, BANK[o], :], ACT.Copy)
                if o < 4:
                    act.wait_ge(acc_done, 18 + o)
                else:
                    act.wait_ge(e_acc, max(1, o - 4))
                A(tmp[:, o % 4, :], ps[:, BANK[o], :], ACT.Square).then_inc(e_sq, 1)
            hi(GATE + 1, (GATE + 1) % 2)
            norm_std(3, bank=0)
            act.wait_ge(e_stats, 1)
            A(std[:, 4:8], ps[:, 2, 0:4], ACT.Sqrt, bias=eps[:], scale=1.0 / D).then_inc(e_std, 1)
            rows_copy(3, bank=1)
            hi(GATE + 2, GATE % 2)
            def scale_first(t):
                act.wait_ge(f_rstd, t + 1)
                A(otile[:, t, 0:T], otile[:, t, 0:T], ACT.Copy, scale=rstd[:, t:t + 1]).then_inc(f_out, 1)

            for o in range(KT):
                if o == 2:
                    hi(GATE + 3, (GATE + 1) % 2)
                if o == KT - 1:
                    act.wait_ge(f_first, 1)
                    for t in range(TT):
                        act.wait_ge(f_mul, t + 1)
                        A(fjunk[:, t, :], ps[:, 4 + t, :], ACT.Square, accum_out=ss[:, t:t + 1]).then_inc(f_ss, 1)
                act.wait_ge(gs_scaled, o + 1)
                A(sgm[:, o % 2, :], sgm[:, o % 2, :], ACT.Sigmoid, bias=cols[:, B_GATE + o:B_GATE + o + 1]).then_inc(sg_done, 1)
            act.wait_ge(f_bias, 1)
            A(std[:, 4:8], fb[:], ACT.Sqrt)
            for t in range(TT):
                act.wait_ge(f_tr, t + 1)
                A(fjunk[:, t, :], ps[:, t, :], ACT.Square, accum_out=ss[:, 4 + t:5 + t]).then_inc(f_ss, 1)
                act.wait_ge(f_ss, TT + t + 1)
                A(std[:, t:t + 1], ss[:, 4 + t:5 + t], ACT.Sqrt, bias=fb[:, t:t + 1], scale=1.0 / D).then_inc(f_std, 1)
                if t:
                    scale_first(t - 1)
            scale_first(TT - 1)

        @block.vector
        def _(dve):
            V = nc.vector
            stt = nc.vector.scalar_tensor_tensor

            def lo(n, p):
                dve.wait_ge(hi_done, n + 1)
                V.tensor_tensor(out=wlo[p][:], in0=raw[p][:], in1=whi[p][:].bitcast(f32), op=ALU.subtract).then_inc(lo_done, 1)

            def residual(og, n_last, factor, g0=None):
                for o in range(KT + 1):
                    if o < KT:
                        if og == 1:
                            dve.wait_ge(w_done, WOUT + o // 2 + 1)
                        elif o < KT - 1:
                            dve.wait_ge(out_done, 7 * (og // 2) + o + 1)
                        else:
                            dve.wait_ge(w_done, n_last + 1)
                        stt(out=hT[:, o, :], in0=ps[:, BANK[o], :], scalar=factor, in1=hT[:, o, :], op0=ALU.mult, op1=ALU.add).then_inc(h_done, 1)
                    if og != 1 and o == 3:
                        lo(n_last + 1, (n_last + 1) % 2)
                    if og == 1 and o in (1, 3):
                        lo(WOUT + 3 + o // 2, (WOUT + 3 + o // 2) % 2)
                    if g0 is not None and 0 <= o - 1 < KT:
                        x_lo(8 * og + 8, o - 1, g0)

            def x_lo(base, k, g0):
                dve.wait_ge(xhi_done, base + k + 1)
                stt(out=xlo[:, k, :], in0=hT[:, k, :], scalar=cols[:, g0 + k:g0 + k + 1], in1=xhi[:, k, :].bitcast(f32),
                    op0=ALU.mult, op1=ALU.subtract).then_inc(x_ready, 1)

            def row_scale(ni):
                dve.wait_ge(std_done, ni + 1)
                V.reciprocal(rstd[:, 0:4], std[:, 0:4]).then_inc(rstd_done, 1)

            def ffn(u, n0):
                r2 = rrow[:].unsqueeze(1).broadcast_to([P, 2, T])

                def pair(i):
                    dve.wait_ge(w_done, i * 2 + (n0 + 1))
                    V.tensor_tensor(out=tmp[:, 0:2, :], in0=ps[:, 0:2, :], in1=r2, op=ALU.mult).then_inc(gr_done, 1)
                    lo(i * 2 + (n0 + 2), n0 % 2)
                    dve.wait_ge(w_done, i * 2 + (n0 + 2))
                    if not isinstance(i, int):
                        dve.wait_ge(gulo_done, i + u * FP)
                    V.tensor_tensor(out=tmp[:, 2:4, :], in0=ps[:, 2:4, :], in1=r2, op=ALU.mult).then_inc(ur_done, 1)
                    dve.wait_ge(silu_done, i + (u * FP + 1))
                    dve.wait_ge(ur_done, i + (u * FP + 1))
                    V.tensor_tensor(out=tmp[:, 2:4, :], in0=tmp[:, 2:4, :], in1=tmp[:, 0:2, :], op=ALU.mult).then_inc(gu_done, 1)
                    lo(i * 2 + (n0 + 3), (n0 + 1) % 2)
                    dve.wait_ge(guhi_done, i + (u * FP + 1))
                    V.tensor_tensor(out=gulo[:, bass.ds(i * 2, 2), :], in0=tmp[:, 2:4, :],
                                    in1=guhi[:, bass.ds(i * 2, 2), :].bitcast(f32), op=ALU.subtract).then_inc(gulo_done, 1)

                row_scale(2 * u)
                dve.wait_ge(rr_done, 2 * u + 1)
                pair(0)
                with dve.Fori(1, FP) as i:
                    pair(i)
                n1 = n0 + 2 * FP
                for jj in range(2, FP):
                    lo(n1 + jj, (n1 + jj) % 2)

            dve.wait_ge(xtr_done, 1)
            def copy_x(k):
                V.tensor_copy(hT[:, k, :], ps[:, k, :]).then_inc(hx_dve, 1)

            copy_x(1)
            lo(F1, F1 % 2)
            x_lo(0, 0, G_FFN1)
            for k in (3, 5, 7):
                copy_x(k)
                x_lo(0, k // 2, G_FFN1)
            for k in range(4, KT):
                x_lo(0, k, G_FFN1)
            lo(F1 + 1, (F1 + 1) % 2)
            ffn(0, F1)
            dve.wait_ge(cols_done, 1)
            residual(0, WIN - 1, 0.5, G_MIX)

            V.memset(wab[:, 128:240], 0.0).then_inc(wab_step, 1)
            lo(WIN + 1, (WIN + 1) % 2)
            row_scale(1)
            dve.wait_ge(wab_hi, 1)
            V.tensor_tensor(out=wablo[:], in0=wab[:], in1=wabhi[:].bitcast(f32), op=ALU.subtract).then_inc(wab_step, 1)
            dve.wait_ge(rr_done, 2)
            taps = [0]

            def z_scale(jj):
                dve.wait_ge(w_done, WIN + jj // 2 + 1)
                V.tensor_tensor(out=ps[:, jj % 4, :], in0=ps[:, jj % 4, :], in1=rrow[:], op=ALU.mult).then_inc(z_scaled, 1)

            def pair_scale(b, n, done):
                dve.wait_ge(w_done, n + 1)
                V.tensor_tensor(out=ps[:, b:b + 2, :], in0=ps[:, b:b + 2, :], in1=rrow[:].unsqueeze(1).broadcast_to([P, 2, T]),
                                op=ALU.mult).then_inc(done, 1)

            def conv(jj):
                z, a = ps[:, jj % 4, :], acc[:, jj % 2, :]
                dve.wait_ge(tap0, jj + 1)
                for j in (0, 1, 3, 4):
                    if j:
                        taps[0] += 1
                        dve.wait_ge(conv_tap, taps[0])
                    d = j - 2
                    w = cols[:, G_CONV + j * 12 + ch(jj):G_CONV + j * 12 + ch(jj) + 1]
                    dst = a[:, max(0, -d):T - max(0, d)]
                    last = stt(out=dst, in0=z[:, max(0, d):T - max(0, -d)], scalar=w, in1=dst, op0=ALU.mult, op1=ALU.add)
                    last.then_inc(conv_done if j == 4 else conv_tap, 1)

            def nkv_evac(jj):
                dve.wait_ge(tok_tr, jj - 3)
                V.tensor_tensor(out=nkv[:, :, jj - 8, :], in0=ps[:, 5 + jj % 2, :].rearrange("p (c d) -> p c d", c=TT),
                                in1=nk[:, (jj - 8) * 4:(jj - 7) * 4].unsqueeze(2).broadcast_to([P, TT, P]), op=ALU.mult).then_inc(nkv_done, 1)

            for s in range(6):
                z_scale(2 * s)
                z_scale(2 * s + 1)
                conv(2 * s)
                lo(WIN + s + 2, (WIN + s) % 2)
                conv(2 * s + 1)
                if s == 1:
                    dve.wait_ge(ab_mm, 1)
                    V.tensor_tensor(out=abT[:], in0=ps[0:16, 7, :], in1=rrow[0:16, :], op=ALU.mult).then_inc(ab_scaled, 1)
                if s == 3:
                    abv = ps[:, 7, 0:64].rearrange("p (c j) -> p c j", j=16)
                    dve.wait_ge(gate_act, 5)
                    stt(out=aa, in0=aa, scalar=0.0, in1=ea, op0=ALU.max, op1=ALU.add).then_inc(gate_dve, 1)
                    V.tensor_scalar(s2, be, 1.0, None, ALU.add).then_inc(gate_dve, 1)
                    dve.wait_ge(gate_dve, 3)
                    V.reciprocal(be, s2).then_inc(gate_dve, 1)
                    for d in range(2):
                        last = stt(out=gg[:, 16 * d:16 * d + 16].rearrange("p (c h) -> p c h", c=TT),
                                   in0=aa.rearrange("p (c j) -> p c j", c=TT)[:, :, 4 * d:4 * d + 4], scalar=-1.0,
                                   in1=bc8[:, 16 + 4 * d:20 + 4 * d].unsqueeze(1).broadcast_to([P, TT, HD]), op0=ALU.mult, op1=ALU.mult)
                    last.then_inc(gate_dve, 1)
                    dve.wait_ge(nk_done, 1)
                    V.reciprocal(rk2, nk).then_inc(rk_step, 1)
                    dve.wait_ge(rk_step, 1)
                    V.tensor_tensor(out=rk2, in0=rk2, in1=rk2, op=ALU.mult).then_inc(rk_step, 1)
                if s == 2:
                    abv = ps[:, 7, 0:64].rearrange("p (c j) -> p c j", j=16)
                    dve.wait_ge(ab_tr, 1)
                    dve.wait_ge(bc_in, 80)
                    V.tensor_tensor(out=aa.rearrange("p (c j) -> p c j", j=8), in0=abv[:, :, 0:8],
                                    in1=bc8[:, 0:8].unsqueeze(1).broadcast_to([P, TT, 8]), op=ALU.add).then_inc(gate_dve, 1)
                if s == 4:
                    dve.wait_ge(cum_done, 1)
                    dve.wait_ge(col_act, 1)
                    V.tensor_copy(Gc, ps[:, 7, 64:96]).then_inc(col_dve, 1)
                    dve.wait_ge(col_dve, 1)
                    V.tensor_tensor(out=egd, in0=ps[:, 7, 96:128], in1=Gc, op=ALU.subtract).then_inc(col_dve, 1)
                    V.tensor_scalar(neG, eG, -1.0, None, ALU.mult).then_inc(col_dve, 1)
                    dve.wait_ge(rk_step, 2)
                    for d in range(2):
                        last = V.tensor_tensor(out=sk[:, 16 * d:16 * d + 16].rearrange("p (c h) -> p c h", c=TT),
                                               in0=be.rearrange("p (c j) -> p c j", c=TT)[:, :, 4 * d:4 * d + 4],
                                               in1=rk2.rearrange("p (h c) -> p c h", c=TT), op=ALU.mult)
                    last.then_inc(col_dve, 1)
                    dve.wait_ge(col_dve, 4)
                    V.tensor_scalar(nsk, sk, -1.0, None, ALU.mult).then_inc(col_dve, 1)
                    dve.wait_ge(col_act, 2)
                    V.tensor_tensor(out=s2, in0=sk, in1=egd, op=ALU.mult).then_inc(col_dve, 1)
                    dve.wait_ge(qk_stat, 8)
                    V.tensor_scalar(misc[:, 16:32], ps[:, 4, 16:32], EPS, float(P), ALU.add, ALU.mult).then_inc(rk_step, 1)
                if s == 5:
                    nkv_evac(8)
                    nkv_evac(9)
            lo(WIN + 8, (WIN + 8) % 2)
            pair_scale(0, WIN + 6, pair_scaled)
            nkv_evac(10)
            nkv_evac(11)
            dve.wait_ge(gin_in, 8 * 16)
            V.tensor_scalar(gi, gi, sgn[:], None, ALU.mult).then_inc(zi_dve, 1)
            dve.wait_ge(zi_dve, 1)
            row = lambda a: a.unsqueeze(2).broadcast_to([P, B, B])
            col = lambda a: a.unsqueeze(1).broadcast_to([P, B, B])
            V.tensor_tensor(out=Ei[:], in0=row(gi), in1=col(gi), op=ALU.subtract).then_inc(zi_dve, 1)
            dve.wait_ge(zi_dve, 2)
            V.tensor_scalar(Ei[:], Ei[:], 0.0, None, ALU.min).then_inc(zi_dve, 1)
            dve.wait_ge(kin_in, 8 * 16)
            V.tensor_tensor(out=Zi[0:64], in0=Zi[0:64], in1=col(si)[0:64], op=ALU.mult)
            V.tensor_tensor(out=Zi[64:P], in0=Zi[64:P], in1=row(si)[64:P], op=ALU.mult).then_inc(zi_dve, 1)
            V.memset(Xi[:], 0.0).then_inc(zi_dve, 1)
            dve.wait_ge(zi_dve, 5)
            V.memset(Xi[:].rearrange("p r c -> p (r c)")[:, 0:B * B:B + 1], 1.0).then_inc(zi_dve, 1)
            dve.wait_ge(zi_exp, 1)
            V.tensor_tensor(out=Zi[:], in0=Zi[:], in1=Ei[:], op=ALU.mult).then_inc(zi_dve, 1)
            dve.wait_ge(zi_dve, 7)

            def substitute(m0, m1):
                for m in range(m0, m1):
                    nr, ncol = B - 1 - m, m + 1
                    if m:
                        dve.wait_ge(xi_step, 2 * m)
                    w = prod[:, 0:nr * ncol].rearrange("p (r c) -> p r c", r=nr)
                    V.tensor_tensor(out=w, in0=Zi[:, m + 1:B, m:m + 1].broadcast_to([P, nr, ncol]),
                                    in1=Xi[:, m:m + 1, 0:ncol].broadcast_to([P, nr, ncol]), op=ALU.mult).then_inc(xi_step, 1)
                    dve.wait_ge(xi_step, 2 * m + 1)
                    V.tensor_tensor(out=Xi[:, m + 1:B, 0:ncol], in0=Xi[:, m + 1:B, 0:ncol], in1=w, op=ALU.add).then_inc(
                        xi_step if m < B - 2 else xi_done, 1)

            lo(WIN + 9, (WIN + 9) % 2)
            pair_scale(2, WIN + 7, pair_scaled)
            substitute(0, 10)
            lo(WIN + 10, (WIN + 10) % 2)
            substitute(10, 22)
            lo(WIN + 11, (WIN + 11) % 2)
            substitute(22, B - 1)
            pair_scale(0, WIN + 10, pair_scaled)
            dve.wait_ge(vgelu, 4)
            for t in range(TT):
                for h in range(HD):
                    V.bn_stats(bns[:, t * 4 + h, :], vg[:, t, h * P:(h + 1) * P]).then_inc(ln_step, 1)
            pair_scale(2, WIN + 11, pair_scaled)
            dve.wait_ge(ln_step, 16)
            for q in range(16):
                last = V.bn_aggr(mv[:, q, :], bns[:, q, :])
            last.then_inc(ln_step, 1)
            dve.wait_ge(ln_sd, 1)
            V.reciprocal(lrs[:], lsd[:]).then_inc(ln_step, 1)

            def center(q0, q1):
                dve.wait_ge(ln_step, 18)
                for q in range(q0, q1):
                    t, h = divmod(q, HD)
                    V.tensor_scalar(vg[:, t, h * P:(h + 1) * P], vg[:, t, h * P:(h + 1) * P], mv[:, q, 0:1], lrs[:, q:q + 1],
                                    ALU.subtract, ALU.mult).then_inc(ln_step, 1)

            def gmlp_out(h):
                i = (h + 2) % 4
                dve.wait_ge(sv_done, i + 1)
                if i >= 2:
                    dve.wait_ge(gm_done, i - 1)
                V.tensor_tensor(out=svb[:, h % 2, :].rearrange("p (c i) -> p c i", c=TT), in0=ps[:, 4 + h, :].rearrange("p (c i) -> p c i", c=TT),
                                in1=bsb[:, h * P:(h + 1) * P].unsqueeze(1).broadcast_to([P, TT, P]), op=ALU.add).then_inc(gm_step, 1)
                dve.wait_ge(gm_step, i + 1)
                V.tensor_tensor(out=uT[:, h, :], in0=uT[:, h, :], in1=svb[:, h % 2, :], op=ALU.mult).then_inc(gm_done, 1)

            ps4 = lambda b: ps[:, b, :].rearrange("p (h n) -> p h n", h=HD)
            both = (0, 1)

            def cell(pr, x):
                c = (pr, TT - 1 - pr)[x]
                return c, 2 * pr + x, x * 16 + c * 4

            def init_blocks(pr, x):
                c, it, q = cell(pr, x)
                dve.wait_ge(r_zero, it + 1)
                dve.wait_ge(xb_in, 16 * 2 * NB)
                for b in range(NB):
                    last = V.tensor_copy(Rm[b * B:(b + 1) * B, pr % 2, x, :, b * B:(b + 1) * B], xb[b * B:(b + 1) * B, x, c])
                last.then_inc(r_init, 1)

            def decay_args(pr, x):
                c, it, q = cell(pr, x)
                dve.wait_ge(grow_done, it + 1)
                if pr:
                    dve.wait_ge(pm_done, it - 1)
                for h in range(HD):
                    last = stt(out=Dm[:, x, h], in0=ps[:, x, h * P:(h + 1) * P], scalar=Gc[:, q + h:q + h + 1], in1=negm[:, x, :],
                               op0=ALU.subtract, op1=ALU.add)
                last.then_inc(dpre_done, 1)

            def nt(pr, x):
                c, it, q = cell(pr, x)
                dve.wait_ge(dm_done, it + 1)
                dve.wait_ge(kk_done, it + 1)
                if pr:
                    dve.wait_ge(t_mm, 4 * (pr - 1) + 3 + x)
                for h in range(HD):
                    last = stt(out=NTm[:, x, h], in0=ps[:, 2 + x, h * P:(h + 1) * P], scalar=nsk[:, q + h:q + h + 1], in1=Dm[:, x, h],
                               op0=ALU.mult, op1=ALU.mult)
                last.then_inc(nt_done, 1)

            def p_mul(pr, x):
                c, it, q = cell(pr, x)
                dve.wait_ge(kq_done, it + 1)
                if pr >= 2:
                    dve.wait_ge(o_mm, it - 3)
                V.tensor_tensor(out=Pm[:, pr % 2, x], in0=ps4(2 + x), in1=Dm[:, x], op=ALU.mult).then_inc(pm_done, 1)

            def level_mask(l, d):
                return lev[:, l, d, :].unsqueeze(1).broadcast_to([P, HD, P])

            def x_update(pr, x):
                dve.wait_ge(w_mm, 2 * pr + x + 1)
                V.copy_predicated((Rm, Om)[x][:, pr % 2, x], level_mask(0, x), ps4(2 + x)).then_inc(x_upd, 1)

            def y_update(pr, li, x):
                dve.wait_ge(wt_mm, 4 * pr + 2 * li + x + 1)
                V.copy_predicated((Om, Rm)[x][:, pr % 2, x], level_mask(li, 1 - x), ps4(2 + x)).then_inc(y_upd, 1)

            def r_step(pr, x):
                c, it, q = cell(pr, x)
                dve.wait_ge(ks_mm, it + 1)
                if pr:
                    dve.wait_ge(v_mm, it - 1)
                for h in range(HD):
                    last = stt(out=rhs[:, x, h], in0=ps[:, 6 + x, h * P:(h + 1) * P], scalar=neG[:, q + h:q + h + 1], in1=nkv[:, c, h],
                               op0=ALU.mult, op1=ALU.add)
                last.then_inc(r_done, 1)

            def vs_step(pr, x):
                c, it, q = cell(pr, x)
                dve.wait_ge(vn_done, it + 1)
                if pr:
                    dve.wait_ge(s_mm, it - 1)
                V.tensor_tensor(out=vs[:, x], in0=ps4(6 + x), in1=s2[:, q:q + 4].unsqueeze(2).broadcast_to([P, HD, P]),
                                op=ALU.mult).then_inc(vs_done, 1)

            def o_out(pr, x):
                c, it, q = cell(pr, x)
                dst = oT[:, :, c * P:(c + 1) * P]
                dve.wait_ge(o_mm, it + 1)
                if pr < 2:
                    V.tensor_copy(dst, ps4(4 + x)).then_inc(o_acc, 1)
                else:
                    dve.wait_ge(o_acc, 2 * (TT - 1 - pr) + 2)
                    V.tensor_tensor(out=dst, in0=ps4(4 + x), in1=dst, op=ALU.add).then_inc(o_acc, 1)

            def s_update(pr, x):
                c, it, q = cell(pr, x)
                dve.wait_ge(s_mm, it + 1)
                for h in range(HD):
                    last = stt(out=St[:, x, h], in0=St[:, x, h], scalar=egl[:, q + h:q + h + 1], in1=ps[:, 6 + x, h * P:(h + 1) * P],
                               op0=ALU.mult, op1=ALU.add)
                last.then_inc(s_upd, 1)

            def y_lo(h):
                dve.wait_ge(yhi_done, h + 1)
                V.tensor_tensor(out=xlo[:, h, :], in0=uT[:, h, :], in1=xhi[:, h, :].bitcast(f32), op=ALU.subtract).then_inc(y_ready, 1)

            for pr in range(TT + 1):
                sc, iv = pr - 1, pr < TT
                if iv:
                    for x in both:
                        decay_args(pr, x)
                if sc >= 0:
                    for x in both:
                        r_step(sc, x)
                if iv:
                    if pr == 0:
                        for x in both:
                            init_blocks(0, x)
                    for x in both:
                        nt(pr, x)
                    if pr == 0:
                        center(0, 8)
                if sc >= 0:
                    for x in both:
                        vs_step(sc, x)
                if iv:
                    for x in both:
                        p_mul(pr, x)
                    if pr == 0:
                        center(8, 16)
                        lo(WOUT, WOUT % 2)
                if iv:
                    for x in both:
                        x_update(pr, x)
                if sc == TT - 1:
                    y_lo(0)
                    y_lo(1)
                if sc >= 0:
                    for x in both:
                        o_out(sc, x)
                        if sc < TT - 1:
                            s_update(sc, x)
                if iv:
                    for x in both:
                        y_update(pr, 0, x)
                    if pr < TT - 1:
                        for x in both:
                            init_blocks(pr + 1, x)
                    for x in both:
                        y_update(pr, 1, x)
                    if pr == 0:
                        lo(WOUT + 1, (WOUT + 1) % 2)
                        for h in (2, 3, 0, 1):
                            gmlp_out(h)
            y_lo(2)
            y_lo(3)
            for h in range(HD):
                dve.wait_ge(osq, h + 1)
                V.tensor_tensor(out=oT[:, h, :], in0=oT[:, h, :], in1=zg[:, h, :], op=ALU.mult).then_inc(y_step, 1)
            dve.wait_ge(ost, 1)
            V.tensor_scalar(misc[:, 16:32], misc[:, 16:32], EPS, None, ALU.mult).then_inc(rk_step, 1)
            dve.wait_ge(rk_step, 4)
            stt(out=misc[:, 0:16], in0=ps[:, 0, 0:16], scalar=1.0 / P, in1=misc[:, 16:32], op0=ALU.mult, op1=ALU.add).then_inc(osd, 1)
            dve.wait_ge(osd, 2)
            V.reciprocal(misc[:, 0:16], misc[:, 0:16]).then_inc(oscale, 1)
            for h in range(HD):
                dve.wait_ge(orow, h + 1)
                dve.wait_ge(y_step, HD + h)
                stt(out=oT[:, h, :], in0=oT[:, h, :], scalar=cols[:, G_OUT:G_OUT + 1], in1=ps[:, h, :], op0=ALU.mult, op1=ALU.mult).then_inc(y_step, 1)
                if h:
                    dve.wait_ge(yhi_done, 4 + h)
                    V.tensor_tensor(out=xlo[:, 3 + h, :], in0=oT[:, h - 1, :], in1=xhi[:, 3 + h, :].bitcast(f32), op=ALU.subtract).then_inc(y_ready, 1)
            dve.wait_ge(yhi_done, 8)
            V.tensor_tensor(out=xlo[:, 7, :], in0=oT[:, 3, :], in1=xhi[:, 7, :].bitcast(f32), op=ALU.subtract).then_inc(y_ready, 1)
            lo(WOUT + 2, WOUT % 2)
            residual(1, None, 1.0, G_FFN2)
            lo(F2 + 1, (F2 + 1) % 2)
            ffn(1, F2)
            dve.wait_ge(pt_hi, 1)
            V.tensor_tensor(out=pTlo[:], in0=pTf[:], in1=pThi[:].bitcast(f32), op=ALU.subtract).then_inc(pt_lo, 1)
            residual(2, PROJ - 1, 0.5, G_GATE)
            lo(GATE, GATE % 2)
            esum = pTf[:, 0, :]
            for o in range(1, KT):
                dve.wait_ge(e_sq, o + 1)
                if o == 1:
                    V.tensor_tensor(out=esum, in0=tmp[:, 0, :], in1=tmp[:, 1, :], op=ALU.add).then_inc(e_acc, 1)
                else:
                    dve.wait_ge(e_acc, o - 1)
                    V.tensor_tensor(out=esum, in0=esum, in1=tmp[:, o % 4, :], op=ALU.add).then_inc(e_acc, 1)
            lo(GATE + 1, (GATE + 1) % 2)
            row_scale(3)
            dve.wait_ge(e_std, 1)
            V.reciprocal(rstd[:, 4:8], std[:, 4:8]).then_inc(e_rstd, 1)
            dve.wait_ge(rr_done, 4)

            def gate_scale(o):
                dve.wait_ge(g_six, 1) if o == 6 else dve.wait_ge(w_done, GATE + o // 2 + 1)
                if o >= 2:
                    dve.wait_ge(ge_done, o - 1)
                V.tensor_tensor(out=sgm[:, o % 2, :], in0=ps[:, BANK[o], :], in1=rrow[:], op=ALU.mult).then_inc(gs_scaled, 1)

            gate_scale(0)
            gate_scale(1)
            lo(GATE + 2, GATE % 2)
            dve.wait_ge(e_rb, 1)
            dve.wait_ge(e_sq, 8)
            for o in range(KT):
                stt(out=eT[:, o, :], in0=eT[:, o, :], scalar=cols[:, G_PLE + o:G_PLE + o + 1], in1=ps[:, 3, :], op0=ALU.mult, op1=ALU.mult).then_inc(en_done, 1)
            for o in range(KT):
                dve.wait_ge(sg_done, o + 1)
                dve.wait_ge(en_done, 8)
                V.tensor_tensor(out=eT[:, o, :], in0=eT[:, o, :], in1=sgm[:, o % 2, :], op=ALU.mult).then_inc(ge_done, 1)
                dve.wait_ge(ge_done, o + 1)
                V.tensor_tensor(out=hT[:, o, :], in0=hT[:, o, :], in1=eT[:, o, :], op=ALU.add).then_inc(hf_done, 1)
                if o in (1, 3):
                    gate_scale(o + 1)
                    gate_scale(o + 2)
                if o == 1:
                    lo(GATE + 3, (GATE + 1) % 2)
                if o == 5:
                    gate_scale(6)
                    dve.wait_ge(f_in, 16)
                    dve.wait_ge(f_first, 1)
                    for t in range(TT):
                        V.tensor_tensor(out=otile[:, t, 0:T], in0=ps[:, 4 + t, :], in1=fbc[:, 0:T], op=ALU.mult).then_inc(f_mul, 1)
                if o == 6:
                    dve.wait_ge(f_ss, TT)
                    V.tensor_scalar(fb[:], ss[:, 0:4], 1.0 / D, EPS, ALU.mult, ALU.add).then_inc(f_bias, 1)
                    gate_scale(7)
            for t in range(TT):
                dve.wait_ge(f_std, t + 1)
                V.reciprocal(rstd[:, t:t + 1], std[:, t:t + 1]).then_inc(f_rstd, 1)
                dve.wait_ge(f_rstd, t + 1)
                stt(out=otile[:, t, T:D], in0=ps[:, t, :], scalar=rstd[:, t:t + 1], in1=fbc[:, T:D], op0=ALU.mult, op1=ALU.mult).then_inc(f_half, 1)


_INS = ["x", "p", "ffn1_norm", "ffn1_w_gate", "ffn1_w_up", "ffn1_w_down", "mix_norm", "w_in", "gm_ln_g", "gm_ln_b", "gm_ws",
        "gm_bs", "dn_conv_w", "dn_a_log", "dn_dt_bias", "dn_out_norm", "w_out", "ffn2_norm", "ffn2_w_gate", "ffn2_w_up",
        "ffn2_w_down", "ple_proj", "ple_norm", "ple_gate_norm", "ple_gate_w", "ple_gate_b", "final_norm"]


def kernel(**inputs):
    import numpy as np
    import concourse.bacc as bacc
    from concourse.bass_utils import run_bass_kernel_spmd as run

    nc = bacc.Bacc("TRN2", target_bir_lowering=False, num_devices=1)
    arrays, io = {}, {}
    for name in _INS:
        a = np.ascontiguousarray(inputs[name])
        arrays[f"in_{name}"] = a
        io[name] = nc.dram_tensor(f"in_{name}", a.shape, mybir.dt.from_np(a.dtype), kind="ExternalInput").ap()
    io["out"] = nc.dram_tensor("out_0", (1, T, D), mybir.dt.float32, kind="ExternalOutput").ap()
    io["kk_rows"] = nc.dram_tensor("kk_rows", (P, TT * HD, B), mybir.dt.float32, kind="Internal").ap()
    io["inv_rows"] = nc.dram_tensor("inv_rows", (P, B, B), mybir.dt.float32, kind="Internal").ap()
    build(nc, io)
    r = run(nc, [arrays], core_ids=[0])
    return r.results[0]["out_0"]
```
